# Optimizing a Trainium2 kernel written in Bass

```python
import math
import jax, jax.numpy as jnp
from jax import lax
import numpy as np

D_MODEL = 2048
BATCH = 1
SEQ = 256
DEPTH = 1

HEAD_DIM = 64
N_MIXERS = 4
GROUP_WIDTH = D_MODEL // N_MIXERS
N_HEADS = GROUP_WIDTH // HEAD_DIM
NSA_KV_HEADS = 2
NSA_GQA = N_HEADS // NSA_KV_HEADS
CMP_LEN = 32
CMP_STRIDE = 16
SLC_LEN = 64
SLC_TOP = 16
WINDOW = 512
FORCE_BONUS = 1.0e3
N_BUCKETS = 32
MAX_DISTANCE = 1024
CONV_W = 3
CHUNK = 128
Q_BLOCK = 128
D_FF = -(-8 * D_MODEL // (3 * 256)) * 256
NEG_INF = -1.0e30

A_Q_COLS = N_HEADS * HEAD_DIM
A_KV_COLS = 6 * NSA_KV_HEADS * HEAD_DIM
A_GATE_COLS = 3 * N_HEADS
B_COLS = 3 * GROUP_WIDTH
C_COLS = 2 * GROUP_WIDTH
D_COLS = 3 * GROUP_WIDTH
SPLIT_POINTS = (A_Q_COLS, A_Q_COLS + A_KV_COLS, A_Q_COLS + A_KV_COLS + A_GATE_COLS, A_Q_COLS + A_KV_COLS + A_GATE_COLS + B_COLS, A_Q_COLS + A_KV_COLS + A_GATE_COLS + B_COLS + C_COLS)
W_IN_COLS = SPLIT_POINTS[-1] + D_COLS


def rms_norm(x, g, eps=1e-6):
    xf = x.astype(jnp.float32)
    y = xf * lax.rsqrt(jnp.mean(xf * xf, axis=-1, keepdims=True) + eps)
    return (y * g.astype(jnp.float32)).astype(x.dtype)

def layer_norm_noaffine(x, eps=1e-5):
    xf = x.astype(jnp.float32)
    mu = jnp.mean(xf, axis=-1, keepdims=True)
    var = jnp.mean(jnp.square(xf - mu), axis=-1, keepdims=True)
    return ((xf - mu) * lax.rsqrt(var + eps)).astype(x.dtype)

def gelu(x):
    return jax.nn.gelu(x, approximate=True)

def rel_bucket(dist):
    n = jnp.maximum(dist, 0)
    max_exact = N_BUCKETS // 2
    nf = jnp.maximum(n, 1).astype(jnp.float32)
    large = max_exact + (jnp.log(nf / max_exact) / math.log(MAX_DISTANCE / max_exact) * (N_BUCKETS - max_exact)).astype(jnp.int32)
    large = jnp.minimum(large, N_BUCKETS - 1)
    return jnp.where(n < max_exact, n, large)

def rel_bias_heads(dist, table):
    b = table[rel_bucket(dist)].astype(jnp.float32)
    b = jnp.moveaxis(b, -1, 0)
    return b.reshape(NSA_KV_HEADS, NSA_GQA, *dist.shape)

def masked_softmax(s, mask):
    s = jnp.where(mask, s, NEG_INF)
    p = jax.nn.softmax(s, axis=-1)
    return jnp.where(mask, p, 0.0)

def cmp_slc_overlap(n_cmp, n_slc):
    c0 = np.arange(n_cmp)[:, None] * CMP_STRIDE
    s0 = np.arange(n_slc)[None, :] * SLC_LEN
    ov = np.minimum(c0 + CMP_LEN, s0 + SLC_LEN) - np.maximum(c0, s0)
    return (np.maximum(ov, 0) / CMP_LEN).astype(np.float32)

def nsa_attention(q, k_c, v_c, k_s, v_s, k_w, v_w, gates, q_gain, k_gain, cmp_pos, cmp_w1, cmp_w2, rel_table):
    B, T = q.shape[0], q.shape[1]
    G, R, Dh = NSA_KV_HEADS, NSA_GQA, HEAD_DIM
    scale = Dh ** -0.5
    q = rms_norm(q, q_gain).reshape(B, T, G, R, Dh)
    k_s = rms_norm(k_s, k_gain)
    k_w = rms_norm(k_w, k_gain)
    t_pos = jnp.arange(T, dtype=jnp.int32)

    n_cmp = (T - CMP_LEN) // CMP_STRIDE + 1
    blk = np.arange(n_cmp)[:, None] * CMP_STRIDE + np.arange(CMP_LEN)[None, :]

    def compress(z, i):
        zb = z[:, blk] + cmp_pos[i][None, None, :, None, :]
        zb = zb.transpose(0, 1, 3, 2, 4).reshape(B, n_cmp, G, CMP_LEN * Dh)
        return gelu(zb @ cmp_w1[i]) @ cmp_w2[i]

    kc = rms_norm(compress(k_c, 0), k_gain)
    vc = compress(v_c, 1)
    cmp_end = jnp.asarray(blk[:, -1], jnp.int32)
    dist_c = t_pos[:, None] - cmp_end[None, :]
    s_c = jnp.einsum('btgrd,bngd->bgrtn', q, kc).astype(jnp.float32) * scale + rel_bias_heads(dist_c, rel_table)
    p_c = masked_softmax(s_c, dist_c >= 0)
    o_cmp = jnp.einsum('bgrtn,bngd->btgrd', p_c.astype(vc.dtype), vc)

    n_slc = T // SLC_LEN
    top = min(SLC_TOP, n_slc)
    imp = jnp.einsum('bgrtn,nj->bgtj', p_c, jnp.asarray(cmp_slc_overlap(n_cmp, n_slc)))
    j_idx = jnp.arange(n_slc, dtype=jnp.int32)
    cur = t_pos // SLC_LEN
    valid = (j_idx[None, :] * SLC_LEN) <= t_pos[:, None]
    forced = (j_idx[None, :] == 0) | (j_idx[None, :] == cur[:, None]) | (j_idx[None, :] == cur[:, None] - 1)
    score = jnp.where(valid, imp + jnp.where(forced, FORCE_BONUS, 0.0), NEG_INF)
    _, sel = lax.top_k(score, top)

    ks_blk = k_s.reshape(B, n_slc, SLC_LEN, G, Dh).transpose(0, 3, 1, 2, 4)
    vs_blk = v_s.reshape(B, n_slc, SLC_LEN, G, Dh).transpose(0, 3, 1, 2, 4)
    pad = ((0, 0), (WINDOW, 0), (0, 0), (0, 0))
    kw_pad = jnp.pad(k_w, pad)
    vw_pad = jnp.pad(v_w, pad)
    table_g = rel_table.reshape(N_BUCKETS, G, R)
    g_idx = jnp.arange(G)[None, :, None, None, None]
    gather_blocks = jax.vmap(jax.vmap(lambda blocks, ix: blocks[ix]))
    win_len = WINDOW + Q_BLOCK

    def block_fn(qb):
        qs = qb * Q_BLOCK
        qt = qs + jnp.arange(Q_BLOCK, dtype=jnp.int32)
        qblk = lax.dynamic_slice_in_dim(q, qs, Q_BLOCK, axis=1)
        ix = lax.dynamic_slice_in_dim(sel, qs, Q_BLOCK, axis=2)
        ksel = gather_blocks(ks_blk, ix)
        vsel = gather_blocks(vs_blk, ix)
        kpos = ix[..., None] * SLC_LEN + jnp.arange(SLC_LEN, dtype=jnp.int32)
        d_s = qt[None, None, :, None, None] - kpos
        b_s = jnp.moveaxis(table_g[rel_bucket(d_s), g_idx].astype(jnp.float32), -1, 2)
        s_s = jnp.einsum('btgrd,bgtkld->bgrtkl', qblk, ksel).astype(jnp.float32) * scale + b_s
        shp = s_s.shape
        p_s = masked_softmax(s_s.reshape(B, G, R, Q_BLOCK, -1), (d_s >= 0).reshape(B, G, 1, Q_BLOCK, -1)).reshape(shp)
        o_s = jnp.einsum('bgrtkl,bgtkld->btgrd', p_s.astype(vsel.dtype), vsel)
        kw = lax.dynamic_slice_in_dim(kw_pad, qs, win_len, axis=1)
        vw = lax.dynamic_slice_in_dim(vw_pad, qs, win_len, axis=1)
        kp = qs - WINDOW + jnp.arange(win_len, dtype=jnp.int32)
        d_w = qt[:, None] - kp[None, :]
        m_w = (d_w >= 0) & (d_w < WINDOW) & (kp[None, :] >= 0)
        s_w = jnp.einsum('btgrd,bsgd->bgrts', qblk, kw).astype(jnp.float32) * scale + rel_bias_heads(d_w, rel_table)
        p_w = masked_softmax(s_w, m_w)
        o_w = jnp.einsum('bgrts,bsgd->btgrd', p_w.astype(vw.dtype), vw)
        return o_s, o_w

    o_slc, o_win = lax.map(block_fn, jnp.arange(T // Q_BLOCK, dtype=jnp.int32))
    o_slc = jnp.moveaxis(o_slc, 0, 1).reshape(B, T, G, R, Dh)
    o_win = jnp.moveaxis(o_win, 0, 1).reshape(B, T, G, R, Dh)

    g = jax.nn.sigmoid(gates.astype(jnp.float32)).astype(q.dtype).reshape(B, T, G, R, 3)
    o = g[..., 0:1] * o_cmp + g[..., 1:2] * o_slc + g[..., 2:3] * o_win
    return o.reshape(B, T, G * R * Dh)

def short_conv_mixer(cols, conv_w):
    b_gate, c_gate, h = jnp.split(cols, 3, axis=-1)
    z = c_gate * h
    T = z.shape[1]
    zp = jnp.pad(z, ((0, 0), (CONV_W - 1, 0), (0, 0)))
    y = conv_w[0] * zp[:, 0:T]
    for i in range(1, CONV_W):
        y = y + conv_w[i] * zp[:, i:i + T]
    return b_gate * y

def spatial_gating_mixer(cols, sgu_w, sgu_b):
    B, T = cols.shape[0], cols.shape[1]
    u, v = jnp.split(gelu(cols), 2, axis=-1)
    v = layer_norm_noaffine(v).reshape(B, T // CHUNK, CHUNK, N_HEADS, HEAD_DIM)
    w = sgu_w * jnp.asarray(np.tril(np.ones((CHUNK, CHUNK), np.float32)), sgu_w.dtype)
    s = jnp.einsum('hpq,bcqhe->bcphe', w, v) + sgu_b.T[None, None, :, :, None]
    return u * s.reshape(B, T, GROUP_WIDTH)

def stick_breaking_attention(q, k, v):
    B, T, H, Dh = q.shape
    scale = Dh ** -0.5
    outs = []
    for qb in range(T // Q_BLOCK):
        qs, qe = qb * Q_BLOCK, (qb + 1) * Q_BLOCK
        z = jnp.einsum('bthd,bshd->bhts', q[:, qs:qe], k[:, :qe]).astype(jnp.float32) * scale
        mask = jnp.asarray(np.arange(qe)[None, :] < np.arange(qs, qe)[:, None])
        log_beta = jax.nn.log_sigmoid(z)
        log_1m = jnp.where(mask, log_beta - z, 0.0)
        tail = lax.cumsum(log_1m, axis=3, reverse=True) - log_1m
        a = jnp.where(mask, jnp.exp(log_beta + tail), 0.0)
        outs.append(jnp.einsum('bhts,bshd->bthd', a.astype(v.dtype), v[:, :qe]))
    return jnp.concatenate(outs, axis=1).reshape(B, T, H * Dh)

def first_inputs(seed: int = 0) -> dict:
    key = jax.random.key(seed)
    ks = jax.random.split(key, 18)
    f32 = jnp.float32

    def nrm(k, shape, scale):
        return jax.random.normal(k, shape, f32) * scale

    res_scale = (2 * DEPTH) ** -0.5
    return {
        'x': nrm(ks[0], (BATCH, SEQ, D_MODEL), 1.0),
        'w_in': nrm(ks[1], (DEPTH, D_MODEL, W_IN_COLS), D_MODEL ** -0.5),
        'w_out': nrm(ks[2], (DEPTH, D_MODEL, D_MODEL), D_MODEL ** -0.5 * res_scale),
        'norm_mix': 1.0 + nrm(ks[3], (DEPTH, D_MODEL), 0.05),
        'norm_ffn': 1.0 + nrm(ks[4], (DEPTH, D_MODEL), 0.05),
        'q_gain': 1.0 + nrm(ks[5], (DEPTH, HEAD_DIM), 0.05),
        'k_gain': 1.0 + nrm(ks[6], (DEPTH, HEAD_DIM), 0.05),
        'cmp_pos': nrm(ks[7], (DEPTH, 2, CMP_LEN, HEAD_DIM), 0.1),
        'cmp_w1': nrm(ks[8], (DEPTH, 2, CMP_LEN * HEAD_DIM, HEAD_DIM), (CMP_LEN * HEAD_DIM) ** -0.5),
        'cmp_w2': nrm(ks[9], (DEPTH, 2, HEAD_DIM, HEAD_DIM), HEAD_DIM ** -0.5),
        'rel_table': nrm(ks[10], (N_BUCKETS, N_HEADS), 0.5),
        'conv_w': nrm(ks[11], (DEPTH, CONV_W, GROUP_WIDTH), CONV_W ** -0.5),
        'sgu_w': nrm(ks[12], (DEPTH, N_HEADS, CHUNK, CHUNK), CHUNK ** -0.5),
        'sgu_b': 1.0 + nrm(ks[13], (DEPTH, N_HEADS, CHUNK), 0.1),
        'group_gain': 1.0 + nrm(ks[14], (DEPTH, D_MODEL), 0.05),
        'w_ffn_gate': nrm(ks[15], (DEPTH, D_MODEL, D_FF), D_MODEL ** -0.5),
        'w_ffn_up': nrm(ks[16], (DEPTH, D_MODEL, D_FF), D_MODEL ** -0.5),
        'w_ffn_down': nrm(ks[17], (DEPTH, D_FF, D_MODEL), D_FF ** -0.5 * res_scale),
    }

def first_block(x, w_in, w_out, norm_mix, norm_ffn, q_gain, k_gain, cmp_pos, cmp_w1, cmp_w2, rel_table, conv_w, sgu_w, sgu_b, group_gain, w_ffn_gate, w_ffn_up, w_ffn_down):
    B, T = x.shape[0], x.shape[1]
    for l in range(DEPTH):
        h = rms_norm(x, norm_mix[l])
        proj = h @ w_in[l]
        a_q, a_kv, a_g, b_cols, c_cols, d_cols = jnp.split(proj, SPLIT_POINTS, axis=-1)
        kv = a_kv.reshape(B, T, 6, NSA_KV_HEADS, HEAD_DIM)
        o_a = nsa_attention(a_q.reshape(B, T, N_HEADS, HEAD_DIM), kv[:, :, 0], kv[:, :, 1], kv[:, :, 2], kv[:, :, 3], kv[:, :, 4], kv[:, :, 5], a_g.reshape(B, T, N_HEADS, 3), q_gain[l], k_gain[l], cmp_pos[l], cmp_w1[l], cmp_w2[l], rel_table)
        o_b = short_conv_mixer(b_cols, conv_w[l])
        o_c = spatial_gating_mixer(c_cols, sgu_w[l], sgu_b[l])
        dq, dk, dv = jnp.split(d_cols, 3, axis=-1)
        o_d = stick_breaking_attention(dq.reshape(B, T, N_HEADS, HEAD_DIM), dk.reshape(B, T, N_HEADS, HEAD_DIM), dv.reshape(B, T, N_HEADS, HEAD_DIM))
        mixed = jnp.stack([o_a, o_b, o_c, o_d], axis=2)
        mixed = rms_norm(mixed, group_gain[l].reshape(N_MIXERS, GROUP_WIDTH))
        x = x + mixed.reshape(B, T, D_MODEL) @ w_out[l]
        h = rms_norm(x, norm_ffn[l])
        x = x + (jax.nn.silu(h @ w_ffn_gate[l]) * (h @ w_ffn_up[l])) @ w_ffn_down[l]
    return x


DEPTH_2 = 2

GRID_W = 64
N_MIXERS_2 = 2
BLOCK_Q = 128
ROPE_THETA = 10000.0
RMS_EPS = 1e-6
LN_EPS = 1e-5

A_HEADS = 16
A_KV_HEADS = 4
A_HEAD_DIM = D_MODEL // A_HEADS
A_GROUP = A_HEADS // A_KV_HEADS
A_WIDTH = A_HEADS * A_HEAD_DIM
A_KV_WIDTH = A_KV_HEADS * A_HEAD_DIM
A_IN = 2 * A_WIDTH + 2 * A_KV_WIDTH

R_HEADS = 8
R_QK_DIM = D_MODEL // R_HEADS
R_V_DIM = 2 * R_QK_DIM
R_QK_WIDTH = R_HEADS * R_QK_DIM
R_V_WIDTH = R_HEADS * R_V_DIM
R_IN = 2 * R_QK_WIDTH + 2 * R_V_WIDTH
R_DECAY_BASE = 5.0

N_A_LAYERS = (DEPTH_2 + 1) // N_MIXERS_2
N_R_LAYERS = DEPTH_2 // N_MIXERS_2
ALPHA = (2.0 * DEPTH_2) ** 0.25
BETA = (8.0 * DEPTH_2) ** -0.25


def axial_rope_tables(seq_len, head_dim):
    rows_n = seq_len // GRID_W
    row = jnp.repeat(jnp.arange(rows_n, dtype=jnp.float32), GRID_W)
    col = jnp.tile(jnp.arange(GRID_W, dtype=jnp.float32), rows_n)
    half = head_dim // 2
    inv_freq = ROPE_THETA ** (-jnp.arange(0, half, 2, dtype=jnp.float32) / half)
    ang_r = row[:, None] * inv_freq
    ang_c = col[:, None] * inv_freq
    ang = jnp.concatenate([ang_r, ang_r, ang_c, ang_c], axis=-1)
    return jnp.cos(ang), jnp.sin(ang)

def apply_rope(x, cos, sin):
    x32 = x.astype(jnp.float32)
    a, b, c, d = jnp.split(x32, 4, axis=-1)
    rot = jnp.concatenate([-b, a, -d, c], axis=-1)
    out = x32 * cos[None, :, None, :] + rot * sin[None, :, None, :]
    return out.astype(x.dtype)

def rms_norm_2(x, gain):
    x32 = x.astype(jnp.float32)
    y = x32 * lax.rsqrt(jnp.mean(x32 * x32, axis=-1, keepdims=True) + RMS_EPS)
    return (y * gain.astype(jnp.float32)).astype(x.dtype)

def layer_norm(x, gain, bias):
    x32 = x.astype(jnp.float32)
    mu = jnp.mean(x32, axis=-1, keepdims=True)
    var = jnp.mean(jnp.square(x32 - mu), axis=-1, keepdims=True)
    y = (x32 - mu) * lax.rsqrt(var + LN_EPS)
    return (y * gain.astype(jnp.float32) + bias.astype(jnp.float32)).astype(x.dtype)

def head_group_norm(x):
    x32 = x.astype(jnp.float32)
    mu = jnp.mean(x32, axis=-1, keepdims=True)
    var = jnp.mean(jnp.square(x32 - mu), axis=-1, keepdims=True)
    return ((x32 - mu) * lax.rsqrt(var + LN_EPS)).astype(x.dtype)

def attention_mixer(h, w_in, q_gain, k_gain, w_out, cos, sin):
    B, S, _ = h.shape
    proj = h @ w_in
    q, k, v, g = jnp.split(proj, [A_WIDTH, A_WIDTH + A_KV_WIDTH, A_WIDTH + 2 * A_KV_WIDTH], axis=-1)
    q = q.reshape(B, S, A_HEADS, A_HEAD_DIM)
    k = k.reshape(B, S, A_KV_HEADS, A_HEAD_DIM)
    v = v.reshape(B, S, A_KV_HEADS, A_HEAD_DIM)
    q = apply_rope(rms_norm_2(q, q_gain), cos, sin) * (A_HEAD_DIM ** -0.5)
    k = apply_rope(rms_norm_2(k, k_gain), cos, sin)
    n_blocks = S // BLOCK_Q
    qb_all = q.reshape(B, n_blocks, BLOCK_Q, A_KV_HEADS, A_GROUP, A_HEAD_DIM).transpose(1, 0, 3, 4, 2, 5)

    def block(qb):
        s = jnp.einsum('bkgqd,bskd->bkgqs', qb, k).astype(jnp.float32)
        p = jax.nn.softmax(s, axis=-1).astype(v.dtype)
        return jnp.einsum('bkgqs,bskd->bkgqd', p, v)

    o = lax.map(block, qb_all)
    o = o.transpose(1, 0, 4, 2, 3, 5).reshape(B, S, A_WIDTH)
    return (o * jax.nn.silu(g)) @ w_out

def chunk_retention(q, k, v, log_g, strict):
    B, S, H, dk = q.shape
    dv = v.shape[-1]
    nc = S // CHUNK

    def to_chunks(t):
        return t.reshape(B, nc, CHUNK, H, t.shape[-1]).transpose(1, 0, 3, 2, 4)

    qc, kc, vc = to_chunks(q), to_chunks(k), to_chunks(v)
    log_g = log_g.astype(jnp.float32)
    pos = jnp.arange(CHUNK, dtype=jnp.float32)
    diff = pos[:, None] - pos[None, :]
    mask = (diff > 0) if strict else (diff >= 0)
    intra_decay = jnp.where(mask[None], jnp.exp(log_g[:, None, None] * jnp.maximum(diff, 0.0)[None]), 0.0)
    q_decay = jnp.exp(log_g[:, None] * (pos + 1.0))[..., None]
    k_decay = jnp.exp(log_g[:, None] * (CHUNK - 1.0 - pos))[..., None]
    chunk_decay = jnp.exp(log_g * CHUNK)[:, None, None]

    def step(state, xs):
        qb, kb, vb = xs
        q32, k32, v32 = qb.astype(jnp.float32), kb.astype(jnp.float32), vb.astype(jnp.float32)
        s = jnp.einsum('bhqd,bhkd->bhqk', q32, k32) * intra_decay
        inner = jnp.einsum('bhqk,bhkv->bhqv', s, v32)
        cross = jnp.einsum('bhqd,bhdv->bhqv', q32, state) * q_decay
        new_state = state * chunk_decay + jnp.einsum('bhkd,bhkv->bhdv', k32 * k_decay, v32)
        return new_state, (inner + cross).astype(vb.dtype)

    state0 = jnp.zeros((B, H, dk, dv), jnp.float32)
    _, out = lax.scan(step, state0, (qc, kc, vc))
    return out.transpose(1, 0, 3, 2, 4).reshape(B, S, H, dv)

def retention_mixer(h, w_in, decay_exp, w_out, cos, sin):
    B, S, _ = h.shape
    proj = h @ w_in
    q, k, v, g = jnp.split(proj, [R_QK_WIDTH, 2 * R_QK_WIDTH, 2 * R_QK_WIDTH + R_V_WIDTH], axis=-1)
    q = apply_rope(q.reshape(B, S, R_HEADS, R_QK_DIM), cos, sin)
    k = apply_rope(k.reshape(B, S, R_HEADS, R_QK_DIM), cos, sin) * (R_QK_DIM ** -0.5)
    v = v.reshape(B, S, R_HEADS, R_V_DIM)
    log_g = jnp.log1p(-jnp.exp2(-decay_exp.astype(jnp.float32)))
    fwd = chunk_retention(q, k, v, log_g[0], strict=False)
    bwd = jnp.flip(chunk_retention(jnp.flip(q, 1), jnp.flip(k, 1), jnp.flip(v, 1), log_g[1], strict=True), 1)
    o = head_group_norm(fwd + bwd).reshape(B, S, R_V_WIDTH)
    return (o * jax.nn.silu(g)) @ w_out

def second_inputs(seed: int = 0) -> dict:
    key = jax.random.key(seed)
    ks = jax.random.split(key, 12)
    f32 = jnp.float32
    x = jax.random.normal(ks[0], (BATCH, SEQ, D_MODEL), f32)

    a_col_scale = jnp.concatenate([jnp.ones((A_WIDTH + A_KV_WIDTH,), f32),
                                   jnp.full((A_KV_WIDTH,), BETA, f32),
                                   jnp.ones((A_WIDTH,), f32)])
    attn_w_in = jax.random.normal(ks[1], (N_A_LAYERS, D_MODEL, A_IN), f32) * (D_MODEL ** -0.5) * a_col_scale
    attn_q_gain = 1.0 + 0.02 * jax.random.normal(ks[2], (N_A_LAYERS, A_HEAD_DIM), f32)
    attn_k_gain = 1.0 + 0.02 * jax.random.normal(ks[3], (N_A_LAYERS, A_HEAD_DIM), f32)
    attn_w_out = jax.random.normal(ks[4], (N_A_LAYERS, A_WIDTH, D_MODEL), f32) * (A_WIDTH ** -0.5) * BETA

    r_col_scale = jnp.concatenate([jnp.ones((2 * R_QK_WIDTH,), f32),
                                   jnp.full((R_V_WIDTH,), BETA, f32),
                                   jnp.ones((R_V_WIDTH,), f32)])
    ret_w_in = jax.random.normal(ks[5], (N_R_LAYERS, D_MODEL, R_IN), f32) * (D_MODEL ** -0.5) * r_col_scale
    base = R_DECAY_BASE + jnp.arange(R_HEADS, dtype=f32)
    base2 = jnp.stack([base, base[::-1]], axis=0)
    ret_decay_exp = base2[None] + 0.1 * jax.random.normal(ks[6], (N_R_LAYERS, 2, R_HEADS), f32)
    ret_w_out = jax.random.normal(ks[7], (N_R_LAYERS, R_V_WIDTH, D_MODEL), f32) * (R_V_WIDTH ** -0.5) * BETA

    ln_gain = 1.0 + 0.02 * jax.random.normal(ks[8], (DEPTH_2, D_MODEL), f32)
    ln_bias = 0.02 * jax.random.normal(ks[9], (DEPTH_2, D_MODEL), f32)
    return {"x": x, "attn_w_in": attn_w_in, "attn_q_gain": attn_q_gain, "attn_k_gain": attn_k_gain,
            "attn_w_out": attn_w_out, "ret_w_in": ret_w_in, "ret_decay_exp": ret_decay_exp,
            "ret_w_out": ret_w_out, "ln_gain": ln_gain, "ln_bias": ln_bias}

def second_block(x, attn_w_in, attn_q_gain, attn_k_gain, attn_w_out, ret_w_in, ret_decay_exp,
              ret_w_out, ln_gain, ln_bias):
    S = x.shape[1]
    cos_a, sin_a = axial_rope_tables(S, A_HEAD_DIM)
    cos_r, sin_r = axial_rope_tables(S, R_QK_DIM)
    for i in range(DEPTH_2):
        j = i // N_MIXERS_2
        if i % N_MIXERS_2 == 0:
            y = attention_mixer(x, attn_w_in[j], attn_q_gain[j], attn_k_gain[j], attn_w_out[j], cos_a, sin_a)
        else:
            y = retention_mixer(x, ret_w_in[j], ret_decay_exp[j], ret_w_out[j], cos_r, sin_r)
        x = layer_norm(ALPHA * x + y, ln_gain[i], ln_bias[i])
    return x


def setup_inputs(seed=0):
    out = dict(first_inputs(seed))
    for name, value in second_inputs(seed + 1).items():
        if name != "x":
            out[name + "_2"] = value
    return out


def reference(
    x, w_in, w_out, norm_mix, norm_ffn, q_gain, k_gain, cmp_pos, cmp_w1, cmp_w2, rel_table,
    conv_w, sgu_w, sgu_b, group_gain, w_ffn_gate, w_ffn_up, w_ffn_down, attn_w_in_2,
    attn_q_gain_2, attn_k_gain_2, attn_w_out_2, ret_w_in_2, ret_decay_exp_2, ret_w_out_2,
    ln_gain_2, ln_bias_2,
):
    x = first_block(
        x, w_in, w_out, norm_mix, norm_ffn, q_gain, k_gain, cmp_pos, cmp_w1, cmp_w2, rel_table,
        conv_w, sgu_w, sgu_b, group_gain, w_ffn_gate, w_ffn_up, w_ffn_down,
    )
    return second_block(
        x, attn_w_in_2, attn_q_gain_2, attn_k_gain_2, attn_w_out_2, ret_w_in_2, ret_decay_exp_2,
        ret_w_out_2, ln_gain_2, ln_bias_2,
    )


_drawn_inputs = setup_inputs


def setup_inputs(seed=0):
    import zlib

    import numpy as np

    out = dict(_drawn_inputs(seed))
    spreads = {}
    factors = {'q_gain': 4.786, 'k_gain': 4.59, 'attn_q_gain_2': 23.227, 'attn_k_gain_2': 25.2}
    for name, (base, spread) in spreads.items():
        noise = np.random.default_rng([zlib.crc32(name.encode()), seed]).standard_normal(out[name].shape)
        drawn = base * np.exp(spread * noise) if base else spread * noise
        out[name] = __import__('jax').numpy.asarray(drawn.astype(out[name].dtype))
    for name, factor in factors.items():
        out[name] = (out[name] * factor).astype(out[name].dtype)
    return out
```

```python
import math
from contextlib import ExitStack

import numpy as np

import concourse.bass as bass
from concourse import mybir

F32 = mybir.dt.float32
F32R = mybir.dt.float32r
ALU = mybir.AluOpType
ACT = mybir.ActivationFunctionType
AX = mybir.AxisListType.X

P = 128
T = 256
J = T // P
D = 2048
KT = D // P
W = 512
FB = D // W
CK = 4
RAWS = 4
HALF = 2
SPLITS = 4

HD = 64
NH = 8
NG = 2
GW = D // 4
NCMP = 15
CL, CS = 32, 16
DFF = 5632
NF = DFF // W
NEG = -1.0e30
Q0, KV0, KV1, B0, C0, D0 = 0, 512, 1024, 1304, 2840, 3864
KV1W = 280

AH, AKV, AD = 16, 4, 128
RH, RD, RV = 8, 256, 512
ALPHA = 4.0 ** 0.25
RMS_EPS, LN_EPS = 1e-6, 1e-5

PHASES = [("in1", 44, 1), ("out1", 16, 1), ("ffn", 8, 11), ("down", 44, 1), ("in2", 40, 1),
          ("out2", 16, 1), ("ret", 24, 4), ("out3", 32, 1)]


def stream_plan():
    plan, chunks, landed = {}, 0, [0] * RAWS
    for name, per, bodies in PHASES:
        incs = [32 if name == "ret" and c % 12 < 4 else 16 for c in range(per)]
        body = [sum(incs[s::RAWS]) for s in range(RAWS)]
        plan[name] = (chunks, per, list(landed), body, incs)
        chunks += per * bodies
        landed = [a + b * bodies for a, b in zip(landed, body)]
    return plan


PLAN = stream_plan()


def two_blocks(nc, A, out):
    ctx = ExitStack()

    base = 16512
    limit = 229368

    def at(name, off, shape, dt=F32):
        n = 4
        for s in shape[1:]:
            n *= s
        assert base + off + n <= limit, (name, off, n)
        return nc.alloc_sbuf_tensor_at(name, shape, dt, offset=base + off)

    KB = 1024
    raw = at("raw", 0, [P, RAWS, CK, W])
    whi = at("whi", 32 * KB, [P, SPLITS, HALF, W], F32R)
    wlo = at("wlo", 48 * KB, [P, SPLITS, HALF, W], F32R)
    T1H = at("T1H", 64 * KB, [P, KT, T], F32R)
    T1L = at("T1L", 80 * KB, [P, KT, T], F32R)
    S0 = 96 * KB
    cst = at("cst", S0, [P, 5, P])
    ident, flip, ntri, nones, tril = (cst[:, n, :] for n in range(5))
    small = at("small", S0 + 2560, [P, 640])
    R0 = S0 + 2560 + 2560
    T2aH = at("T2aH", R0, [P, KT, T], F32R)
    T2aL = at("T2aL", R0 + 16 * KB, [P, KT, T], F32R)
    X = at("X", R0, [P, J, D])
    XG = at("XG", R0 + 16 * KB, [P, J, D])
    PJ = R0 + 32 * KB
    Aq = at("Aq", PJ, [P, J, W])
    Akv = at("Akv", PJ + 4 * KB, [P, J, W])
    Dq = at("Dq", PJ + 8 * KB, [P, J, W])
    Dk = at("Dk", PJ + 12 * KB, [P, J, W])
    Dv = at("Dv", PJ + 16 * KB, [P, J, W])
    Cu = at("Cu", PJ + 20 * KB, [P, J, W])
    Cv = at("Cv", PJ + 24 * KB, [P, J, W])
    Bb = at("Bb", PJ + 28 * KB, [P, J, W])
    Bc = at("Bc", PJ + 32 * KB, [P, J, W])
    Bh = at("Bh", PJ + 36 * KB, [P, J, W])
    Akw = at("Akw", PJ + 40 * KB, [P, J, KV1W])
    MS = PJ + 40 * KB + J * KV1W * 4 + 64
    gB = at("gB", MS, [P, D])
    bias = at("bias", MS + 8 * KB, [P, NH, 384])
    w1s = at("w1s", MS + 20 * KB, [P, 2, CS, HD])
    w2s = at("w2s", MS + 28 * KB, [HD, 2, HD])
    M0 = 64 * KB
    qT = at("qT", M0, [P, 4, T])
    kT = at("kT", M0 + 4 * KB, [P, 2, T])
    zz = at("zz", M0 + 6 * KB, [P, 2, NG, T])
    dqT = at("dqT", M0 + 10 * KB, [P, 4, T])
    dkT = at("dkT", M0 + 14 * KB, [P, 4, T])
    PB = at("PB", M0 + 18 * KB, [P, 2, 2, 384])
    PT = at("PT", M0 + 24 * KB, [P, 2, 2, 384])
    cap3 = at("cap3", M0 + 30 * KB, [P, 384])
    TQ = at("TQ", R0, [P, J, W])
    TK = at("TK", R0 + 4 * KB, [P, 2, J, P])
    msk3 = at("msk3", R0 + 6 * KB, [P, 384])
    AR = at("AR", R0 + 8 * KB, [P, 2, 384])
    LB = at("LB", R0 + 11 * KB, [P, 2, 384])
    SG = at("SG", R0 + 14 * KB, [P, NH, P])
    WT = at("WT", R0 + 18 * KB, [P, NH, P])
    PcT = at("PcT", R0 + 22 * KB, [NCMP, 2 * NH, P])
    zd = at("zd", R0 + 22 * KB, [P, J, 4, 2, HD])
    z1 = at("z1", R0 + 22 * KB, [P, J, W])
    z2 = at("z2", R0 + 26 * KB, [P, J, W])
    cwB = at("cwB", MS + 8 * KB, [P, 3, W])
    yb = at("yb", MS + 14 * KB, [P, J, W])
    junk = at("junk", R0, [P, W])
    x1b = at("x1b", PJ, [P, 2, J, W])
    xrb = at("xrb", PJ + 8 * KB, [P, 2, J, W])
    xgb = at("xgb", PJ + 16 * KB, [P, 2, J, W])
    junk2 = at("junk2", PJ + 24 * KB, [P, W])
    gF = at("gF", PJ + 32 * KB, [P, D])
    T2bH = at("T2bH", R0, [P, DFF // P, T], F32R)
    T2bL = at("T2bL", R0 + 44 * KB, [P, DFF // P, T], F32R)
    FT = R0 + 88 * KB
    sg = at("sg", FT, [P, J, W])
    av = at("av", FT + 4 * KB, [P, J, W])
    x2b = at("x2b", FT + 8 * KB, [P, J, W])
    xr2 = at("xr2", FT + 12 * KB, [P, J, W])
    T2cH = at("T2cH", R0, [P, KT, T], F32R)
    T2cL = at("T2cL", R0 + 16 * KB, [P, KT, T], F32R)
    E0 = R0 + 32 * KB
    kTa = at("kTa", E0, [P, AKV, T])
    vA = at("vA", E0 + 4 * KB, [P, J, W])
    tabs = [at(f"tab{n}", E0 + (8 + 4 * n) * KB, [P, J, 4, P]) for n in range(4)]
    xq = at("xq", E0 + 24 * KB, [P, J, W])
    ta = at("ta", E0 + 28 * KB, [P, J, W])
    tb = at("tb", E0 + 32 * KB, [P, J, W])
    qTa = at("qTa", E0 + 36 * KB, [P, 2, 4, T])
    gA = at("gA", E0 + 44 * KB, [P, J, W])
    PA = at("PA", E0 + 48 * KB, [P, 2, J, T])
    PTa = at("PTa", E0 + 52 * KB, [P, 2, J, T])
    oA = at("oA", E0 + 56 * KB, [P, AKV, J, W])
    gn = at("gn", E0 + 72 * KB, [P, 4, P])
    X3 = at("X3", R0 + 32 * KB, [P, J, D])
    xr3 = at("xr3", R0 + 48 * KB, [P, 2, J, W])
    lnG = at("lnG", R0 + 56 * KB, [P, D])
    lnB = at("lnB", R0 + 64 * KB, [P, D])
    T2dH = at("T2dH", R0, [P, RH * 4, T], F32R)
    T2dL = at("T2dL", R0 + 32 * KB, [P, RH * 4, T], F32R)
    G0 = R0 + 64 * KB
    MM = at("MM", G0, [P, RH, 2, T])
    rc = at("rc", G0 + 16 * KB, [P, J, W])
    rs_ = at("rs_", G0 + 20 * KB, [P, J, W])
    xr = at("xr", G0 + 24 * KB, [P, J, W])
    rb = at("rb", G0 + 28 * KB, [P, J, W])
    rT = at("rT", G0 + 32 * KB, [P, 2, 2, T])
    vR = at("vR", G0 + 36 * KB, [P, J, W])
    SM = at("SM", G0 + 24 * KB, [P, 2, T])
    oR = at("oR", G0 + 24 * KB, [P, J, W])
    gR = at("gR", G0 + 28 * KB, [P, J, W])
    X4 = at("X4", G0, [P, J, D])
    xr4 = at("xr4", G0 + 16 * KB, [P, 2, J, W])
    lnG2 = at("lnG2", G0 + 24 * KB, [P, D])
    lnB2 = at("lnB2", G0 + 32 * KB, [P, D])
    dpos = at("dpos", R0, [P, 2, T])
    dneg = at("dneg", R0 + 2 * KB, [P, 2, T])
    mt = at("mt", R0 + 4 * KB, [P, 2, 2 * T])
    lg = at("lg", R0 + 8 * KB, [P, 8, 2 * RH])

    used = [0]

    def cols(n):
        used[0] += n
        assert used[0] <= 640
        return small[:, used[0] - n:used[0]]

    ssx, rstd1 = cols(8), cols(2)
    posT = cols(64)
    sgubT = cols(8)
    qg8, kg = cols(64), cols(64)
    nss, nrs, ntmp = cols(24), cols(24), cols(24)
    gsig, gtmp = cols(48), cols(48)
    psd = [nc.alloc_psum_tensor(f"bank{n}", [P, W], F32) for n in range(8)]
    bank = [b[:, :] for b in psd]
    ACC = [[bank[0], bank[1]], [bank[2], bank[3]]]
    prow = at("prow", PJ + 28 * KB, [HD, P])
    sbrow = at("sbrow", PJ + 29 * KB, [NH, P])
    tabaug = at("tabaug", PJ + 30 * KB, [33, NH])
    onehot = at("onehot", PJ + 31 * KB, [33, W])
    vrow = at("vrow", PJ + 34 * KB, [NH, W])
    nmx, nsum, nrw = cols(8), cols(8), cols(8)
    cmx, csum, crw = cols(16), cols(16), cols(16)
    hT = cols(2 * NG * NCMP)
    gss, grs = cols(8), cols(8)
    ss1, rstd2 = cols(8), cols(2)
    bst, bag, brs = cols(8 * 6), cols(4), cols(2)
    nsx, nrx = cols(8), cols(8)
    pcm = at("pcm", R0 + 30 * KB, [P, 2 * NH, 16])
    KVC = at("KVC", R0 + 31 * KB, [NCMP, 2, NG, HD])
    kcT = cols(16)

    scr_bias = nc.dram_tensor("scr_bias", [NH * W], F32).ap()
    scr_x1 = nc.dram_tensor("scr_x1", [T, D], F32).ap()
    scr_x2 = nc.dram_tensor("scr_x2", [T, D], F32).ap()
    scr_x3 = nc.dram_tensor("scr_x3", [T, D], F32).ap()

    def sem(name):
        return ctx.enter_context(nc.semaphore(name))

    landed = [sem(f"landed{n}") for n in range(RAWS)]
    hi_ready, lo_ready, mm_done = sem("hi_ready"), sem("lo_ready"), sem("mm_done")
    acc_out = [sem("acc_out0"), sem("acc_out1")]
    tb_full, tb_hi, tb_done = sem("tb_full"), sem("tb_hi"), sem("tb_done")
    act_c, dve_c, pool_c = sem("act_chain"), sem("dve_chain"), sem("pool_chain")
    ret_c, reta_c = sem("ret_chain"), sem("reta_chain")
    x_in = [sem(f"x_in{n}") for n in range(FB)]
    cst_in, par_in, oh_in = sem("cst_in"), sem("par_in"), sem("oh_in")
    g_in = [sem(f"g_in{n}") for n in range(FB)]
    xg_ready, ssx_done, ms1, rs1 = sem("xg_ready"), sem("ssx_done"), sem("ms1"), sem("rs1")
    par_T, par_out, vrow_ps, vrow_sb = sem("par_T"), sem("par_out"), sem("vrow_ps"), sem("vrow_sb")
    vscr, bias_in = sem("vscr"), sem("bias_in")
    zd_ready, msk_in = sem("zd_ready"), sem("msk_in")
    nsa_ms, nsa_rs, nsa_qk, z_T, zz_ready = (sem(x) for x in ("nsa_ms", "nsa_rs", "nsa_qk", "z_T", "zz_ready"))
    qk_T, qkT_out, cmp1, hT_ready, cmp2 = (sem(x) for x in ("qk_T", "qkT_out", "cmp1", "hT_ready", "cmp2"))
    kc_ms, kc_rs, kcn_ready, kc_T, kcT_out = (sem(x) for x in ("kc_ms", "kc_rs", "kcn_ready", "kc_T", "kcT_out"))
    cs_full, cs_sub, cs_exp, pc_ready, pc_T, pcT_out = (
        sem(x) for x in ("cs_full", "cs_sub", "cs_exp", "pc_ready", "pc_T", "pcT_out"))
    gexp, s_full, s_max, s_exp, p_norm, p_T, pT_out, nsa_pv, nsa_o = (
        sem(x) for x in ("gexp", "s_full", "s_max", "s_exp", "p_norm", "p_T", "pT_out", "nsa_pv", "nsa_o"))
    d_T, dT_out, z_full, d_log, d_sp, d_arg, d_cap, d_a, d_pv, d_o = (
        sem(x) for x in ("d_T", "dT_out", "z_full", "d_log", "d_sp", "d_arg", "d_cap", "d_a", "d_pv", "d_o"))
    sg_in, sg_ready, w_T, wT_out, cv_ms, cv_rs, cv_ready, sgu_full, oc_ready = (
        sem(x) for x in ("sg_in", "sg_ready", "w_T", "wT_out", "cv_ms", "cv_rs", "cv_ready", "sgu_full", "oc_ready"))
    cw_in, shift_in, z_conv, ob_ready, gg_in, g_sq, g_ms, g_rs, mixed_ready = (
        sem(x) for x in ("cw_in", "shift_in", "z_conv", "ob_ready", "gg_in", "g_sq", "g_ms", "g_rs", "mixed_ready"))
    gF_in, xg2, x1_sq, ms2, rs2 = (sem(x) for x in ("gF_in", "xg2", "x1_sq", "ms2", "rs2"))
    xr1_in, x1_st, xr3_in, xr4_in = ([sem(f"{x}{n}") for n in range(2)] for x in ("xr1_in", "x1_st", "xr3_in", "xr4_in"))
    xr2_in, x2_st = sem("xr2_in"), sem("x2_st")
    tab_in, tab_ready, q_ms, q_rs, rot, rot_T, rotT_out, q_sq, q_norm, q_swap = (
        sem(x) for x in ("tab_in", "tab_ready", "q_ms", "q_rs", "rot", "rot_T", "rotT_out", "q_sq", "q_norm", "q_swap"))
    a_S, a_max, a_exp, a_PT, a_PTo, a_PV, a_O, a_og = (
        sem(x) for x in ("a_S", "a_max", "a_exp", "a_PT", "a_PTo", "a_PV", "a_O", "a_og"))
    ln_in, ln_ms, ln_rs, x3_ready, x3_st = (
        sem(x) for x in ("ln_in", "ln_ms", "ln_rs", "x3_ready", "x3_st"))
    rr_in = sem("rr_in")
    dist_in, lg1, mt_ready, mm_ready = (sem(x) for x in ("dist_in", "lg1", "mt_ready", "mm_ready"))
    r_rot, r_T, r_Tout, r_S, r_SM, r_out, r_ms, r_rs, r_norm, r_og = (
        sem(x) for x in ("r_rot", "r_T", "r_Tout", "r_S", "r_SM", "r_out", "r_ms", "r_rs", "r_norm", "r_og"))
    ln2_in, x4_ready, out_st = sem("ln2_in"), sem("x4_ready"), sem("out_st")

    class Chain:

        def __init__(self, eng, s):
            self.eng, self.s, self.n, self.base = eng, s, 0, 0

        def link(self, ins):
            ins.then_inc(self.s, 1)
            self.n += 1
            self.eng.wait_ge(self.s, self.base + self.n)

    def half_no(ph, c, hf, i):
        before, per = PLAN[ph][:2]
        q = 2 * (before + c) + hf
        return (q if isinstance(i, int) and i == 0 else i * (2 * per) + q), (2 * c + hf) % SPLITS

    def load(eng, ph, c, srcs, i=0):
        before, per, _, _, _ = PLAN[ph]
        if isinstance(i, int):
            g = before + i * per + c
            if g >= RAWS:
                eng.wait_ge(lo_ready, 2 * (g - RAWS) + 2)
        else:
            eng.wait_ge(lo_ready, i * (2 * per) + 2 * (before + c - RAWS) + 2)
        for lo, hi_, src in srcs:
            eng.dma_start(raw[:, c % RAWS, :, lo:hi_], src).then_inc(landed[c % RAWS], 16)

    def land(eng, ph, c, i):
        _, _, start, body, incs = PLAN[ph]
        v = start[c % RAWS] + sum(incs[c % RAWS:c + 1:RAWS])
        eng.wait_ge(landed[c % RAWS], v if isinstance(i, int) and i == 0 else i * body[c % RAWS] + v)

    def split_hi(eng, ph, c, hf, n=W, i=0):
        q, s = half_no(ph, c, hf, i)
        if hf == 0:
            land(eng, ph, c, i)
        if not isinstance(q, int) or q >= SPLITS:
            eng.wait_ge(mm_done, q - (SPLITS - 1))
        eng.activation(whi[:, s, :, :n], raw[:, c % RAWS, HALF * hf:HALF * (hf + 1), :n],
                       ACT.Copy).then_inc(hi_ready, 1)

    def split_lo(eng, ph, c, hf, n=W, i=0):
        q, s = half_no(ph, c, hf, i)
        eng.wait_ge(hi_ready, q + 1)
        eng.tensor_tensor(wlo[:, s, :, :n], raw[:, c % RAWS, HALF * hf:HALF * (hf + 1), :n],
                          whi[:, s, :, :n].bitcast(F32), ALU.subtract).then_inc(lo_ready, 1)

    def products(eng, ph, c, hf, TH, TL, kt0, blk, n=W, first=False, last=False, i=0):
        q, s = half_no(ph, c, hf, i)
        buf = blk % 2
        if first:
            uses = 2 * (blk // 2)
            if not isinstance(i, int) or i:
                nb = {"ffn": 2, "ret": 6}[ph]
                eng.wait_ge(acc_out[buf], i * nb + uses)
            elif uses:
                eng.wait_ge(acc_out[buf], uses)
        eng.wait_ge(lo_ready, q + 1)
        for t in range(HALF):
            kt = kt0 + HALF * hf + t
            for j in range(J):
                xs, o = slice(j * P, (j + 1) * P), ACC[buf][j][:, :n]
                eng.matmul(o, TH[:, kt, xs], whi[:, s, t, :n], start=first and t == 0, stop=False)
                eng.matmul(o, TH[:, kt, xs], wlo[:, s, t, :n], start=False, stop=False)
                m = eng.matmul(o, TL[:, kt, xs], whi[:, s, t, :n], start=False, stop=last and t == HALF - 1)
        m.then_inc(mm_done, 1)

    def block_done(eng, ph, c, i=0):
        q, _ = half_no(ph, c, 1, i)
        eng.wait_ge(mm_done, q + 1)

    def tr_pe(eng, n, src, banks=(4, 5), k=0):
        if not isinstance(n, int) or n >= len(banks):
            eng.wait_ge(tb_done, n + 1 - len(banks))
        for a in range(4):
            m = eng.transpose(bank[banks[k % len(banks)]][:, a * P:(a + 1) * P], src[:, a * P:(a + 1) * P], ident)
        m.then_inc(tb_full, 1)

    def tr_act(eng, n, dst, banks=(4, 5), k=0):
        eng.wait_ge(tb_full, n + 1)
        eng.activation(dst, bank[banks[k % len(banks)]].rearrange("p (a t) -> p a t", a=4), ACT.Copy).then_inc(tb_hi, 1)

    def tr_dve(eng, n, hi_, lo, banks=(4, 5), k=0):
        eng.wait_ge(tb_hi, n + 1)
        eng.tensor_tensor(lo, bank[banks[k % len(banks)]].rearrange("p (a t) -> p a t", a=4), hi_.bitcast(F32),
                          ALU.subtract).then_inc(tb_done, 1)

    def part(t, fb, j):
        return t[:, 4 * fb:4 * fb + 4, j * P:(j + 1) * P]

    def rep(ap, at_, n):
        dims = [list(d) for d in ap.ap]
        return bass.AP(ap.tensor, ap.offset, dims[:1 + at_] + [[0, n]] + dims[1 + at_:])

    def heads(ap, d):
        return ap.rearrange("p j (h d) -> p (j h) d", d=d)

    def swapped(eng, out, x, table, d):
        o, v, t = (a.rearrange("p j (n s d) -> p (j n) s d", s=2, d=d) for a in (out, x, table))
        return [eng.tensor_tensor(o[:, :, s, :], v[:, :, 1 - s, :], t[:, :, s, :], ALU.mult) for s in range(2)]

    def flat(t):
        return t.rearrange("p j h d -> p j (h d)")

    def rows(ap):
        return ap.rearrange("(j p) c -> p j c", p=P)

    def spread(ap, n, start=0):
        return bass.AP(ap.tensor, ap.offset + start, [[0, P], [1, n]])

    BLOCKS1 = [(Q0, W, Aq), (KV0, W, Akv), (KV1, KV1W, Akw), (D0, W, Dq), (D0 + W, W, Dk), (D0 + 2 * W, W, Dv),
               (C0, W, Cu), (C0 + W, W, Cv), (B0, W, Bb), (B0 + W, W, Bc), (B0 + 2 * W, W, Bh)]
    NB1 = len(BLOCKS1)
    BLK = {"in1": 0, "out1": 11, "ffn": 15, "down": 37, "in2": 41, "out2": 51, "ret": 55, "out3": 79}
    TB = {"in1": 0, "mix": 8, "out1": 16, "ffn": 24, "down": 46, "in2": 54, "out2": 62, "ret": 70}
    BLOCKS2 = [("q", 0), ("k", 0), ("v", 0), ("q", 1), ("q", 2), ("q", 3), ("g", 0), ("g", 1), ("g", 2), ("g", 3)]
    COL2 = {"q": 0, "k": D, "v": D + W, "g": D + 2 * W}
    ROT = [(0, 11, "q", 0), (1, 19, "k", 0), (3, 35, "q", 1), (4, 43, "q", 2), (5, 51, "q", 3)]
    S_AT = [28, 43, 55, 67]
    OT_AT = [(61, 64), (69, 72), (77, 79), (84, 85)]
    SW = [(0, P), (P, 3 * P)]

    def kbank(h, kind):
        return bank[2 * (h % 2) + kind]

    block = ctx.enter_context(nc.Block())

    @block.sync
    def _(sp):
        def chunk(w, kc, col, n=W):
            return w[kc * W:(kc + 1) * W, col:col + n].rearrange("(a p) n -> p a n", p=P)

        def dyn(w, kc, col, n=W):
            return w[kc * W:(kc + 1) * W, bass.ds(col, n)].rearrange("(a p) n -> p a n", p=P)

        for b, (col, n, _) in enumerate(BLOCKS1):
            for cc in range(4):
                if b == 0:
                    cs = slice(cc * W, (cc + 1) * W)
                    sp.dma_start(X[:, :, cs], rows(A["x"][0])[:, :, cs]).then_inc(x_in[cc], 16)
                load(sp, "in1", 4 * b + cc, [(0, n, chunk(A["w_in"][0], cc, col, n))])
        for c in range(16):
            load(sp, "out1", c, [(0, W, chunk(A["w_out"][0], c % 4, c // 4 * W))])
        with sp.Fori(0, NF) as f:
            for c in range(8):
                w = A["w_ffn_gate"] if c < 4 else A["w_ffn_up"]
                load(sp, "ffn", c, [(0, W, dyn(w[0], c % 4, f * W))], f)
        for c in range(44):
            load(sp, "down", c, [(0, W, chunk(A["w_ffn_down"][0], c % 11, c // 11 * W))])
        for b, (kind, g) in enumerate(BLOCKS2):
            for cc in range(4):
                load(sp, "in2", 4 * b + cc, [(0, W, chunk(A["attn_w_in_2"][0], cc, COL2[kind] + g * W))])
        for c in range(16):
            load(sp, "out2", c, [(0, W, chunk(A["attn_w_out_2"][0], c % 4, c // 4 * W))])
        with sp.Fori(0, RH // 2) as i:
            for c in range(24):
                e, w, kc = c // 12, A["ret_w_in_2"][0], c % 4
                if c % 12 < 4:
                    load(sp, "ret", c, [(0, RD, dyn(w, kc, i * (2 * RD) + e * RD, RD)),
                                        (RD, 2 * RD, dyn(w, kc, i * (2 * RD) + (D + e * RD), RD))], i)
                else:
                    off = 2 * D + (0 if c % 12 < 8 else RH * RV) + e * RV
                    load(sp, "ret", c, [(0, W, dyn(w, kc, i * (2 * RV) + off))], i)
        for c in range(32):
            load(sp, "out3", c, [(0, W, chunk(A["ret_w_out_2"][0], c % 8, c // 8 * W))])
        n = 0
        for fb in range(FB):
            for j in range(J):
                n += 1
                sp.wait_ge(x4_ready, n)
                cs = slice(fb * W, (fb + 1) * W)
                sp.dma_start(rows(out[0])[:, j, cs], X4[:, j, cs]).then_inc(out_st, 16)
        sp.wait_ge(out_st, 16 * n)

    @block.gpsimd
    def _(pool):
        ch = Chain(pool, pool_c)

        for half in range(2):
            ps = slice(half * HD, (half + 1) * HD)
            pool.dma_start(prow[:, ps], A["cmp_pos"][0].rearrange("i l d -> (i l) d")).then_inc(par_in, 16)
            for i in range(2):
                src = A["cmp_w1"][0, i].rearrange("(l d) e -> d l e", d=HD)
                pool.dma_start(w1s[ps, i, :, :], src[:, half * CS:(half + 1) * CS, :]).then_inc(par_in, 16)
        pool.dma_start(w2s[:, :, :], A["cmp_w2"][0].rearrange("i d e -> d i e")).then_inc(par_in, 16)
        pool.dma_start(sbrow[:, :], A["sgu_b"][0]).then_inc(par_in, 16)
        pool.dma_start(qg8, spread(A["q_gain"], HD)).then_inc(par_in, 16)
        pool.dma_start(kg, spread(A["k_gain"], HD)).then_inc(par_in, 16)
        pool.dma_start(onehot[:, :], A["onehot"]).then_inc(oh_in, 16)
        ch.link(pool.memset(tabaug[:, :], 1.0))
        pool.dma_start(tabaug[0:32, :], A["rel_table"]).then_inc(oh_in, 16)
        pool.wait_ge(vrow_sb, 1)
        pool.dma_start(scr_bias.rearrange("(h c) -> h c", h=NH), vrow[:, :]).then_inc(vscr, 16)
        pool.wait_ge(vscr, 16)
        pool.dma_start(bias[:, :, :], bass.AP(scr_bias.tensor, 0, [[1, P], [W, NH], [1, 384]])).then_inc(bias_in, 16)
        pool.wait_ge(xg_ready, FB)
        pool.dma_start(gB[:, :], spread(A["group_gain"], D)).then_inc(gg_in, 16)
        pool.wait_ge(mm_done, 8 * NB1)
        pool.dma_start(cap3[:, :], A["cap3"]).then_inc(msk_in, 16)
        pool.dma_start(msk3[:, :], A["msk3"]).then_inc(msk_in, 16)
        pool.dma_start(SG[:, :, :], A["sgu_w"][0].rearrange("h p q -> p h q")).then_inc(sg_in, 16)
        pool.wait_ge(acc_out[0], 12)
        pool.wait_ge(acc_out[1], 10)
        pool.tensor_tensor(Bh[:, :, :], Bc[:, :, :], Bh[:, :, :], ALU.mult).then_inc(z_conv, 1)
        pool.wait_ge(nsa_pv, NH)
        pool.dma_start(cwB[:, :, :], bass.AP(A["conv_w"].tensor, 0, [[0, P], [W, 3], [1, W]])).then_inc(cw_in, 16)
        pool.memset(z1[0:1, 0, :], 0.0).then_inc(z_conv, 1)
        pool.memset(z2[0:2, 0, :], 0.0).then_inc(z_conv, 1)
        pool.wait_ge(z_conv, 3)
        pool.dma_start(z1[1:P, :, :], Bh[0:P - 1, :, :]).then_inc(shift_in, 16)
        pool.dma_start(z1[0:1, 1, :], Bh[P - 1:P, 0, :]).then_inc(shift_in, 16)
        pool.dma_start(z2[2:P, :, :], Bh[0:P - 2, :, :]).then_inc(shift_in, 16)
        pool.dma_start(z2[0:2, 1, :], Bh[P - 2:P, 0, :]).then_inc(shift_in, 16)
        pool.wait_ge(cw_in, 16)
        pool.wait_ge(shift_in, 64)
        ch.link(pool.tensor_tensor(yb[:, :, :], z2[:, :, :], rep(cwB[:, 0, :], 0, J), ALU.mult))
        ch.link(pool.tensor_tensor(z1[:, :, :], z1[:, :, :], rep(cwB[:, 1, :], 0, J), ALU.mult))
        ch.link(pool.tensor_tensor(yb[:, :, :], yb[:, :, :], z1[:, :, :], ALU.add))
        ch.link(pool.tensor_tensor(Bh[:, :, :], Bh[:, :, :], rep(cwB[:, 2, :], 0, J), ALU.mult))
        ch.link(pool.tensor_tensor(yb[:, :, :], yb[:, :, :], Bh[:, :, :], ALU.add))
        pool.tensor_tensor(Bb[:, :, :], Bb[:, :, :], yb[:, :, :], ALU.mult).then_inc(ob_ready, 1)
        pool.wait_ge(tb_done, TB["out1"])
        pool.dma_start(gF[:, :], spread(A["norm_ffn"], D)).then_inc(gF_in, 16)
        for b in range(FB):
            cs = slice(b * W, (b + 1) * W)
            if b < 2:
                pool.dma_start(xrb[:, b % 2, :, :], rows(A["x"][0])[:, :, cs]).then_inc(xr1_in[b % 2], 16)
        for b in range(FB):
            cs = slice(b * W, (b + 1) * W)
            done = 2 * ((BLK["out1"] + b) // 2) + 2
            pool.wait_ge(acc_out[(BLK["out1"] + b) % 2], done)
            pool.dma_start(rows(scr_x1)[:, :, cs], x1b[:, b % 2, :, :]).then_inc(x1_st[b % 2], 16)
            if b + 2 < FB:
                cs = slice((b + 2) * W, (b + 3) * W)
                pool.dma_start(xrb[:, b % 2, :, :], rows(A["x"][0])[:, :, cs]).then_inc(xr1_in[b % 2], 16)
        for n in range(2):
            pool.wait_ge(x1_st[n], 32)
        for b in range(FB):
            cs = slice(b * W, (b + 1) * W)
            if b == 0:
                pool.wait_ge(mm_done, 2 * PLAN["ffn"][0])
            done = 2 * ((BLK["down"] + b) // 2) + 2
            pool.dma_start(xr2[:, :, :], rows(scr_x1)[:, :, cs]).then_inc(xr2_in, 16)
            pool.wait_ge(acc_out[(BLK["down"] + b) % 2], done)
            pool.dma_start(rows(scr_x2)[:, :, cs], x2b[:, :, :]).then_inc(x2_st, 16)
        for n, g in enumerate((A["attn_q_gain_2"], A["attn_k_gain_2"])):
            pool.dma_start(gn[:, n, :], spread(g, P)).then_inc(tab_in, 16)
            for q in range(4):
                pool.dma_start(gn[:, 2 + n, 32 * q:32 * q + 32],
                               bass.AP(g.tensor, 32 * (q ^ 1), [[0, P], [1, 32]])).then_inc(tab_in, 16)
        pool.wait_ge(mm_done, 2 * PLAN["in2"][0])
        for n in range(2):
            pool.dma_start(tabs[2 * n][:, :, :, :], A["rope_c"]).then_inc(tab_in, 16)
            pool.dma_start(tabs[2 * n + 1][:, :, :, :], A["rope_s"]).then_inc(tab_in, 16)
        pool.wait_ge(tab_in, 16 * 14)
        for n in range(4):
            g = (0, 2, 1, 3)[n]
            t = tabs[n][:, :, :, :].rearrange("p j h d -> p (j h) d")
            pool.tensor_tensor(t, t, rep(gn[:, g, :], 0, 8), ALU.mult).then_inc(tab_ready, 1)
        pool.wait_ge(tab_ready, 4)
        for n, (b, e, kind, g) in enumerate(ROT):
            pool.wait_ge(q_norm, n + 1)
            if n:
                pool.wait_ge(rot, n)
            for ins in swapped(pool, tb[:, :, :], xq[:, :, :], flat(tabs[3 if kind == "k" else 1][:, :, :, :]), 32):
                ch.link(ins)
            pool.sem_inc(q_swap, 1)
        pool.wait_ge(x2_st, 16 * FB)
        pool.wait_ge(tb_done, TB["out2"])
        pool.dma_start(lnG[:, :], spread(A["ln_gain_2"][0], D)).then_inc(ln_in, 16)
        pool.dma_start(lnB[:, :], spread(A["ln_bias_2"][0], D)).then_inc(ln_in, 16)
        for b in range(FB):
            if b >= 2:
                pool.wait_ge(acc_out[(BLK["out2"] + b) % 2], 2 * ((BLK["out2"] + b) // 2))
            pool.dma_start(xr3[:, b % 2, :, :], rows(scr_x2)[:, :, b * W:(b + 1) * W]).then_inc(xr3_in[b % 2], 16)
        pool.wait_ge(mm_done, 2 * PLAN["ret"][0])
        pool.dma_start(dpos[:, :, :], A["dist"][:, 0:2, :]).then_inc(dist_in, 16)
        pool.dma_start(dneg[:, :, :], A["dist"][:, 2:4, :]).then_inc(dist_in, 16)
        pool.dma_start(lg[:, 0, :], spread(A["ret_decay_exp_2"], 2 * RH)).then_inc(dist_in, 16)
        pool.wait_ge(x3_ready, FB * J)
        pool.dma_start(rc[:, :, :], A["rope2_c"]).then_inc(rr_in, 16)
        pool.dma_start(rs_[:, :, :], A["rope2_s"]).then_inc(rr_in, 16)
        pool.dma_start(rows(scr_x3), X3[:, :, :]).then_inc(x3_st, 16)
        pool.wait_ge(x3_st, 16)
        pool.wait_ge(tb_done, TB["ret"] + 2 * RH)
        pool.dma_start(lnG2[:, :], spread(A["ln_gain_2"][1], D)).then_inc(ln2_in, 16)
        pool.dma_start(lnB2[:, :], spread(A["ln_bias_2"][1], D)).then_inc(ln2_in, 16)
        for b in range(FB):
            if b >= 2:
                pool.wait_ge(acc_out[(BLK["out3"] + b) % 2], 2 * ((BLK["out3"] + b) // 2))
            pool.dma_start(xr4[:, b % 2, :, :], rows(scr_x3)[:, :, b * W:(b + 1) * W]).then_inc(xr4_in[b % 2], 16)

    @block.scalar
    def _(act):
        ch = Chain(act, act_c)

        def rstd(ms, ms_sem, n, done):
            act.wait_ge(ms_sem, n)
            ch.link(act.activation(ms, ms, ACT.Ln))
            act.activation(ms, ms, ACT.Exp, scale=-0.5).then_inc(done, 1)

        for fb in range(FB):
            cs = slice(fb * W, (fb + 1) * W)
            act.dma_start(gB[:, cs], spread(A["norm_mix"], W, fb * W)).then_inc(g_in[fb], 16)
            if fb == 0:
                act.dma_start(cst[:, :, :], A["cst"]).then_inc(cst_in, 16)

        def out1_block(b):
            _, n, dst = BLOCKS1[b]
            block_done(act, "in1", 4 * b + 3)
            if b == 0:
                act.wait_ge(rs1, 1)
            if dst is Bb:
                act.wait_ge(vscr, 16)
            for j in range(J):
                f = ACT.Gelu_apprx_tanh if dst in (Cu, Cv) else ACT.Copy
                act.activation(dst[:, j, :n], ACC[b % 2][j][:, :n], f, scale=rstd1[:, j:j + 1]).then_inc(acc_out[b % 2], 1)

        for h in range(2):
            split_hi(act, "in1", h // 2, h % 2)
        for n in range(2):
            tr_act(act, n, part(T1H, n // 2, n % 2), k=n)
        for h in range(2, 4):
            split_hi(act, "in1", h // 2, h % 2)
        for n in range(2, 8):
            tr_act(act, n, part(T1H, n // 2, n % 2), k=n)
        for b in range(NB1):
            for h in range(8):
                if 8 * b + h >= 4:
                    split_hi(act, "in1", 4 * b + h // 2, h % 2, BLOCKS1[b][1])
                if b == 0 and h == 4:
                    for fb in range(FB):
                        for j in range(J):
                            ch.link(act.activation(Aq[:, 0, :], X[:, j, fb * W:(fb + 1) * W], ACT.Square,
                                                   accum_out=ssx[:, 4 * j + fb:4 * j + fb + 1]))
                    act.sem_inc(ssx_done, 1)
                if b == 0 and h == 6:
                    rstd(rstd1, ms1, 1, rs1)
                if h == 3 and b:
                    out1_block(b - 1)
        out1_block(NB1 - 1)
        act.wait_ge(acc_out[0], 12)

        for n in range(2):
            act.activation(zd[:, :, :, n, :], Akv[:, :, 0:4 * HD].rearrange("p j (u d) -> p j u d", d=HD), ACT.Copy).then_inc(zd_ready, 1)
        rstd(ntmp, nsa_ms, 1, nsa_rs)
        act.activation(gtmp, Akw[:, :, 256:KV1W], ACT.Exp, scale=-1.0).then_inc(gexp, 1)
        for j in range(J):
            act.wait_ge(qk_T, j + 1)
            act.activation(qT[:, :, j * P:(j + 1) * P], bank[j].rearrange("p (r t) -> p r t", r=4), ACT.Copy).then_inc(qkT_out, 1)
        act.wait_ge(qk_T, 3)
        act.activation(kT[:, :, :], bank[2].rearrange("p (k t) -> p k t", k=2), ACT.Copy).then_inc(qkT_out, 1)
        act.wait_ge(cmp1, 1)
        act.activation(hT[0:HD, :].rearrange("p (i n) -> p i n", i=2), bank[7][0:HD, 0:64].rearrange("p (i n) -> p i n", i=2)[:, :, 0:2 * NCMP],
                       ACT.Gelu_apprx_tanh).then_inc(hT_ready, 1)
        rstd(cmx[0:NCMP, 0:2], kc_ms, 1, kc_rs)
        act.wait_ge(kc_T, 1)
        act.activation(kcT[:, 0:NCMP], bank[6][:, 0:NCMP], ACT.Copy).then_inc(kcT_out, 1)
        act.wait_ge(cs_sub, 2)
        act.activation(pcm[:, :, 0:NCMP], pcm[:, :, 0:NCMP], ACT.Exp).then_inc(cs_exp, 1)
        for n in range(4):
            act.wait_ge(pc_T, n + 1)
            act.activation(PcT[:, 4 * n:4 * n + 4, :], bank[n][0:NCMP, :].rearrange("p (u t) -> p u t", u=4), ACT.Copy).then_inc(pcT_out, 1)
        for k in range(NH + 1):
            if k < NH:
                for kind in range(2):
                    act.wait_ge(s_max, 2 * k + kind + 1)
                    if kind == 0 and k >= 2:
                        act.wait_ge(p_T, 2 * (k - 1))
                    for j, (a, z) in enumerate(SW):
                        c = 4 * (k % 2) + 2 * kind + j
                        act.activation(PB[:, k % 2, kind, a:z] if j else PB[:, k % 2, kind, 0:P],
                                       kbank(k, kind)[:, P:3 * P] if j else kbank(k, kind)[:, 0:P], ACT.Exp,
                                       bias=nmx[:, c:c + 1], accum_out=nsum[:, c:c + 1]).then_inc(s_exp, 1)
            if k >= 1:
                for kind in range(2):
                    act.wait_ge(p_T, 2 * (k - 1) + kind + 1)
                    if kind == 0 and k >= 3:
                        act.wait_ge(nsa_pv, k - 2)
                    act.activation(PT[:, (k - 1) % 2, kind, :], bank[4 + kind][:, 0:384], ACT.Copy).then_inc(pT_out, 1)
        act.wait_ge(nsa_pv, NH)
        for j in range(J):
            act.activation(Aq[:, j, :], bank[6 + j], ACT.Copy).then_inc(nsa_o, 1)

        for n in range(4):
            act.wait_ge(d_T, n + 1)
            dst = (dqT, dkT)[n // 2][:, :, (n % 2) * P:(n % 2 + 1) * P]
            act.activation(dst, bank[n].rearrange("p (r t) -> p r t", r=4), ACT.Copy,
                           scale=HD ** -0.5 if n < 2 else 1.0).then_inc(dT_out, 1)
        for k in range(NH + 1):
            if k < NH:
                act.wait_ge(z_full, k + 1)
                if k >= 2:
                    act.wait_ge(d_arg, k - 1)
                lb = LB[:, k % 2, :]
                ch.link(act.activation(lb, bank[k % 4][:, 0:384], ACT.Abs))
                ch.link(act.activation(lb, lb, ACT.Exp, scale=-1.0))
                act.activation(lb, lb, ACT.Ln, bias=1.0).then_inc(d_log, 1)
            if k >= 1:
                act.wait_ge(d_cap, k)
                act.activation(AR[:, (k - 1) % 2, :], AR[:, (k - 1) % 2, :], ACT.Exp).then_inc(d_a, 1)
        for n in range(2):
            act.wait_ge(w_T, n + 1)
            act.activation(WT[:, 4 * n:4 * n + 4, :], bank[4 + n].rearrange("p (h t) -> p h t", h=4), ACT.Copy).then_inc(wT_out, 1)
        rstd(brs, cv_ms, 1, cv_rs)
        act.wait_ge(d_pv, NH)
        for j in range(J):
            act.activation(Dq[:, j, :], bank[6 + j], ACT.Copy).then_inc(d_o, 1)
        for g, (src, s_, n) in enumerate(((Aq, nsa_o, 2), (Bb, ob_ready, 1), (Cu, oc_ready, NH), (Dq, d_o, 2))):
            act.wait_ge(s_, n)
            for j in range(J):
                ch.link(act.activation(junk[:, :], src[:, j, :], ACT.Square, accum_out=gss[:, 2 * g + j:2 * g + j + 1]))
        act.sem_inc(g_sq, 1)
        rstd(grs, g_ms, 1, g_rs)
        for n in range(8):
            tr_act(act, TB["mix"] + n, part(T2aH, n // 2, n % 2), k=n)

        def x1_squares(b):
            act.wait_ge(acc_out[(BLK["out1"] + b) % 2], 2 * ((BLK["out1"] + b) // 2) + 2)
            for j in range(J):
                ch.link(act.activation(junk2[:, :], x1b[:, b % 2, j, :], ACT.Square, accum_out=ss1[:, 4 * j + b:4 * j + b + 1]))
            act.sem_inc(x1_sq, 1)

        for b in range(FB):
            for h in range(8):
                split_hi(act, "out1", 4 * b + h // 2, h % 2)
                if b and h == 4:
                    x1_squares(b - 1)
                if b and h == 7:
                    for j in range(J):
                        tr_act(act, TB["out1"] + 2 * (b - 1) + j, part(T1H, b - 1, j), k=j)

        def ffn(f, first):
            for h in range(16):
                split_hi(act, "ffn", h // 2, h % 2, i=f)
                if first and h == 1:
                    x1_squares(FB - 1)
                if first and h == 3:
                    for j in range(J):
                        tr_act(act, TB["out1"] + 6 + j, part(T1H, 3, j), k=j)
                if first and h == 4:
                    rstd(rstd2, ms2, 1, rs2)
                if not first and h == 7:
                    for j in range(J):
                        n = f * 2 + (TB["ffn"] - 2 + j)
                        tr_act(act, n, T2bH[:, bass.ds(f * 4 - 4, 4), j * P:(j + 1) * P], k=j)
                if first and h == 11:
                    act.wait_ge(x1_st[0], 32)
                    act.wait_ge(x1_st[1], 32)
                if h == 11:
                    block_done(act, "ffn", 3, f)
                    if not first:
                        act.wait_ge(acc_out[(BLK["ffn"] + 1) % 2], f * 2 + 2 * ((BLK["ffn"] + 1) // 2))
                    for j in range(J):
                        act.activation(sg[:, j, :], ACC[BLK["ffn"] % 2][j], ACT.Silu, scale=rstd2[:, j:j + 1]).then_inc(acc_out[BLK["ffn"] % 2], 1)

        ffn(0, True)
        with act.Fori(1, NF) as f:
            ffn(f, False)

        for b in range(FB):
            for h in range(22):
                split_hi(act, "down", 11 * b + h // 2, h % 2)
                if b == 0 and h == 7:
                    for j in range(J):
                        tr_act(act, TB["ffn"] + 20 + j, part(T2bH, 10, j), k=j)
                if b and h == 7:
                    for j in range(J):
                        tr_act(act, TB["down"] + 2 * (b - 1) + j, part(T1H, b - 1, j), k=j)

        def exps(g, a):
            u = 4 * g + a
            act.wait_ge(a_max, u + 1)
            if u >= 2:
                act.wait_ge(a_PT, u - 1)
            for j in range(J):
                c = 2 * (u % 2) + j
                act.activation(PA[:, u % 2, j, :], bank[6][:, j * T:(j + 1) * T], ACT.Exp, bias=nmx[:, c:c + 1],
                               accum_out=nsum[:, c:c + 1]).then_inc(a_exp, 1)

        def pt_out(u):
            act.wait_ge(a_PT, u + 1)
            if u >= 2:
                act.wait_ge(a_PV, u - 1)
            act.activation(PTa[:, u % 2, :, :], bank[7].rearrange("p (s t) -> p s t", s=2), ACT.Copy).then_inc(a_PTo, 1)

        def in2_at(p):
            if p == 3:
                for j in range(J):
                    tr_act(act, TB["down"] + 6 + j, part(T1H, 3, j), k=j)
            for b, (kind, g) in enumerate(BLOCKS2):
                if p == 8 * b + 11:
                    B = BLK["in2"] + b
                    block_done(act, "in2", 4 * b + 3)
                    dst = {"q": xq, "k": xq, "v": vA, "g": gA}[kind]
                    n_rot = [r[0] for r in ROT]
                    if kind in "qk" and n_rot.index(b):
                        act.wait_ge(rot, n_rot.index(b))
                    if kind == "g" and g:
                        act.wait_ge(a_og, 2 * g)
                    for j in range(J):
                        act.activation(dst[:, j, :], ACC[B % 2][j], ACT.Silu if kind == "g" else ACT.Copy).then_inc(acc_out[B % 2], 1)
            for n, (b, e, kind, g) in enumerate(ROT):
                if p == e:
                    act.wait_ge(acc_out[(BLK["in2"] + b) % 2], 2 * ((BLK["in2"] + b) // 2) + 2)
                    if n:
                        act.wait_ge(rot_T, 2 * n)
                    act.activation(ta[:, :, :], xq[:, :, :], ACT.Square).then_inc(q_sq, 1)
                if p == e + 1:
                    rstd(nrx, q_ms, n + 1, q_rs)
                for j in range(J):
                    if p == e + 7 + 2 * j:
                        act.wait_ge(rot_T, 2 * n + j + 1)
                        dst = kTa[:, :, j * P:(j + 1) * P] if kind == "k" else qTa[:, g % 2, :, j * P:(j + 1) * P]
                        act.activation(dst, bank[4].rearrange("p (a t) -> p a t", a=4), ACT.Copy,
                                       scale=1.0 if kind == "k" else AD ** -0.5).then_inc(rotT_out, 1)
            for g in range(AKV):
                for a in range(4):
                    if p == S_AT[g] + 3 * a + 2:
                        exps(g, a)
                    if p == S_AT[g] + 3 * a + 5:
                        pt_out(4 * g + a)
                for j in range(J):
                    if p == OT_AT[g][j] + 3:
                        tr_act(act, TB["in2"] + 2 * g + j, part(T2cH, g, j), (4, 4), j)

        for p in range(80):
            split_hi(act, "in2", p // 2, p % 2)
            in2_at(p)
        for b in range(FB):
            for h in range(8):
                split_hi(act, "out2", 4 * b + h // 2, h % 2)
                in2_at(80 + 8 * b + h)
        for h in range(3):
            split_hi(act, "ret", h // 2, h % 2)
        rstd(brs, ln_ms, 1, ln_rs)

        def ret(i, rc_, first):
            def rstd_(ms, ms_sem, n, done):
                act.wait_ge(ms_sem, n)
                rc_.link(act.activation(ms, ms, ACT.Ln))
                act.activation(ms, ms, ACT.Exp, scale=-0.5).then_inc(done, 1)

            def gate(e, k):
                n = i * 2 + (e + 2 * k)
                block_done(act, "ret", 12 * e + 11, i + k if k else i)
                B = BLK["ret"] + 3 * e + 2
                for j in range(J):
                    act.activation(gR[:, j, :], ACC[B % 2][j], ACT.Silu).then_inc(acc_out[B % 2], 1)

            def tr(e, k):
                for j in range(J):
                    n = i * 4 + (4 * k + 2 * e + j)
                    tr_act(act, n + TB["ret"], T2dH[:, bass.ds(i * 8 + (8 * k + 4 * e), 4), j * P:(j + 1) * P] if not isinstance(i, int)
                           else part(T2dH, 2 * (i + k) + e, j), (4, 6), j)

            for h in range(48):
                e, p = h // 24, h % 24
                if not first or h >= 3:
                    split_hi(act, "ret", h // 2, h % 2, i=i)
                if first and 2 <= h < 8:
                    for n in ((0, 1), (2, 3), (4,), (5,), (6,), (7,))[h - 2]:
                        tr_act(act, TB["out2"] + n, part(T1H, n // 2, n % 2), (4, 5, 6, 7), n)
                if first and h == 6:
                    act.wait_ge(dist_in, 48)
                    rc_.link(act.activation(lg[:, 1, :], lg[:, 0, :], ACT.Exp, scale=-math.log(2.0)))
                    rc_.link(act.activation(lg[:, 2, :], lg[:, 1, :], ACT.Copy, scale=-1.0, bias=1.0))
                    act.activation(lg[:, 5, :], lg[:, 2, :], ACT.Ln).then_inc(lg1, 1)
                if first and 9 <= h < 9 + RH:
                    m = h - 9
                    act.wait_ge(mt_ready, m + 1)
                    act.activation(MM[:, m, :, :], mt[:, m % 2, :].rearrange("p (s t) -> p s t", s=2), ACT.Exp).then_inc(mm_ready, 1)
                if p == 11:
                    block_done(act, "ret", 12 * e + 3, i)
                    B = BLK["ret"] + 3 * e
                    if not first or e:
                        act.wait_ge(tb_done, i * 4 + (TB["ret"] + 2 * e))
                    for j in range(J):
                        act.activation(xr[:, j, :], ACC[B % 2][j], ACT.Copy).then_inc(acc_out[B % 2], 1)
                if p == 17:
                    for j in range(J):
                        act.wait_ge(r_T, i * 4 + (2 * e + j + 1))
                        v = bank[4 + j].rearrange("p (k d t) -> p k d t", k=2, d=2)
                        act.activation(rT[:, 0, :, j * P:(j + 1) * P], v[:, 0, :, :], ACT.Copy).then_inc(r_Tout, 1)
                        act.activation(rT[:, 1, :, j * P:(j + 1) * P], v[:, 1, :, :], ACT.Copy, scale=RD ** -0.5).then_inc(r_Tout, 1)
                if p == 19:
                    block_done(act, "ret", 12 * e + 7, i)
                    B = BLK["ret"] + 3 * e + 1
                    if not first or e:
                        act.wait_ge(r_out, i * 2 + e)
                    for j in range(J):
                        act.activation(vR[:, j, :], ACC[B % 2][j], ACT.Copy).then_inc(acc_out[B % 2], 1)
                if h == 24 or (h == 0 and not first):
                    rstd_(brs, r_ms, i * 2 + e, r_rs)
                if h == 27:
                    gate(0, 0)
                if h == 31:
                    tr(0, 0)
                if h == 3 and not first:
                    gate(1, -1)
                if h == 7 and not first:
                    tr(1, -1)

        RETA = (3, 2)
        rc_ = Chain(act, reta_c)
        ret(0, rc_, True)
        assert rc_.n == RETA[0], rc_.n
        with act.Fori(1, RH // 2) as i:
            rc_.base, rc_.n = i * RETA[1] + (RETA[0] - RETA[1]), 0
            ret(i, rc_, False)
            assert rc_.n == RETA[1], rc_.n
        last = RH // 2
        for b in range(FB):
            for h in range(16):
                split_hi(act, "out3", 8 * b + h // 2, h % 2)
                if b == 0 and h == 0:
                    rstd(brs, r_ms, RH, r_rs)
                if b == 0 and h == 3:
                    block_done(act, "ret", 23, last - 1)
                    B = BLK["ret"] + 5
                    for j in range(J):
                        act.activation(gR[:, j, :], ACC[B % 2][j], ACT.Silu).then_inc(acc_out[B % 2], 1)
                if b == 0 and h == 7:
                    for j in range(J):
                        tr_act(act, TB["ret"] + 2 * RH - 2 + j, part(T2dH, RH - 1, j), (4, 6), j)
        rstd(brs, ln_ms, 2, ln_rs)

    @block.vector
    def _(dve):
        ch = Chain(dve, dve_c)
        tt, ts, stt = dve.tensor_tensor, dve.tensor_scalar, dve.scalar_tensor_tensor
        MUL, ADD, SUB, MAX, MIN = ALU.mult, ALU.add, ALU.subtract, ALU.max, ALU.min

        def gain(fb):
            dve.wait_ge(x_in[fb], 16)
            dve.wait_ge(g_in[fb], 16)
            cs = slice(fb * W, (fb + 1) * W)
            tt(XG[:, :, cs], X[:, :, cs], rep(gB[:, cs], 0, J), MUL).then_inc(xg_ready, 1)

        def tr1(n):
            tr_dve(dve, n, part(T1H, n // 2, n % 2), part(T1L, n // 2, n % 2), k=n)

        gain(0)
        for h in range(2):
            split_lo(dve, "in1", h // 2, h % 2)
        gain(1)
        tr1(0), tr1(1)
        for h in range(2, 4):
            split_lo(dve, "in1", h // 2, h % 2)
        gain(2)
        tr1(2), tr1(3)
        gain(3)
        for n in range(4, 8):
            tr1(n)
        for b in range(NB1):
            for h in range(8):
                if 8 * b + h >= 4:
                    split_lo(dve, "in1", 4 * b + h // 2, h % 2, BLOCKS1[b][1])
                if b == 0 and h == 5:
                    dve.wait_ge(ssx_done, 1)
                    ch.link(dve.tensor_reduce(rstd1, ssx.rearrange("p (j f) -> p j f", j=J), AX, ADD))
                    ts(rstd1, rstd1, 1.0 / D, RMS_EPS, MUL, ADD).then_inc(ms1, 1)
                    dve.wait_ge(vrow_ps, 1)
                    dve.tensor_copy(vrow[:, :], bank[6][0:NH, :]).then_inc(vrow_sb, 1)
                    dve.wait_ge(par_T, 1)
                    dve.tensor_copy(posT, bank[7][:, 0:HD]).then_inc(par_out, 1)
                    dve.tensor_copy(sgubT, bank[7][:, HD:HD + NH]).then_inc(par_out, 1)
                    ch.link(ts(qg8, qg8, HD ** -0.5, None, MUL))

        dve.wait_ge(acc_out[0], 12)
        dve.wait_ge(acc_out[1], 10)
        ks, kw = Akv[:, :, 256:384], Akw[:, :, 0:128]
        ch.link(tt(TQ[:, :, :], Aq[:, :, :], Aq[:, :, :], MUL))
        ch.link(tt(TK[:, 0, :, :], ks, ks, MUL))
        ch.link(tt(TK[:, 1, :, :], kw, kw, MUL))
        ch.link(dve.tensor_reduce(nss[:, 0:16], heads(TQ[:, :, :], HD), AX, ADD))
        ch.link(dve.tensor_reduce(nss[:, 16:24], TK[:, :, :, :].rearrange("p k j (h d) -> p (k j h) d", d=HD), AX, ADD))
        ts(ntmp, nss, 1.0 / HD, RMS_EPS, MUL, ADD).then_inc(nsa_ms, 1)
        for i in range(2):
            zb = bank[(3, 6)[i]]
            dve.wait_ge(z_T, i + 1)
            tt(zz[0:HD, i, :, :].rearrange("p g (n l) -> p (g n) l", l=CS), zb[0:HD, :].rearrange("p (n l) -> p n l", l=CS),
               rep(posT[0:HD, i * CL:i * CL + CS], 0, NG * T // CS), ADD).then_inc(zz_ready, 1)
            for g in range(NG):
                tt(zz[HD:P, i, g, 0:T - CS].rearrange("p (n l) -> p n l", l=CS),
                   zb[HD:P, g * T + CS:(g + 1) * T].rearrange("p (n l) -> p n l", l=CS),
                   rep(posT[HD:P, i * CL + CS:(i + 1) * CL], 0, NCMP), ADD).then_inc(zz_ready, 1)
        dve.wait_ge(nsa_rs, 1)
        ch.link(tt(heads(Aq[:, :, :], HD), heads(Aq[:, :, :], HD), rep(ntmp[:, 0:16], 1, HD), MUL))
        for j in range(J):
            tt(TQ[:, j, :].rearrange("p (r g d) -> p g r d", r=4, g=NG), Aq[:, j, :].rearrange("p (g r d) -> p g r d", r=4, g=NG),
               rep(rep(qg8, 0, 4), 0, NG), MUL).then_inc(nsa_qk, 1)
        for n, src in enumerate((ks, kw)):
            tt(TK[:, n, :, :].rearrange("p j (h d) -> p j h d", d=HD), src.rearrange("p j (h d) -> p j h d", d=HD),
               rep(ntmp[:, 16 + 4 * n:20 + 4 * n].rearrange("p (j h) -> p j h", j=J), 2, HD), MUL).then_inc(dve_c, 1)
        ch.n += 2
        dve.wait_ge(dve_c, ch.n)
        kf = TK[:, :, :, :].rearrange("p k j (h d) -> p (k j h) d", d=HD)
        tt(kf, kf, rep(kg, 0, 8), MUL).then_inc(nsa_qk, 1)
        dve.wait_ge(gexp, 1)
        ch.link(ts(gsig, gtmp, 1.0, None, ADD))
        ch.link(dve.reciprocal(gsig, gsig))
        gv = gsig.rearrange("p (j h k) -> p j h k", j=J, h=NH)
        dve.wait_ge(cmp2, 1)
        ch.link(dve.tensor_copy(KVC[:, :, :, :], bank[3][0:NCMP, 0:4 * HD].rearrange("p (i g d) -> p i g d", i=2, g=NG)))
        kcv = KVC[:, 0, :, :]
        sq = TQ[0:NCMP, 0, 0:P].rearrange("p (g d) -> p g d", g=NG)
        dve.wait_ge(qk_T, 3)
        ch.link(tt(sq, kcv, kcv, MUL))
        ch.link(dve.tensor_reduce(cmx[0:NCMP, 0:2], sq, AX, ADD))
        ts(cmx[0:NCMP, 0:2], cmx[0:NCMP, 0:2], 1.0 / HD, RMS_EPS, MUL, ADD).then_inc(kc_ms, 1)
        dve.wait_ge(kc_rs, 1)
        ch.link(tt(sq, kcv, rep(cmx[0:NCMP, 0:2], 1, HD), MUL))
        tt(sq, sq, rep(kg[0:NCMP, :], 0, NG), MUL).then_inc(kcn_ready, 1)
        dve.wait_ge(sg_in, 16)
        tt(SG[:, :, :], SG[:, :, :], rep(tril, 0, NH), MUL).then_inc(sg_ready, 1)
        dve.wait_ge(cs_full, 1)
        cs = [bank[6 + g][:, 0:128].rearrange("p (u n) -> p u n", n=16)[:, :, 0:NCMP] for g in range(NG)]
        for g in range(NG):
            ch.link(dve.tensor_reduce(cmx[:, 8 * g:8 * g + 8], cs[g], AX, MAX))
        ch.link(ts(cmx, cmx, 0.1 * NEG, None, MAX))
        for g in range(NG):
            tt(pcm[:, 8 * g:8 * g + 8, 0:NCMP], cs[g], rep(cmx[:, 8 * g:8 * g + 8], 1, NCMP), SUB).then_inc(cs_sub, 1)
        dve.wait_ge(cs_exp, 1)
        ch.link(dve.tensor_reduce(csum, pcm[:, :, 0:NCMP], AX, ADD))
        ch.link(ts(csum, csum, 1e-30, None, MAX))
        ch.link(dve.reciprocal(csum, csum))
        ch.link(tt(crw.rearrange("p (h j) -> p h j", j=J), csum.rearrange("p (h j) -> p h j", j=J),
                   gv[:, :, :, 0].rearrange("p j h -> p h j"), MUL))
        tt(pcm[:, :, 0:NCMP], pcm[:, :, 0:NCMP], rep(crw, 1, NCMP), MUL).then_inc(pc_ready, 1)
        for k in range(NH + 1):
            if k < NH:
                for kind in range(2):
                    dve.wait_ge(s_full, 2 * k + kind + 1)
                    c = 4 * (k % 2) + 2 * kind
                    ch.link(dve.tensor_reduce(nmx[:, c:c + 1], kbank(k, kind)[:, 0:P], AX, MAX, negate=True))
                    dve.tensor_reduce(nmx[:, c + 1:c + 2], kbank(k, kind)[:, P:3 * P], AX, MAX, negate=True).then_inc(s_max, 1)
            if k >= 1:
                h, c = k - 1, 4 * ((k - 1) % 2)
                dve.wait_ge(s_exp, 4 * k)
                ch.link(dve.reciprocal(nsum[:, c:c + 4], nsum[:, c:c + 4]))
                ch.link(tt(nrw[:, c:c + 4].rearrange("p (k j) -> p k j", k=2), nsum[:, c:c + 4].rearrange("p (k j) -> p k j", k=2),
                           gv[:, :, h, 1:3].rearrange("p j k -> p k j"), MUL))
                for kind in range(2):
                    for j, (a, z) in enumerate(((0, P), (P, 3 * P))):
                        pb = PB[:, h % 2, kind, a:z]
                        ts(pb, pb, nrw[:, c + 2 * kind + j:c + 2 * kind + j + 1], None, MUL).then_inc(p_norm, 1)
        dve.wait_ge(msk_in, 32)
        for k in range(NH + 1):
            if k < NH:
                dve.wait_ge(d_log, k + 1)
                lb = LB[:, k % 2, :]
                ch.link(stt(lb, bank[k % 4][:, 0:384], 0.0, lb, MAX, ADD))
                tt(lb, lb, msk3[:, :], MUL).then_inc(d_sp, 1)
            if k >= 1:
                dve.wait_ge(d_arg, k)
                if k >= 3:
                    dve.wait_ge(d_pv, k - 2)
                tt(AR[:, (k - 1) % 2, :], bank[(k - 1) % 4][:, 0:384], cap3[:, :], MIN).then_inc(d_cap, 1)
        for j in range(J):
            ch.link(dve.bn_stats(bst[:, 6 * j:6 * j + 6], Cv[:, j, :]))
            ch.link(dve.bn_aggr(bag[:, 2 * j:2 * j + 2], bst[:, 6 * j:6 * j + 6]))
        ts(brs, bag.rearrange("p (j k) -> p j k", j=J)[:, :, 1], LN_EPS, None, ADD).then_inc(cv_ms, 1)
        dve.wait_ge(cv_rs, 1)
        for j in range(J):
            ts(Cv[:, j, :], Cv[:, j, :], bag[:, 2 * j:2 * j + 1], brs[:, j:j + 1], SUB, MUL).then_inc(cv_ready, 1)
        dve.wait_ge(par_out, 2)
        for h in range(NH):
            if h % 4 == 0:
                dve.wait_ge(sgu_full, h // 4 + 1)
            u = Cu[:, :, h * HD:(h + 1) * HD]
            stt(u, bank[h // 4][:, (h % 4) * P:(h % 4 + 1) * P].rearrange("p (j d) -> p j d", j=J), sgubT[:, h:h + 1], u,
                ADD, MUL).then_inc(oc_ready, 1)
        dve.wait_ge(g_sq, 1)
        ts(grs, gss, 1.0 / GW, RMS_EPS, MUL, ADD).then_inc(g_ms, 1)
        dve.wait_ge(g_rs, 1)
        dve.wait_ge(gg_in, 16)
        mixed = (Aq, Bb, Cu, Dq)
        for n in range(8):
            g, j = n // 2, n % 2
            stt(mixed[g][:, j, :], mixed[g][:, j, :], grs[:, n:n + 1], gB[:, g * W:(g + 1) * W], MUL, MUL).then_inc(mixed_ready, 1)
            if n >= 1:
                m = n - 1
                tr_dve(dve, TB["mix"] + m, part(T2aH, m // 2, m % 2), part(T2aL, m // 2, m % 2), k=m)
        tr_dve(dve, TB["mix"] + 7, part(T2aH, 3, 1), part(T2aL, 3, 1), k=7)

        def x1_block(b):
            B = BLK["out1"] + b
            block_done(dve, "out1", 4 * b + 3)
            dve.wait_ge(xr1_in[b % 2], 16 * (b // 2 + 1))
            if b >= 2:
                dve.wait_ge(x1_st[b % 2], 16 * (b // 2))
                dve.wait_ge(x1_sq, b - 1)
            for j in range(J):
                tt(x1b[:, b % 2, j, :], ACC[B % 2][j], xrb[:, b % 2, j, :], ADD).then_inc(acc_out[B % 2], 1)
            dve.wait_ge(acc_out[B % 2], 2 * (B // 2) + 2)
            dve.wait_ge(gF_in, 16)
            if b >= 2:
                dve.wait_ge(tb_full, TB["out1"] + 2 * (b - 1))
            tt(xgb[:, b % 2, :, :], x1b[:, b % 2, :, :], rep(gF[:, b * W:(b + 1) * W], 0, J), MUL).then_inc(xg2, 1)

        for b in range(FB):
            for h in range(8):
                split_lo(dve, "out1", 4 * b + h // 2, h % 2)
                if b and h == 3:
                    x1_block(b - 1)
                if b and h == 7:
                    for j in range(J):
                        tr_dve(dve, TB["out1"] + 2 * (b - 1) + j, part(T1H, b - 1, j), part(T1L, b - 1, j), k=j)

        def up(k, j, i):
            B = BLK["ffn"] + 1
            return stt(av[:, j, :], ACC[B % 2][j], rstd2[:, j:j + 1], sg[:, j, :], MUL, MUL)

        def gated(f):
            B = BLK["ffn"] + 1
            block_done(dve, "ffn", 7, f)
            dve.wait_ge(acc_out[BLK["ffn"] % 2], f * 2 + (2 * (BLK["ffn"] // 2) + 2) if not isinstance(f, int) else 2 * (BLK["ffn"] // 2) + 2 + 2 * f)
            dve.wait_ge(tb_full, f * 2 + TB["ffn"])
            for j in range(J):
                up(None, j, f).then_inc(acc_out[B % 2], 1)

        def ffn(f, first):
            for h in range(16):
                split_lo(dve, "ffn", h // 2, h % 2, i=f)
                if first and h == 0:
                    x1_block(FB - 1)
                if first and h == 2:
                    dve.wait_ge(x1_sq, FB)
                    ch.link(dve.tensor_reduce(rstd2, ss1.rearrange("p (j f) -> p j f", j=J), AX, ADD))
                    ts(rstd2, rstd2, 1.0 / D, RMS_EPS, MUL, ADD).then_inc(ms2, 1)
                if first and h == 3:
                    for j in range(J):
                        tr_dve(dve, TB["out1"] + 6 + j, part(T1H, 3, j), part(T1L, 3, j), k=j)
                if first and h == 9:
                    dve.wait_ge(x1_st[0], 32)
                    dve.wait_ge(x1_st[1], 32)
                if not first and h == 3:
                    gated(f - 1)
                if not first and h == 8:
                    for j in range(J):
                        cols_, ts_ = bass.ds(f * 4 - 4, 4), slice(j * P, (j + 1) * P)
                        tr_dve(dve, f * 2 + (TB["ffn"] - 2 + j), T2bH[:, cols_, ts_], T2bL[:, cols_, ts_], k=j)

        ffn(0, True)
        with dve.Fori(1, NF) as f:
            ffn(f, False)

        def x2_block(b):
            B = BLK["down"] + b
            block_done(dve, "down", 11 * b + 10)
            dve.wait_ge(xr2_in, 16 * (b + 1))
            if b:
                dve.wait_ge(x2_st, 16 * b)
                dve.wait_ge(tb_full, TB["down"] + 2 * b)
            for j in range(J):
                tt(x2b[:, j, :], ACC[B % 2][j], xr2[:, j, :], ADD).then_inc(acc_out[B % 2], 1)

        for b in range(FB):
            for h in range(22):
                split_lo(dve, "down", 11 * b + h // 2, h % 2)
                if b == 0 and h == 3:
                    gated(NF - 1)
                if b == 0 and h == 8:
                    for j in range(J):
                        tr_dve(dve, TB["ffn"] + 20 + j, part(T2bH, 10, j), part(T2bL, 10, j), k=j)
                if b and h == 3:
                    x2_block(b - 1)
                if b and h == 8:
                    for j in range(J):
                        tr_dve(dve, TB["down"] + 2 * (b - 1) + j, part(T1H, b - 1, j), part(T1L, b - 1, j), k=j)

        def max_of(u):
            dve.wait_ge(a_S, u + 1)
            c = 2 * (u % 2)
            dve.tensor_reduce(nmx[:, c:c + 2], bank[6].rearrange("p (j s) -> p j s", j=J), AX, MAX, negate=True).then_inc(a_max, 1)

        def head_out(u):
            g, a = u // 4, u % 4
            dve.wait_ge(a_PV, u + 1)
            c = 2 * (u % 2)
            ch.link(dve.reciprocal(nrw[:, c:c + 2], nsum[:, c:c + 2]))
            for j in range(J):
                ts(oA[:, g, j, a * P:(a + 1) * P], bank[5][:, j * P:(j + 1) * P], nrw[:, c + j:c + j + 1], None, MUL).then_inc(a_O, 1)

        def in2_at(p):
            if p == 0:
                x2_block(FB - 1)
            if p == 3:
                for j in range(J):
                    tr_dve(dve, TB["down"] + 6 + j, part(T1H, 3, j), part(T1L, 3, j), k=j)
            for n, (b, e, kind, g) in enumerate(ROT):
                C_ = flat(tabs[2 if kind == "k" else 0][:, :, :, :])
                if p == e + 1:
                    dve.wait_ge(q_sq, n + 1)
                    ch.link(dve.tensor_reduce(nsx, heads(ta[:, :, :], P), AX, ADD))
                    ts(nrx, nsx, 1.0 / AD, RMS_EPS, MUL, ADD).then_inc(q_ms, 1)
                if p == e + 2:
                    dve.wait_ge(q_rs, n + 1)
                    tt(heads(xq[:, :, :], P), heads(xq[:, :, :], P), rep(nrx, 1, P), MUL).then_inc(q_norm, 1)
                if p == e + 3:
                    dve.wait_ge(q_norm, n + 1)
                    if n == 0:
                        dve.wait_ge(tab_ready, 4)
                    ch.link(tt(ta[:, :, :], xq[:, :, :], C_, MUL))
                if p == e + 4:
                    dve.wait_ge(q_swap, n + 1)
                    tt(ta[:, :, :], ta[:, :, :], tb[:, :, :], ADD).then_inc(rot, 1)
            for g in range(AKV):
                for a in range(4):
                    if p == S_AT[g] + 3 * a + 2:
                        max_of(4 * g + a)
                    if p == S_AT[g] + 3 * a + 8:
                        head_out(4 * g + a)
                if p == 60 + 8 * g:
                    B = BLK["in2"] + 6 + g
                    dve.wait_ge(acc_out[B % 2], 2 * (B // 2) + 2)
                    dve.wait_ge(a_O, 8 * g + 8)
                    for j in range(J):
                        tt(oA[:, g, j, :], oA[:, g, j, :], gA[:, j, :], MUL).then_inc(a_og, 1)
                for j in range(J):
                    if p == OT_AT[g][j] + 3:
                        tr_dve(dve, TB["in2"] + 2 * g + j, part(T2cH, g, j), part(T2cL, g, j), (4, 4), j)

        for p in range(80):
            split_lo(dve, "in2", p // 2, p % 2)
            in2_at(p)

        def ln_block(ph, dst, res, res_in, b, cpb):
            B = BLK[ph] + b
            block_done(dve, ph, cpb * b + cpb - 1)
            dve.wait_ge(res_in[b % 2], 16 * (b // 2 + 1))
            for j in range(J):
                stt(dst[:, j, b * W:(b + 1) * W], res[:, b % 2, j, :], ALPHA, ACC[B % 2][j], MUL, ADD).then_inc(acc_out[B % 2], 1)
            dve.wait_ge(acc_out[B % 2], 2 * (B // 2) + 2)
            for j in range(J):
                c = 6 * (FB * j + b)
                ch.link(dve.bn_stats(bst[:, c:c + 6], dst[:, j, b * W:(b + 1) * W]))

        def ln_end(dst, layer, gain_in, G, Bv, ready, each):
            for j in range(J):
                ch.link(dve.bn_aggr(bag[:, 2 * j:2 * j + 2], bst[:, 24 * j:24 * j + 24]))
            ts(brs, bag.rearrange("p (j k) -> p j k", j=J)[:, :, 1], LN_EPS, None, ADD).then_inc(ln_ms, 1)
            dve.wait_ge(ln_rs, layer)
            dve.wait_ge(gain_in, 32)
            for n in range(FB * J):
                cs_, j = slice(n // J * W, (n // J + 1) * W), n % J
                d = dst[:, j, cs_]
                ch.link(stt(d, d, bag[:, 2 * j:2 * j + 1], G[:, cs_], SUB, MUL))
                stt(d, d, brs[:, j:j + 1], Bv[:, cs_], MUL, ADD).then_inc(ready, 1)
                each(n)

        for b in range(FB):
            for h in range(8):
                split_lo(dve, "out2", 4 * b + h // 2, h % 2)
                in2_at(80 + 8 * b + h)
                if b and h == 6:
                    ln_block("out2", X3, xr3, xr3_in, b - 1, 4)
        for h in range(3):
            split_lo(dve, "ret", h // 2, h % 2)
        ln_block("out2", X3, xr3, xr3_in, FB - 1, 4)

        def x3_tr(n):
            if n:
                m = n - 1
                tr_dve(dve, TB["out2"] + m, part(T1H, m // 2, m % 2), part(T1L, m // 2, m % 2), (4, 5, 6, 7), m)
            if n in (2, 4, 5, 6):
                h = {2: 3, 4: 4, 5: 5, 6: 6}[n]
                split_lo(dve, "ret", h // 2, h % 2)

        ln_end(X3, 1, ln_in, lnG, lnB, x3_ready, x3_tr)
        x3_tr(8)

        def ret(i, rc_, first):
            def stats(n):
                dve.wait_ge(r_out, n + 1)
                for j in range(J):
                    dve.bn_stats(bst[:, 6 * j:6 * j + 6], bank[(7, 5)[j]]).then_inc(rc_.s, 1)
                rc_.n += 2
                dve.wait_ge(rc_.s, rc_.base + rc_.n)
                v = bst[:, 0:12].rearrange("p (j k) -> p k j", j=J)
                mean, dif = bag.rearrange("p (j k) -> p k j", j=J)[:, 0, :], bag.rearrange("p (j k) -> p k j", j=J)[:, 1, :]
                rc_.link(tt(mean, v[:, 1, :], v[:, 4, :], ADD))
                rc_.link(tt(dif, v[:, 1, :], v[:, 4, :], SUB))
                rc_.link(tt(brs, v[:, 2, :], v[:, 5, :], ADD))
                rc_.link(ts(mean, mean, 0.5, None, MUL))
                rc_.link(tt(dif, dif, dif, MUL))
                rc_.link(ts(dif, dif, 0.25, LN_EPS, MUL, ADD))
                stt(brs, brs, 1.0 / RV, dif, MUL, ADD).then_inc(r_ms, 1)

            def norm(n):
                dve.wait_ge(r_rs, n + 1)
                for j in range(J):
                    ts(oR[:, j, :], bank[(7, 5)[j]], bag[:, 2 * j:2 * j + 1], brs[:, j:j + 1], SUB, MUL).then_inc(r_norm, 1)

            def gate(n, e, k):
                B = BLK["ret"] + 3 * e + 2
                dve.wait_ge(r_norm, n * 2 + 2)
                v = 2 * (B // 2) + 2 + 6 * k
                dve.wait_ge(acc_out[B % 2], i * 6 + v if not isinstance(i, int) else 6 * i + v)
                for j in range(J):
                    tt(oR[:, j, :], oR[:, j, :], gR[:, j, :], MUL).then_inc(r_og, 1)

            def tr(e, k):
                for j in range(J):
                    n = i * 4 + (4 * k + 2 * e + j)
                    if isinstance(i, int):
                        h_, l_ = part(T2dH, 2 * (i + k) + e, j), part(T2dL, 2 * (i + k) + e, j)
                    else:
                        c_, t_ = bass.ds(i * 8 + (8 * k + 4 * e), 4), slice(j * P, (j + 1) * P)
                        h_, l_ = T2dH[:, c_, t_], T2dL[:, c_, t_]
                    tr_dve(dve, n + TB["ret"], h_, l_, (4, 6), j)

            for h in range(48):
                e, p = h // 24, h % 24
                if not first or h >= 7:
                    split_lo(dve, "ret", h // 2, h % 2, i=i)
                hd = i * 2 + e
                if first and h == 7:
                    dve.wait_ge(lg1, 1)
                    y, u, d_, e_, l_ = (lg[:, n, :] for n in range(1, 6))
                    rc_.link(ts(d_, u, -1.0, 1.0, MUL, ADD))
                    rc_.link(ts(e_, d_, 0.0, None, ALU.is_equal))
                    rc_.link(tt(d_, d_, e_, ADD))
                    rc_.link(dve.reciprocal(d_, d_))
                    rc_.link(tt(d_, d_, y, MUL))
                    rc_.link(tt(l_, l_, d_, MUL))
                    rc_.link(tt(e_, e_, y, MUL))
                    rc_.link(tt(l_, l_, e_, SUB))
                if first and 8 <= h < 8 + RH:
                    m = h - 8
                    if m >= 2:
                        dve.wait_ge(mm_ready, m - 1)
                    b_ = mt[:, m % 2, :]
                    rc_.link(ts(b_, dpos[:, :, :].rearrange("p s t -> p (s t)"), lg[:, 5, m:m + 1], None, MUL))
                    stt(b_, dneg[:, :, :].rearrange("p s t -> p (s t)"), lg[:, 5, RH + m:RH + m + 1], b_, MUL, ADD).then_inc(mt_ready, 1)
                if p == 12:
                    B = BLK["ret"] + 3 * e
                    v = 2 * (B // 2) + 2
                    dve.wait_ge(acc_out[B % 2], v if first else i * 6 + v)
                    dve.wait_ge(rr_in, 32)
                    for ins in swapped(dve, rb[:, :, :], xr[:, :, :], rs_[:, :, :], 64):
                        ins.then_inc(rc_.s, 1)
                    rc_.n += 2
                    dve.wait_ge(rc_.s, rc_.base + rc_.n)
                    rc_.link(tt(xr[:, :, :], xr[:, :, :], rc[:, :, :], MUL))
                    tt(xr[:, :, :], xr[:, :, :], rb[:, :, :], ADD).then_inc(r_rot, 1)
                if p == 20:
                    dve.wait_ge(r_S, hd + 1)
                    if first and e == 0:
                        dve.wait_ge(mm_ready, RH)
                    M_ = MM[:, bass.ds(hd, 1), :, :].rearrange("p h s t -> p (h s) t") if not isinstance(i, int) else MM[:, hd, :, :]
                    tt(SM[:, :, :], bank[6].rearrange("p (s t) -> p s t", s=2), M_, MUL).then_inc(r_SM, 1)
                if h == 23:
                    stats(hd)
                if h == 24:
                    norm(i * 2)
                if h == 28:
                    gate(i * 2, 0, 0)
                if first and h == 30:
                    dve.wait_ge(x3_st, 16)
                if h == 31:
                    tr(0, 0)
                if h == 47:
                    stats(hd)
                if not first:
                    if h == 0:
                        norm(i * 2 - 1)
                    if h == 4:
                        gate(i * 2 - 1, 1, -1)
                    if h == 7:
                        tr(1, -1)

        RET = (8 + 8 + 6 + 16, 6 + 16)
        rc_ = Chain(dve, ret_c)
        ret(0, rc_, True)
        assert rc_.n == RET[0], rc_.n
        with dve.Fori(1, RH // 2) as i:
            rc_.base, rc_.n = i * RET[1] + (RET[0] - RET[1]), 0
            ret(i, rc_, False)
            assert rc_.n == RET[1], rc_.n

        for b in range(FB):
            for h in range(16):
                split_lo(dve, "out3", 8 * b + h // 2, h % 2)
                if b == 0 and h == 0:
                    dve.wait_ge(r_rs, RH)
                    for j in range(J):
                        ts(oR[:, j, :], bank[(7, 5)[j]], bag[:, 2 * j:2 * j + 1], brs[:, j:j + 1], SUB, MUL).then_inc(r_norm, 1)
                if b == 0 and h == 4:
                    B = BLK["out3"] - 1
                    dve.wait_ge(r_norm, 2 * RH)
                    dve.wait_ge(acc_out[B % 2], 2 * (B // 2) + 2)
                    for j in range(J):
                        tt(oR[:, j, :], oR[:, j, :], gR[:, j, :], MUL).then_inc(r_og, 1)
                if b == 0 and h == 7:
                    for j in range(J):
                        tr_dve(dve, TB["ret"] + 2 * RH - 2 + j, part(T2dH, RH - 1, j), part(T2dL, RH - 1, j), (4, 6), j)
                if b and h == 3:
                    ln_block("out3", X4, xr4, xr4_in, b - 1, 8)
        ln_block("out3", X4, xr4, xr4_in, FB - 1, 8)
        ln_end(X4, 2, ln2_in, lnG2, lnB2, x4_ready, lambda n: None)

    @block.tensor
    def _(pe):
        mm = pe.matmul

        def tr1(n):
            pe.wait_ge(xg_ready, n // 2 + 1)
            tr_pe(pe, n, XG[:, n % 2, (n // 2) * W:(n // 2 + 1) * W], k=n)

        def half1(p):
            b, h = p // 8, p % 8
            if b == 0 and h % 2 == 0:
                pe.wait_ge(tb_done, h + 2)
            products(pe, "in1", 4 * b + h // 2, h % 2, T1H, T1L, 4 * (h // 2), b, BLOCKS1[b][1], h == 0, h == 7)

        pe.wait_ge(cst_in, 16)
        tr1(0), tr1(1), half1(0), half1(1), tr1(2), tr1(3), half1(2), half1(3)
        for n in range(4, 8):
            tr1(n)
        half1(4)
        pe.wait_ge(oh_in, 32)
        mm(bank[6][0:NH, :], tabaug[:, :], onehot[:, :], start=True, stop=True).then_inc(vrow_ps, 1)
        pe.wait_ge(par_in, 160)
        pe.transpose(bank[7][:, 0:HD], prow[:, :], ident[0:HD, 0:HD])
        pe.transpose(bank[7][:, HD:HD + NH], sbrow[:, :], ident[0:NH, 0:NH]).then_inc(par_T, 1)
        for p in range(5, 8 * NB1):
            half1(p)

        pe.wait_ge(acc_out[0], 12)
        pe.wait_ge(acc_out[1], 10)
        pe.wait_ge(zd_ready, 2)
        for i in range(2):
            for g in range(NG):
                for j in range(J):
                    o = (2 * g + j) * P
                    m = pe.transpose(bank[(3, 6)[i]][:, o:o + P], zd[:, j, 2 * i + g, :, :].rearrange("p n d -> p (n d)"), ident)
            m.then_inc(z_T, 1)
        pe.wait_ge(nsa_qk, 2)
        for j in range(J):
            for r in range(4):
                m = pe.transpose(bank[j][:, r * P:(r + 1) * P], TQ[:, j, r * P:(r + 1) * P], ident)
            m.then_inc(qk_T, 1)
        pe.wait_ge(nsa_qk, 3)
        for kind in range(2):
            for j in range(J):
                o = (2 * kind + j) * P
                m = pe.transpose(bank[2][:, o:o + P], TK[:, kind, j, :], ident)
        m.then_inc(qk_T, 1)
        pe.wait_ge(zz_ready, 6)
        for i in range(2):
            for l in range(CS):
                m = mm(bank[7][0:HD, 32 * i:32 * i + 2 * NCMP], w1s[:, i, l, :], zz[:, i, :, l:l + CS * (NCMP - 1) + 1:CS],
                       start=l == 0, stop=l == CS - 1)
        m.then_inc(cmp1, 1)
        pe.wait_ge(hT_ready, 1)
        for i in range(2):
            for g in range(NG):
                o = (2 * i + g) * HD
                m = mm(bank[3][0:NCMP, o:o + HD], hT[0:HD, (2 * i + g) * NCMP:(2 * i + g + 1) * NCMP], w2s[:, i, :], start=True, stop=True)
        m.then_inc(cmp2, 1)
        pe.wait_ge(kcn_ready, 1)
        pe.transpose(bank[6][:, 0:NCMP], TQ[0:NCMP, 0, 0:P], ident[0:NCMP, 0:NCMP]).then_inc(kc_T, 1)
        pe.wait_ge(bias_in, 16)
        pe.wait_ge(kcT_out, 1)
        pe.wait_ge(qkT_out, 3)
        for h in range(NH):
            gs, r = slice(HD * (h // 4), HD * (h // 4 + 1)), h % 4
            for j in range(J):
                o = bank[6 + h // 4][:, (2 * h + j) % 8 * 16:(2 * h + j) % 8 * 16 + NCMP]
                a = 159 - P * j
                mm(o, flip, bias[:, h, a:a + CS * (NCMP - 1) + 1:CS], start=True, stop=False)
                m = mm(o, qT[gs, r, j * P:(j + 1) * P], kcT[gs, 0:NCMP], start=False, stop=True)
        m.then_inc(cs_full, 1)
        pe.wait_ge(pc_ready, 1)
        for u in range(2 * NH):
            m = pe.transpose(bank[u // 4][0:NCMP, (u % 4) * P:(u % 4 + 1) * P], pcm[:, u, 0:NCMP], ident)
            if u % 4 == 3:
                m.then_inc(pc_T, 1)

        def scores(h):
            gs, r = slice(HD * (h // 4), HD * (h // 4 + 1)), h % 4
            if h >= 2:
                pe.wait_ge(s_exp, 4 * (h - 1))
            for kind in range(2):
                o = kbank(h, kind)
                mm(o[:, 0:P], flip, bias[:, h, P:2 * P], start=True, stop=False)
                mm(o[:, 0:P], qT[gs, r, 0:P], kT[gs, kind, 0:P], start=False, stop=True)
                mm(o[:, P:3 * P], flip, bias[:, h, 0:T], start=True, stop=False)
                mm(o[:, P:3 * P], qT[gs, r, P:T], kT[gs, kind, :], start=False, stop=True).then_inc(s_full, 1)

        def prob_T(h):
            pe.wait_ge(p_norm, 4 * h + 4)
            if h:
                pe.wait_ge(pT_out, 2 * h)
            for kind in range(2):
                for n in range(3):
                    m = pe.transpose(bank[4 + kind][:, n * P:(n + 1) * P], PB[:, h % 2, kind, n * P:(n + 1) * P], ident)
                m.then_inc(p_T, 1)

        def values(h):
            g = h // 4
            pe.wait_ge(pT_out, 2 * h + 2)
            for j in range(J):
                o = bank[6 + j][:, h * HD:(h + 1) * HD]
                mm(o, PcT[:, 2 * h + j, :], KVC[:, 1, g, :], start=True, stop=False)
                for kind in range(2):
                    for s in range(j + 1):
                        v = Akv[:, s, 384 + g * HD:384 + (g + 1) * HD] if kind == 0 else Akw[:, s, P + g * HD:P + (g + 1) * HD]
                        n = (j + s) * P
                        m = mm(o, PT[:, h % 2, kind, n:n + P], v, start=False, stop=kind == 1 and s == j)
            m.then_inc(nsa_pv, 1)

        pe.wait_ge(pcT_out, 4)
        for k in range(NH + 2):
            if k < NH:
                scores(k)
            if 1 <= k <= NH:
                prob_T(k - 1)
            if k >= 2:
                values(k - 2)

        pe.wait_ge(s_exp, 4 * NH)
        for n in range(4):
            for r in range(4):
                m = pe.transpose(bank[n][:, r * P:(r + 1) * P], (Dq, Dk)[n // 2][:, n % 2, r * P:(r + 1) * P], ident)
            m.then_inc(d_T, 1)
        pe.wait_ge(dT_out, 4)
        for k in range(NH + 2):
            if k < NH:
                hs, o = slice(HD * (k % 2), HD * (k % 2 + 1)), bank[k % 4]
                if k >= 4:
                    pe.wait_ge(d_cap, k - 3)
                mm(o[:, 0:T], dkT[hs, k // 2, 0:P], dqT[hs, k // 2, :], start=True, stop=False, skip_group_check=True)
                mm(o[:, T:T + P], dkT[hs, k // 2, P:T], dqT[hs, k // 2, P:T], start=False, stop=False,
                   skip_group_check=True).then_inc(z_full, 1)
            if 1 <= k <= NH:
                o, s_ = bank[(k - 1) % 4], LB[:, (k - 1) % 2, :]
                pe.wait_ge(d_sp, k)
                mm(o[:, 0:T], ntri, s_[:, 0:T], start=False, stop=False, skip_group_check=True)
                mm(o[:, P:T], nones, s_[:, T:T + P], start=False, stop=False, skip_group_check=True)
                mm(o[:, T:T + P], ntri, s_[:, T:T + P], start=False, stop=True, skip_group_check=True).then_inc(d_arg, 1)
            if k >= 2:
                h = k - 2
                pe.wait_ge(d_a, h + 1)
                if h == 0:
                    pe.wait_ge(nsa_o, 2)
                a, vs = AR[:, h % 2, :], slice(h * HD, (h + 1) * HD)
                mm(bank[6][:, vs], a[:, 0:P], Dv[:, 0, vs], start=True, stop=True)
                mm(bank[7][:, vs], a[:, P:T], Dv[:, 0, vs], start=True, stop=False)
                mm(bank[7][:, vs], a[:, T:T + P], Dv[:, 1, vs], start=False, stop=True).then_inc(d_pv, 1)

        pe.wait_ge(sg_ready, 1)
        for h in range(NH):
            m = pe.transpose(bank[4 + h // 4][:, (h % 4) * P:(h % 4 + 1) * P], SG[:, h, :], ident)
            if h % 4 == 3:
                m.then_inc(w_T, 1)
        pe.wait_ge(d_cap, NH)
        pe.wait_ge(wT_out, 2)
        pe.wait_ge(cv_ready, 2)
        for h in range(NH):
            m = mm(bank[h // 4][:, (h % 4) * P:(h % 4 + 1) * P], WT[:, h, :], Cv[:, :, h * HD:(h + 1) * HD], start=True, stop=True)
            if h % 4 == 3:
                m.then_inc(sgu_full, 1)
        for n in range(8):
            pe.wait_ge(mixed_ready, n + 1)
            tr_pe(pe, TB["mix"] + n, (Aq, Bb, Cu, Dq)[n // 2][:, n % 2, :], k=n)

        def x1_tr(b):
            pe.wait_ge(xg2, b + 1)
            for j in range(J):
                tr_pe(pe, TB["out1"] + 2 * b + j, xgb[:, b % 2, j, :], k=j)

        pe.wait_ge(oc_ready, NH)
        for b in range(FB):
            for h in range(8):
                if b == 0 and h % 2 == 0:
                    pe.wait_ge(tb_done, TB["mix"] + h + 2)
                products(pe, "out1", 4 * b + h // 2, h % 2, T2aH, T2aL, 4 * (h // 2), BLK["out1"] + b, W, h == 0, h == 7)
                if b and h == 5:
                    x1_tr(b - 1)

        def ffn(f, first):
            for h in range(16):
                if first and h == 6:
                    pe.wait_ge(tb_done, TB["out1"] + 8)
                products(pe, "ffn", h // 2, h % 2, T1H, T1L, 4 * (h % 8 // 2), BLK["ffn"] + h // 8, W, h % 8 == 0, h % 8 == 7, f)
                if first and h == 1:
                    x1_tr(FB - 1)
                if not first and h == 5:
                    gated_tr(f)

        def gated_tr(f):
            B = BLK["ffn"] + 1
            v = 2 * (B // 2)
            pe.wait_ge(acc_out[B % 2], f * 2 + v if not isinstance(f, int) else v + 2 * f)
            for j in range(J):
                tr_pe(pe, f * 2 + (TB["ffn"] - 2 + j), av[:, j, :], k=j)

        ffn(0, True)
        with pe.Fori(1, NF) as f:
            ffn(f, False)

        def x2_tr(b):
            B = BLK["down"] + b
            pe.wait_ge(acc_out[B % 2], 2 * (B // 2) + 2)
            for j in range(J):
                tr_pe(pe, TB["down"] + 2 * b + j, x2b[:, j, :], k=j)

        for b in range(FB):
            for h in range(22):
                if b == 0 and h == 20:
                    pe.wait_ge(tb_done, TB["down"])
                products(pe, "down", 11 * b + h // 2, h % 2, T2bH, T2bL, 4 * (h // 2), BLK["down"] + b, W, h == 0, h == 21)
                if b == 0 and h == 5:
                    gated_tr(NF)
                if b and h == 5:
                    x2_tr(b - 1)

        def in2_at(p):
            for n, (b, e, kind, g) in enumerate(ROT):
                for j in range(J):
                    if p == e + 5 + 2 * j:
                        pe.wait_ge(rot, n + 1)
                        pe.wait_ge(rotT_out, 2 * n + j)
                        for a in range(4):
                            m = pe.transpose(bank[4][:, a * P:(a + 1) * P], ta[:, j, a * P:(a + 1) * P], ident)
                        m.then_inc(rot_T, 1)
            for g in range(AKV):
                for a in range(4):
                    u = 4 * g + a
                    if p == S_AT[g] + 3 * a:
                        if u == 0:
                            pe.wait_ge(rotT_out, 4)
                        elif a == 0:
                            pe.wait_ge(rotT_out, 4 + 2 * g)
                        if u:
                            pe.wait_ge(a_exp, 2 * u)
                        for j in range(J):
                            m = mm(bank[6][:, j * T:(j + 1) * T], qTa[:, g % 2, a, j * P:(j + 1) * P], kTa[:, g, :], start=True, stop=True)
                        m.then_inc(a_S, 1)
                    if p == S_AT[g] + 3 * a + 3:
                        pe.wait_ge(a_exp, 2 * u + 2)
                        pe.wait_ge(a_PTo, u)
                        for s in range(2):
                            for j in range(J):
                                m = pe.transpose(bank[7][:, (2 * s + j) * P:(2 * s + j + 1) * P], PA[:, u % 2, j, s * P:(s + 1) * P], ident)
                        m.then_inc(a_PT, 1)
                    if p == S_AT[g] + 3 * a + 6:
                        pe.wait_ge(a_PTo, u + 1)
                        if u == 0:
                            B = BLK["in2"] + 2
                            pe.wait_ge(acc_out[B % 2], 2 * (B // 2) + 2)
                        if u:
                            pe.wait_ge(a_O, 2 * u)
                        for j in range(J):
                            for s in range(2):
                                m = mm(bank[5][:, j * P:(j + 1) * P], PTa[:, u % 2, s, j * P:(j + 1) * P], vA[:, s, g * P:(g + 1) * P],
                                       start=s == 0, stop=s == 1)
                        m.then_inc(a_PV, 1)
                for j in range(J):
                    if p == OT_AT[g][j]:
                        pe.wait_ge(a_og, 2 * g + 2)
                        pe.wait_ge(tb_done, TB["in2"] + 2 * g + j)
                        pe.wait_ge(rotT_out, 10)
                        tr_pe(pe, TB["in2"] + 2 * g + j, oA[:, g, j, :], (4, 4), j)

        for p in range(80):
            b, h = p // 8, p % 8
            if p == 6:
                pe.wait_ge(tb_done, TB["down"] + 8)
            products(pe, "in2", p // 2, p % 2, T1H, T1L, 4 * (h // 2), BLK["in2"] + b, W, h == 0, h == 7)
            if p == 1:
                x2_tr(FB - 1)
            in2_at(p)
        for b in range(FB):
            for h in range(8):
                if b == 0 and h in (0, 4, 6):
                    pe.wait_ge(tb_done, TB["in2"] + max(h, 2) + 2)
                products(pe, "out2", 4 * b + h // 2, h % 2, T2cH, T2cL, 4 * (h // 2), BLK["out2"] + b, W, h == 0, h == 7)
                in2_at(80 + 8 * b + h)

        def ret(i, first):
            def tr(e, k):
                n = i * 2 + (e + 2 * k)
                pe.wait_ge(r_og, n * 2 + 2)
                for j in range(J):
                    m = i * 4 + (4 * k + 2 * e + j)
                    tr_pe(pe, m + TB["ret"], oR[:, j, :], (4, 6), j)

            for h in range(48):
                e, p = h // 24, h % 24
                hd = i * 2 + e
                if first:
                    for n in range(0 if h == 0 else h + 2, min(h + 3, 8)):
                        pe.wait_ge(x3_ready, n + 1)
                        tr_pe(pe, TB["out2"] + n, X3[:, n % 2, (n // 2) * W:(n // 2 + 1) * W], (4, 5, 6, 7), n)
                    if h < 8 and h % 2 == 0:
                        pe.wait_ge(tb_done, TB["out2"] + h + 2)
                products(pe, "ret", h // 2, h % 2, T1H, T1L, 4 * (h % 8 // 2), BLK["ret"] + h // 8, W, h % 8 == 0, h % 8 == 7, i)
                if p == 15:
                    pe.wait_ge(r_rot, hd + 1)
                    for j in range(J):
                        for a in range(4):
                            m = pe.transpose(bank[4 + j][:, a * P:(a + 1) * P], xr[:, j, a * P:(a + 1) * P], ident)
                        m.then_inc(r_T, 1)
                if p == 18:
                    pe.wait_ge(r_Tout, hd * 4 + 4)
                    for s in range(2):
                        for dc in range(2):
                            m = mm(bank[6][:, s * T:(s + 1) * T], rT[:, 1, dc, s * P:(s + 1) * P], rT[:, 0, dc, :], start=dc == 0, stop=dc == 1)
                    m.then_inc(r_S, 1)
                if p == 21:
                    pe.wait_ge(r_SM, hd + 1)
                    B = BLK["ret"] + 3 * e + 1
                    v = 2 * (B // 2) + 2
                    pe.wait_ge(acc_out[B % 2], v if first else i * 6 + v)
                    for j in range(J):
                        for s in range(2):
                            m = mm(bank[(7, 5)[j]], SM[:, s, j * P:(j + 1) * P], vR[:, s, :], start=s == 0, stop=s == 1)
                    m.then_inc(r_out, 1)
                if h == 29:
                    tr(0, 0)
                if h == 5 and not first:
                    tr(1, -1)

        ret(0, True)
        with pe.Fori(1, RH // 2) as i:
            ret(i, False)
        for b in range(FB):
            for h in range(16):
                if b == 0 and h == 0:
                    pe.wait_ge(tb_done, TB["ret"] + 2 * RH - 2)
                if b == 0 and h == 14:
                    pe.wait_ge(tb_done, TB["ret"] + 2 * RH)
                products(pe, "out3", 8 * b + h // 2, h % 2, T2dH, T2dL, 4 * (h // 2), BLK["out3"] + b, W, h == 0, h == 15)
                if b == 0 and h == 5:
                    pe.wait_ge(r_og, 2 * RH)
                    for j in range(J):
                        tr_pe(pe, TB["ret"] + 2 * RH - 2 + j, oR[:, j, :], (4, 6), j)

    ctx.close()


def constants():
    f = np.float32
    p = np.arange(P)
    c = {}
    cst = np.zeros((P, 5, P), f)
    cst[:, 0] = np.eye(P)
    cst[:, 1] = np.eye(P)[::-1]
    cst[:, 2] = -(p[:, None] >= p[None, :]).astype(f)
    cst[:, 3] = -1
    cst[:, 4] = p[None, :] <= p[:, None]
    c["cst"] = cst
    before = (p[:, None] < p[None, :]).astype(f)
    c["msk3"] = np.concatenate([before, np.ones((P, P), f), before], 1)
    c["cap3"] = np.concatenate([(before - 1) * f(-NEG), np.zeros((P, P), f), (before - 1) * f(-NEG)], 1).astype(f)
    d = np.arange(T)
    n = np.maximum(d, 1).astype(f)
    large = 16 + (np.log(n / f(16)).astype(f) / f(math.log(64)) * f(16)).astype(np.int32)
    bucket = np.where(d < 16, d, np.minimum(large, 31))
    oh = np.zeros((33, W), f)
    oh[bucket[::-1], np.arange(T)] = 1
    oh[32, T:] = NEG
    c["onehot"] = oh
    for name, hd, n in (("rope", AD, 4), ("rope2", RD, 2)):
        row, col = np.repeat(np.arange(4, dtype=f), 64), np.tile(np.arange(64, dtype=f), 4)
        half = hd // 2
        inv = (f(10000.0) ** (-np.arange(0, half, 2, dtype=f) / f(half))).astype(f)
        a, b = row[:, None] * inv, col[:, None] * inv
        ang = np.concatenate([a, a, b, b], -1)
        sign = np.repeat(np.array([-1, 1, -1, 1], f), hd // 4)
        for k, t in (("c", np.cos(ang)), ("s", np.sin(ang) * sign)):
            t = t.astype(f).reshape(J, P, 1, hd).transpose(1, 0, 2, 3)
            t = np.broadcast_to(t, (P, J, n, hd))
            c[f"{name}_{k}"] = np.ascontiguousarray(t if n == 4 else t.reshape(P, J, n * hd))
    dist = d[None, None, :] - (np.arange(2)[None, :, None] * P + p[:, None, None])
    c["dist"] = np.concatenate([np.maximum(dist, 0), np.maximum(-dist, 0)], 1).astype(f)
    return c


_INS = ["x", "w_in", "w_out", "norm_mix", "norm_ffn", "q_gain", "k_gain", "cmp_pos", "cmp_w1", "cmp_w2", "rel_table",
        "conv_w", "sgu_w", "sgu_b", "group_gain", "w_ffn_gate", "w_ffn_up", "w_ffn_down", "attn_w_in_2", "attn_q_gain_2",
        "attn_k_gain_2", "attn_w_out_2", "ret_w_in_2", "ret_decay_exp_2", "ret_w_out_2", "ln_gain_2", "ln_bias_2"]


def kernel(**inputs):
    import concourse.bacc as _bacc
    from concourse.bass_utils import run_bass_kernel_spmd as _run

    nc = _bacc.Bacc("TRN2", target_bir_lowering=False, num_devices=1)
    arrays, args = {}, {}
    given = {name: np.ascontiguousarray(inputs[name]) for name in _INS}
    for name, a in {**given, **constants()}.items():
        arrays[f"in_{name}"] = a
        args[name] = nc.dram_tensor(f"in_{name}", a.shape, mybir.dt.from_np(a.dtype), kind="ExternalInput").ap()
    out = nc.dram_tensor("out_0", (1, T, D), F32, kind="ExternalOutput").ap()
    two_blocks(nc, args, out)
    r = _run(nc, [arrays], core_ids=[0])
    return r.results[0]["out_0"]
```

```python
import math
from contextlib import ExitStack

import numpy as np

import concourse.bass as bass
from concourse import mybir

F32 = mybir.dt.float32
F32R = mybir.dt.float32r
ALU = mybir.AluOpType
ACT = mybir.ActivationFunctionType
AX = mybir.AxisListType.X

P = 128
T = 256
J = T // P
D = 2048
KT = D // P
W = 512
FB = D // W
CK = 4
RAWS = 4
HALF = 2
SPLITS = 4

HD = 64
NH = 8
NG = 2
GW = D // 4
NCMP = 15
CL, CS = 32, 16
DFF = 5632
NF = DFF // W
NEG = -1.0e30
Q0, KV0, KV1, B0, C0, D0 = 0, 512, 1024, 1304, 2840, 3864
KV1W = 280

AH, AKV, AD = 16, 4, 128
RH, RD, RV = 8, 256, 512
ALPHA = 4.0 ** 0.25
RMS_EPS, LN_EPS = 1e-6, 1e-5

PHASES = [("in1", 44, 1), ("out1", 16, 1), ("ffn", 8, 11), ("down", 44, 1), ("in2", 40, 1),
          ("out2", 16, 1), ("ret", 24, 4), ("out3", 32, 1)]


def stream_plan():
    plan, chunks, landed = {}, 0, [0] * RAWS
    for name, per, bodies in PHASES:
        incs = [32 if name == "ret" and c % 12 < 4 else 16 for c in range(per)]
        body = [sum(incs[s::RAWS]) for s in range(RAWS)]
        plan[name] = (chunks, per, list(landed), body, incs)
        chunks += per * bodies
        landed = [a + b * bodies for a, b in zip(landed, body)]
    return plan


PLAN = stream_plan()


def two_blocks(nc, A, out):
    ctx = ExitStack()

    base = 16512
    limit = 229368

    def at(name, off, shape, dt=F32):
        n = 4
        for s in shape[1:]:
            n *= s
        assert base + off + n <= limit, (name, off, n)
        return nc.alloc_sbuf_tensor_at(name, shape, dt, offset=base + off)

    KB = 1024
    raw = at("raw", 0, [P, RAWS, CK, W])
    whi = at("whi", 32 * KB, [P, SPLITS, HALF, W], F32R)
    wlo = at("wlo", 48 * KB, [P, SPLITS, HALF, W], F32R)
    T1H = at("T1H", 64 * KB, [P, KT, T], F32R)
    T1L = at("T1L", 80 * KB, [P, KT, T], F32R)
    S0 = 96 * KB
    cst = at("cst", S0, [P, 5, P])
    ident, flip, ntri, nones, tril = (cst[:, n, :] for n in range(5))
    small = at("small", S0 + 2560, [P, 640])
    R0 = S0 + 2560 + 2560
    T2aH = at("T2aH", R0, [P, KT, T], F32R)
    T2aL = at("T2aL", R0 + 16 * KB, [P, KT, T], F32R)
    X = at("X", R0, [P, J, D])
    XG = at("XG", R0 + 16 * KB, [P, J, D])
    PJ = R0 + 32 * KB
    Aq = at("Aq", PJ, [P, J, W])
    Akv = at("Akv", PJ + 4 * KB, [P, J, W])
    Dq = at("Dq", PJ + 8 * KB, [P, J, W])
    Dk = at("Dk", PJ + 12 * KB, [P, J, W])
    Dv = at("Dv", PJ + 16 * KB, [P, J, W])
    Cu = at("Cu", PJ + 20 * KB, [P, J, W])
    Cv = at("Cv", PJ + 24 * KB, [P, J, W])
    Bb = at("Bb", PJ + 28 * KB, [P, J, W])
    Bc = at("Bc", PJ + 32 * KB, [P, J, W])
    Bh = at("Bh", PJ + 36 * KB, [P, J, W])
    Akw = at("Akw", PJ + 40 * KB, [P, J, KV1W])
    MS = PJ + 40 * KB + J * KV1W * 4 + 64
    gB = at("gB", MS, [P, D])
    bias = at("bias", MS + 8 * KB, [P, NH, 384])
    w1s = at("w1s", MS + 20 * KB, [P, 2, CS, HD])
    w2s = at("w2s", MS + 28 * KB, [HD, 2, HD])
    PT = at("PT", PJ + 20 * KB, [P, 2, 2, 384])
    kT = at("kT", PJ + 26 * KB, [P, 2, T])
    PB = at("PB", MS + 20 * KB, [P, 2, 2, 384])
    dqT = at("dqT", MS + 20 * KB, [P, 4, T])
    dkT = at("dkT", MS + 24 * KB, [P, 4, T])
    qT = at("qT", MS + 28 * KB + 512, [P, 4, T])
    TQ = at("TQ", R0, [P, J, W])
    TK = at("TK", R0 + 4 * KB, [P, 2, J, P])
    cap3 = at("cap3", R0 + 4 * KB, [P, 384])
    msk3 = at("msk3", R0 + 6 * KB, [P, 384])
    zz = at("zz", R0 + 8 * KB, [P, 2, NG, T])
    AR = at("AR", R0 + 8 * KB, [P, 2, 384])
    LB = at("LB", R0 + 11 * KB, [P, 2, 384])
    SG = at("SG", R0 + 14 * KB, [P, NH, P])
    WT = at("WT", R0 + 18 * KB, [P, NH, P])
    PcT = at("PcT", R0 + 22 * KB, [NCMP, 2 * NH, P])
    zd = at("zd", R0 + 22 * KB, [P, J, 4, 2, HD])
    z1 = at("z1", PJ + 4 * KB, [P, J, W])
    z2 = at("z2", MS + 28 * KB + 512, [P, J, W])
    cwB = at("cwB", MS + 8 * KB, [P, 3, W])
    yb = at("yb", MS + 14 * KB, [P, J, W])
    junk = at("junk", PJ + 12 * KB, [P, W])
    x1b = at("x1b", PJ, [P, 2, J, W])
    xrb = at("xrb", PJ + 8 * KB, [P, 2, J, W])
    xgb = at("xgb", PJ + 16 * KB, [P, 2, J, W])
    junk2 = at("junk2", PJ + 24 * KB, [P, W])
    gF = at("gF", PJ + 32 * KB, [P, D])
    T2bH = at("T2bH", R0, [P, DFF // P, T], F32R)
    T2bL = at("T2bL", R0 + 44 * KB, [P, DFF // P, T], F32R)
    FT = R0 + 88 * KB
    sg = at("sg", FT, [P, J, W])
    av = at("av", FT + 4 * KB, [P, J, W])
    x2b = at("x2b", FT + 8 * KB, [P, J, W])
    xr2 = at("xr2", FT + 12 * KB, [P, J, W])
    T2cH = at("T2cH", R0, [P, KT, T], F32R)
    T2cL = at("T2cL", R0 + 16 * KB, [P, KT, T], F32R)
    E0 = R0 + 32 * KB
    kTa = at("kTa", E0, [P, AKV, T])
    vA = at("vA", E0 + 4 * KB, [P, J, W])
    tabs = [at(f"tab{n}", E0 + (8 + 4 * n) * KB, [P, J, 4, P]) for n in range(4)]
    xq = at("xq", E0 + 24 * KB, [P, J, W])
    ta = at("ta", E0 + 28 * KB, [P, J, W])
    tb = at("tb", E0 + 32 * KB, [P, J, W])
    qTa = at("qTa", E0 + 36 * KB, [P, 2, 4, T])
    gA = at("gA", E0 + 44 * KB, [P, J, W])
    PA = at("PA", E0 + 48 * KB, [P, 2, J, T])
    PTa = at("PTa", E0 + 52 * KB, [P, 2, J, T])
    oA = at("oA", E0 + 56 * KB, [P, AKV, J, W])
    gn = at("gn", E0 + 72 * KB, [P, 4, P])
    X3 = at("X3", R0 + 32 * KB, [P, J, D])
    xr3 = at("xr3", R0 + 48 * KB, [P, 2, J, W])
    lnG = at("lnG", R0 + 56 * KB, [P, D])
    lnB = at("lnB", R0 + 64 * KB, [P, D])
    T2dH = at("T2dH", R0, [P, RH * 4, T], F32R)
    T2dL = at("T2dL", R0 + 32 * KB, [P, RH * 4, T], F32R)
    G0 = R0 + 64 * KB
    MM = at("MM", G0, [P, RH, 2, T])
    rc = at("rc", G0 + 16 * KB, [P, J, W])
    rs_ = at("rs_", G0 + 20 * KB, [P, J, W])
    xr = at("xr", G0 + 24 * KB, [P, J, W])
    rb = at("rb", G0 + 28 * KB, [P, J, W])
    rT = at("rT", G0 + 32 * KB, [P, 2, 2, T])
    vR = at("vR", G0 + 36 * KB, [P, J, W])
    SM = at("SM", G0 + 24 * KB, [P, 2, T])
    oR = at("oR", G0 + 24 * KB, [P, J, W])
    gR = at("gR", G0 + 28 * KB, [P, J, W])
    X4 = at("X4", G0, [P, J, D])
    xr4 = at("xr4", G0 + 16 * KB, [P, 2, J, W])
    lnG2 = at("lnG2", G0 + 24 * KB, [P, D])
    lnB2 = at("lnB2", G0 + 32 * KB, [P, D])
    dpos = at("dpos", R0, [P, 2, T])
    dneg = at("dneg", R0 + 2 * KB, [P, 2, T])
    mt = at("mt", R0 + 4 * KB, [P, 2, 2 * T])
    lg = at("lg", R0 + 8 * KB, [P, 8, 2 * RH])

    used = [0]

    def cols(n):
        used[0] += n
        assert used[0] <= 640
        return small[:, used[0] - n:used[0]]

    ssx, rstd1 = cols(8), cols(2)
    posT = cols(64)
    sgubT = cols(8)
    qg8, kg = cols(64), cols(64)
    nss, nrs, ntmp = cols(24), cols(24), cols(24)
    gsig, gtmp = cols(48), cols(48)
    psd = [nc.alloc_psum_tensor(f"bank{n}", [P, W], F32) for n in range(8)]
    bank = [b[:, :] for b in psd]
    ACC = [[bank[0], bank[1]], [bank[2], bank[3]]]
    prow = at("prow", PJ + 28 * KB, [HD, P])
    sbrow = at("sbrow", PJ + 29 * KB, [NH, P])
    tabaug = at("tabaug", PJ + 30 * KB, [33, NH])
    onehot = at("onehot", PJ + 31 * KB, [33, W])
    vrow = at("vrow", PJ + 34 * KB, [NH, W])
    nmx, nsum, nrw = cols(8), cols(8), cols(8)
    cmx, csum, crw = cols(16), cols(16), cols(16)
    hT = cols(2 * NG * NCMP)
    gss, grs = cols(8), cols(8)
    ss1, rstd2 = cols(8), cols(2)
    bst, bag, brs = cols(8 * 6), cols(4), cols(2)
    nsx, nrx = cols(8), cols(8)
    pcm = at("pcm", R0 + 30 * KB, [P, 2 * NH, 16])
    KVC = at("KVC", R0 + 31 * KB, [NCMP, 2, NG, HD])
    kcT = cols(16)

    scr_bias = nc.dram_tensor("scr_bias", [NH * W], F32).ap()
    scr_x1 = nc.dram_tensor("scr_x1", [T, D], F32).ap()
    scr_x2 = nc.dram_tensor("scr_x2", [T, D], F32).ap()
    scr_x3 = nc.dram_tensor("scr_x3", [T, D], F32).ap()

    def sem(name):
        return ctx.enter_context(nc.semaphore(name))

    landed = [sem(f"landed{n}") for n in range(RAWS)]
    hi_ready, lo_ready, mm_done = sem("hi_ready"), sem("lo_ready"), sem("mm_done")
    acc_out = [sem("acc_out0"), sem("acc_out1")]
    tb_full, tb_hi, tb_done = sem("tb_full"), sem("tb_hi"), sem("tb_done")
    act_c, dve_c, pool_c = sem("act_chain"), sem("dve_chain"), sem("pool_chain")
    ret_c, reta_c = sem("ret_chain"), sem("reta_chain")
    x_in = [sem(f"x_in{n}") for n in range(FB)]
    cst_in, rest_in, par_in, oh_in, w1_in = (sem(x) for x in ("cst_in", "rest_in", "par_in", "oh_in", "w1_in"))
    g_in = [sem(f"g_in{n}") for n in range(FB)]
    xg_ready, ssx_done, ms1, rs1 = sem("xg_ready"), sem("ssx_done"), sem("ms1"), sem("rs1")
    par_T, par_out, vrow_ps, vrow_sb = sem("par_T"), sem("par_out"), sem("vrow_ps"), sem("vrow_sb")
    vscr, bias_in = sem("vscr"), sem("bias_in")
    zd_ready, msk_in = sem("zd_ready"), sem("msk_in")
    nsa_ms, nsa_rs, nsa_qk, z_T, zz_ready = (sem(x) for x in ("nsa_ms", "nsa_rs", "nsa_qk", "z_T", "zz_ready"))
    qk_T, qkT_out, cmp1, hT_ready, cmp2 = (sem(x) for x in ("qk_T", "qkT_out", "cmp1", "hT_ready", "cmp2"))
    kc_ms, kc_rs, kcn_ready, kc_T, kcT_out = (sem(x) for x in ("kc_ms", "kc_rs", "kcn_ready", "kc_T", "kcT_out"))
    cs_full, cs_sub, cs_exp, pc_ready, pc_T, pcT_out = (
        sem(x) for x in ("cs_full", "cs_sub", "cs_exp", "pc_ready", "pc_T", "pcT_out"))
    gexp, s_full, s_max, s_exp, p_norm, p_T, pT_out, nsa_pv, nsa_o = (
        sem(x) for x in ("gexp", "s_full", "s_max", "s_exp", "p_norm", "p_T", "pT_out", "nsa_pv", "nsa_o"))
    d_T, dT_out, z_full, d_log, d_sp, d_arg, d_cap, d_a, d_pv, d_o = (
        sem(x) for x in ("d_T", "dT_out", "z_full", "d_log", "d_sp", "d_arg", "d_cap", "d_a", "d_pv", "d_o"))
    sg_in, sg_ready, w_T, wT_out, cv_ms, cv_rs, cv_ready, sgu_full, oc_ready = (
        sem(x) for x in ("sg_in", "sg_ready", "w_T", "wT_out", "cv_ms", "cv_rs", "cv_ready", "sgu_full", "oc_ready"))
    cw_in, shift_in, z_conv, ob_ready, gg_in, g_sq, g_ms, g_rs, mixed_ready = (
        sem(x) for x in ("cw_in", "shift_in", "z_conv", "ob_ready", "gg_in", "g_sq", "g_ms", "g_rs", "mixed_ready"))
    gF_in, xg2, x1_sq, ms2, rs2 = (sem(x) for x in ("gF_in", "xg2", "x1_sq", "ms2", "rs2"))
    xr1_in, x1_st, xr3_in, xr4_in = ([sem(f"{x}{n}") for n in range(2)] for x in ("xr1_in", "x1_st", "xr3_in", "xr4_in"))
    xr2_in, x2_st = sem("xr2_in"), sem("x2_st")
    tab_in, tab_ready, q_ms, q_rs, rot, rot_T, rotT_out, q_sq, q_norm, q_swap = (
        sem(x) for x in ("tab_in", "tab_ready", "q_ms", "q_rs", "rot", "rot_T", "rotT_out", "q_sq", "q_norm", "q_swap"))
    a_S, a_max, a_exp, a_PT, a_PTo, a_PV, a_O, a_og = (
        sem(x) for x in ("a_S", "a_max", "a_exp", "a_PT", "a_PTo", "a_PV", "a_O", "a_og"))
    ln_in, ln_ms, ln_rs, x3_ready, x3_st = (
        sem(x) for x in ("ln_in", "ln_ms", "ln_rs", "x3_ready", "x3_st"))
    rr_in = sem("rr_in")
    dist_in, lg1, mt_ready, mm_ready = (sem(x) for x in ("dist_in", "lg1", "mt_ready", "mm_ready"))
    r_rot, r_T, r_Tout, r_S, r_SM, r_out, r_ms, r_rs, r_norm, r_og = (
        sem(x) for x in ("r_rot", "r_T", "r_Tout", "r_S", "r_SM", "r_out", "r_ms", "r_rs", "r_norm", "r_og"))
    ln2_in, x4_ready, out_st = sem("ln2_in"), sem("x4_ready"), sem("out_st")

    class Chain:

        def __init__(self, eng, s):
            self.eng, self.s, self.n, self.base = eng, s, 0, 0

        def link(self, ins):
            ins.then_inc(self.s, 1)
            self.n += 1
            self.eng.wait_ge(self.s, self.base + self.n)

    def half_no(ph, c, hf, i):
        before, per = PLAN[ph][:2]
        q = 2 * (before + c) + hf
        return (q if isinstance(i, int) and i == 0 else i * (2 * per) + q), (2 * c + hf) % SPLITS

    def load(eng, ph, c, srcs, i=0):
        before, per, _, _, _ = PLAN[ph]
        if isinstance(i, int):
            g = before + i * per + c
            if g >= RAWS:
                eng.wait_ge(lo_ready, 2 * (g - RAWS) + 2)
        else:
            eng.wait_ge(lo_ready, i * (2 * per) + 2 * (before + c - RAWS) + 2)
        for lo, hi_, src in srcs:
            eng.dma_start(raw[:, c % RAWS, :, lo:hi_], src).then_inc(landed[c % RAWS], 16)

    def land(eng, ph, c, i):
        _, _, start, body, incs = PLAN[ph]
        v = start[c % RAWS] + sum(incs[c % RAWS:c + 1:RAWS])
        eng.wait_ge(landed[c % RAWS], v if isinstance(i, int) and i == 0 else i * body[c % RAWS] + v)

    def split_hi(eng, ph, c, hf, n=W, i=0):
        q, s = half_no(ph, c, hf, i)
        if hf == 0:
            land(eng, ph, c, i)
        if not isinstance(q, int) or q >= SPLITS:
            eng.wait_ge(mm_done, q - (SPLITS - 1))
        eng.activation(whi[:, s, :, :n], raw[:, c % RAWS, HALF * hf:HALF * (hf + 1), :n],
                       ACT.Copy).then_inc(hi_ready, 1)

    def split_lo(eng, ph, c, hf, n=W, i=0):
        q, s = half_no(ph, c, hf, i)
        eng.wait_ge(hi_ready, q + 1)
        eng.tensor_tensor(wlo[:, s, :, :n], raw[:, c % RAWS, HALF * hf:HALF * (hf + 1), :n],
                          whi[:, s, :, :n].bitcast(F32), ALU.subtract).then_inc(lo_ready, 1)

    def products(eng, ph, c, hf, TH, TL, kt0, blk, n=W, first=False, last=False, i=0):
        q, s = half_no(ph, c, hf, i)
        buf = blk % 2
        if first:
            uses = 2 * (blk // 2)
            if not isinstance(i, int) or i:
                nb = {"ffn": 2, "ret": 6}[ph]
                eng.wait_ge(acc_out[buf], i * nb + uses)
            elif uses:
                eng.wait_ge(acc_out[buf], uses)
        eng.wait_ge(lo_ready, q + 1)
        for t in range(HALF):
            kt = kt0 + HALF * hf + t
            for j in range(J):
                xs, o = slice(j * P, (j + 1) * P), ACC[buf][j][:, :n]
                eng.matmul(o, TH[:, kt, xs], whi[:, s, t, :n], start=first and t == 0, stop=False)
                eng.matmul(o, TH[:, kt, xs], wlo[:, s, t, :n], start=False, stop=False)
                m = eng.matmul(o, TL[:, kt, xs], whi[:, s, t, :n], start=False, stop=last and t == HALF - 1)
        m.then_inc(mm_done, 1)

    def block_done(eng, ph, c, i=0):
        q, _ = half_no(ph, c, 1, i)
        eng.wait_ge(mm_done, q + 1)

    def tr_pe(eng, n, src, banks=(4, 5), k=0):
        if not isinstance(n, int) or n >= len(banks):
            eng.wait_ge(tb_done, n + 1 - len(banks))
        for a in range(4):
            m = eng.transpose(bank[banks[k % len(banks)]][:, a * P:(a + 1) * P], src[:, a * P:(a + 1) * P], ident)
        m.then_inc(tb_full, 1)

    def tr_act(eng, n, dst, banks=(4, 5), k=0):
        eng.wait_ge(tb_full, n + 1)
        eng.activation(dst, bank[banks[k % len(banks)]].rearrange("p (a t) -> p a t", a=4), ACT.Copy).then_inc(tb_hi, 1)

    def tr_dve(eng, n, hi_, lo, banks=(4, 5), k=0):
        eng.wait_ge(tb_hi, n + 1)
        eng.tensor_tensor(lo, bank[banks[k % len(banks)]].rearrange("p (a t) -> p a t", a=4), hi_.bitcast(F32),
                          ALU.subtract).then_inc(tb_done, 1)

    def part(t, fb, j):
        return t[:, 4 * fb:4 * fb + 4, j * P:(j + 1) * P]

    def rep(ap, at_, n):
        dims = [list(d) for d in ap.ap]
        return bass.AP(ap.tensor, ap.offset, dims[:1 + at_] + [[0, n]] + dims[1 + at_:])

    def heads(ap, d):
        return ap.rearrange("p j (h d) -> p (j h) d", d=d)

    def swapped(eng, out, x, table, d):
        o, v, t = (a.rearrange("p j (n s d) -> p (j n) s d", s=2, d=d) for a in (out, x, table))
        return [eng.tensor_tensor(o[:, :, s, :], v[:, :, 1 - s, :], t[:, :, s, :], ALU.mult) for s in range(2)]

    def flat(t):
        return t.rearrange("p j h d -> p j (h d)")

    def rows(ap):
        return ap.rearrange("(j p) c -> p j c", p=P)

    def spread(ap, n, start=0):
        return bass.AP(ap.tensor, ap.offset + start, [[0, P], [1, n]])

    BLOCKS1 = [(Q0, W, Aq), (KV0, W, Akv), (KV1, KV1W, Akw), (D0, W, Dq), (D0 + W, W, Dk), (D0 + 2 * W, W, Dv),
               (B0, W, Bb), (B0 + W, W, Bc), (B0 + 2 * W, W, Bh), (C0 + W, W, Cv), (C0, W, Cu)]
    NB1 = len(BLOCKS1)
    BLK = {"in1": 0, "out1": 11, "ffn": 15, "down": 37, "in2": 41, "out2": 51, "ret": 55, "out3": 79}
    TB = {"in1": 0, "mix": 8, "out1": 16, "ffn": 24, "down": 46, "in2": 54, "out2": 62, "ret": 70}
    BLOCKS2 = [("q", 0), ("k", 0), ("v", 0), ("q", 1), ("q", 2), ("q", 3), ("g", 0), ("g", 1), ("g", 2), ("g", 3)]
    COL2 = {"q": 0, "k": D, "v": D + W, "g": D + 2 * W}
    ROT = [(0, 11, "q", 0), (1, 19, "k", 0), (3, 35, "q", 1), (4, 43, "q", 2), (5, 51, "q", 3)]
    S_AT = [28, 43, 55, 67]
    OT_AT = [(61, 64), (69, 72), (77, 79), (84, 85)]
    SW = [(0, P), (P, 3 * P)]

    U0 = 41
    Z0 = U0 + 22
    NU = 2 * NH
    MIX = [(0, Aq), (1, Bb), (3, Dq), (2, Cu)]

    def ubank(u):
        return bank[4 + u % 2]

    def zbank(k):
        return bank[4 + k % 3]

    def head_cols(h, j):
        return slice((2 * (h % 4) + j) * HD, (2 * (h % 4) + j + 1) * HD)

    block = ctx.enter_context(nc.Block())

    @block.sync
    def _(sp):
        def chunk(w, kc, col, n=W):
            return w[kc * W:(kc + 1) * W, col:col + n].rearrange("(a p) n -> p a n", p=P)

        def dyn(w, kc, col, n=W):
            return w[kc * W:(kc + 1) * W, bass.ds(col, n)].rearrange("(a p) n -> p a n", p=P)

        for b, (col, n, _) in enumerate(BLOCKS1):
            for cc in range(4):
                if b == 0:
                    cs = slice(cc * W, (cc + 1) * W)
                    sp.dma_start(X[:, :, cs], rows(A["x"][0])[:, :, cs]).then_inc(x_in[cc], 16)
                load(sp, "in1", 4 * b + cc, [(0, n, chunk(A["w_in"][0], cc, col, n))])
        for c in range(16):
            load(sp, "out1", c, [(0, W, chunk(A["w_out"][0], MIX[c % 4][0], c // 4 * W))])
        with sp.Fori(0, NF) as f:
            for c in range(8):
                w = A["w_ffn_gate"] if c < 4 else A["w_ffn_up"]
                load(sp, "ffn", c, [(0, W, dyn(w[0], c % 4, f * W))], f)
        for c in range(44):
            load(sp, "down", c, [(0, W, chunk(A["w_ffn_down"][0], c % 11, c // 11 * W))])
        for b, (kind, g) in enumerate(BLOCKS2):
            for cc in range(4):
                load(sp, "in2", 4 * b + cc, [(0, W, chunk(A["attn_w_in_2"][0], cc, COL2[kind] + g * W))])
        for c in range(16):
            load(sp, "out2", c, [(0, W, chunk(A["attn_w_out_2"][0], c % 4, c // 4 * W))])
        with sp.Fori(0, RH // 2) as i:
            for c in range(24):
                e, w, kc = c // 12, A["ret_w_in_2"][0], c % 4
                if c % 12 < 4:
                    load(sp, "ret", c, [(0, RD, dyn(w, kc, i * (2 * RD) + e * RD, RD)),
                                        (RD, 2 * RD, dyn(w, kc, i * (2 * RD) + (D + e * RD), RD))], i)
                else:
                    off = 2 * D + (0 if c % 12 < 8 else RH * RV) + e * RV
                    load(sp, "ret", c, [(0, W, dyn(w, kc, i * (2 * RV) + off))], i)
        for c in range(32):
            load(sp, "out3", c, [(0, W, chunk(A["ret_w_out_2"][0], c % 8, c // 8 * W))])
        n = 0
        for fb in range(FB):
            for j in range(J):
                n += 1
                sp.wait_ge(x4_ready, n)
                cs = slice(fb * W, (fb + 1) * W)
                sp.dma_start(rows(out[0])[:, j, cs], X4[:, j, cs]).then_inc(out_st, 16)
        sp.wait_ge(out_st, 16 * n)

    @block.gpsimd
    def _(pool):
        ch = Chain(pool, pool_c)

        for half in range(2):
            pool.dma_start(prow[:, half * HD:(half + 1) * HD], A["cmp_pos"][0].rearrange("i l d -> (i l) d")).then_inc(par_in, 16)
        pool.dma_start(sbrow[:, :], A["sgu_b"][0]).then_inc(par_in, 16)
        pool.dma_start(onehot[:, :], A["onehot"]).then_inc(oh_in, 16)
        ch.link(pool.memset(tabaug[:, :], 1.0))
        pool.dma_start(tabaug[0:32, :], A["rel_table"]).then_inc(oh_in, 16)
        pool.dma_start(qg8, spread(A["q_gain"], HD)).then_inc(par_in, 16)
        pool.dma_start(kg, spread(A["k_gain"], HD)).then_inc(par_in, 16)
        for n in range(FB):
            pool.wait_ge(x_in[n], 16)
        for half in range(2):
            for i in range(2):
                src = A["cmp_w1"][0, i].rearrange("(l d) e -> d l e", d=HD)
                pool.dma_start(w1s[half * HD:(half + 1) * HD, i, :, :], src[:, half * CS:(half + 1) * CS, :]).then_inc(w1_in, 16)
        pool.dma_start(w2s[:, :, :], A["cmp_w2"][0].rearrange("i d e -> d i e")).then_inc(w1_in, 16)
        pool.wait_ge(vrow_sb, 1)
        pool.dma_start(scr_bias.rearrange("(h c) -> h c", h=NH), vrow[:, :]).then_inc(vscr, 16)
        pool.wait_ge(vscr, 16)
        pool.dma_start(bias[:, :, :], bass.AP(scr_bias.tensor, 0, [[1, P], [W, NH], [1, 384]])).then_inc(bias_in, 16)
        pool.wait_ge(xg_ready, FB)
        pool.dma_start(gB[:, :], spread(A["group_gain"], D)).then_inc(gg_in, 16)
        pool.wait_ge(ssx_done, 1)
        pool.wait_ge(tb_full, 8)
        pool.dma_start(SG[:, :, :], A["sgu_w"][0].rearrange("h p q -> p h q")).then_inc(sg_in, 16)
        pool.dma_start(msk3[:, :], A["msk3"]).then_inc(msk_in, 16)
        pool.wait_ge(qk_T, 3)
        pool.dma_start(cap3[:, :], A["cap3"]).then_inc(msk_in, 16)
        pool.wait_ge(acc_out[0], 10)
        pool.wait_ge(acc_out[1], 8)
        pool.tensor_tensor(Bh[:, :, :], Bc[:, :, :], Bh[:, :, :], ALU.mult).then_inc(z_conv, 1)
        pool.wait_ge(nsa_pv, NH)
        pool.dma_start(cwB[:, :, :], bass.AP(A["conv_w"].tensor, 0, [[0, P], [W, 3], [1, W]])).then_inc(cw_in, 16)
        pool.memset(z1[0:1, 0, :], 0.0).then_inc(z_conv, 1)
        pool.memset(z2[0:2, 0, :], 0.0).then_inc(z_conv, 1)
        pool.wait_ge(z_conv, 3)
        pool.dma_start(z1[1:P, :, :], Bh[0:P - 1, :, :]).then_inc(shift_in, 16)
        pool.dma_start(z1[0:1, 1, :], Bh[P - 1:P, 0, :]).then_inc(shift_in, 16)
        pool.dma_start(z2[2:P, :, :], Bh[0:P - 2, :, :]).then_inc(shift_in, 16)
        pool.dma_start(z2[0:2, 1, :], Bh[P - 2:P, 0, :]).then_inc(shift_in, 16)
        pool.wait_ge(cw_in, 16)
        pool.wait_ge(shift_in, 64)
        ch.link(pool.tensor_tensor(yb[:, :, :], z2[:, :, :], rep(cwB[:, 0, :], 0, J), ALU.mult))
        ch.link(pool.tensor_tensor(z1[:, :, :], z1[:, :, :], rep(cwB[:, 1, :], 0, J), ALU.mult))
        ch.link(pool.tensor_tensor(yb[:, :, :], yb[:, :, :], z1[:, :, :], ALU.add))
        ch.link(pool.tensor_tensor(Bh[:, :, :], Bh[:, :, :], rep(cwB[:, 2, :], 0, J), ALU.mult))
        ch.link(pool.tensor_tensor(yb[:, :, :], yb[:, :, :], Bh[:, :, :], ALU.add))
        pool.tensor_tensor(Bb[:, :, :], Bb[:, :, :], yb[:, :, :], ALU.mult).then_inc(ob_ready, 1)
        pool.wait_ge(tb_done, TB["out1"])
        pool.dma_start(gF[:, :], spread(A["norm_ffn"], D)).then_inc(gF_in, 16)
        for b in range(FB):
            cs = slice(b * W, (b + 1) * W)
            if b < 2:
                pool.dma_start(xrb[:, b % 2, :, :], rows(A["x"][0])[:, :, cs]).then_inc(xr1_in[b % 2], 16)
        for b in range(FB):
            cs = slice(b * W, (b + 1) * W)
            done = 2 * ((BLK["out1"] + b) // 2) + 2
            pool.wait_ge(acc_out[(BLK["out1"] + b) % 2], done)
            pool.dma_start(rows(scr_x1)[:, :, cs], x1b[:, b % 2, :, :]).then_inc(x1_st[b % 2], 16)
            if b + 2 < FB:
                cs = slice((b + 2) * W, (b + 3) * W)
                pool.dma_start(xrb[:, b % 2, :, :], rows(A["x"][0])[:, :, cs]).then_inc(xr1_in[b % 2], 16)
        for n in range(2):
            pool.wait_ge(x1_st[n], 32)
        for b in range(FB):
            cs = slice(b * W, (b + 1) * W)
            if b == 0:
                pool.wait_ge(mm_done, 2 * PLAN["ffn"][0])
            done = 2 * ((BLK["down"] + b) // 2) + 2
            pool.dma_start(xr2[:, :, :], rows(scr_x1)[:, :, cs]).then_inc(xr2_in, 16)
            pool.wait_ge(acc_out[(BLK["down"] + b) % 2], done)
            pool.dma_start(rows(scr_x2)[:, :, cs], x2b[:, :, :]).then_inc(x2_st, 16)
        for n, g in enumerate((A["attn_q_gain_2"], A["attn_k_gain_2"])):
            pool.dma_start(gn[:, n, :], spread(g, P)).then_inc(tab_in, 16)
            for q in range(4):
                pool.dma_start(gn[:, 2 + n, 32 * q:32 * q + 32],
                               bass.AP(g.tensor, 32 * (q ^ 1), [[0, P], [1, 32]])).then_inc(tab_in, 16)
        pool.wait_ge(mm_done, 2 * PLAN["in2"][0])
        for n in range(2):
            pool.dma_start(tabs[2 * n][:, :, :, :], A["rope_c"]).then_inc(tab_in, 16)
            pool.dma_start(tabs[2 * n + 1][:, :, :, :], A["rope_s"]).then_inc(tab_in, 16)
        pool.wait_ge(tab_in, 16 * 14)
        for n in range(4):
            g = (0, 2, 1, 3)[n]
            t = tabs[n][:, :, :, :].rearrange("p j h d -> p (j h) d")
            pool.tensor_tensor(t, t, rep(gn[:, g, :], 0, 8), ALU.mult).then_inc(tab_ready, 1)
        pool.wait_ge(tab_ready, 4)
        for n, (b, e, kind, g) in enumerate(ROT):
            pool.wait_ge(q_norm, n + 1)
            if n:
                pool.wait_ge(rot, n)
            for ins in swapped(pool, tb[:, :, :], xq[:, :, :], flat(tabs[3 if kind == "k" else 1][:, :, :, :]), 32):
                ch.link(ins)
            pool.sem_inc(q_swap, 1)
        pool.wait_ge(x2_st, 16 * FB)
        pool.wait_ge(tb_done, TB["out2"])
        pool.dma_start(lnG[:, :], spread(A["ln_gain_2"][0], D)).then_inc(ln_in, 16)
        pool.dma_start(lnB[:, :], spread(A["ln_bias_2"][0], D)).then_inc(ln_in, 16)
        for b in range(FB):
            if b >= 2:
                pool.wait_ge(acc_out[(BLK["out2"] + b) % 2], 2 * ((BLK["out2"] + b) // 2))
            pool.dma_start(xr3[:, b % 2, :, :], rows(scr_x2)[:, :, b * W:(b + 1) * W]).then_inc(xr3_in[b % 2], 16)
        pool.wait_ge(mm_done, 2 * PLAN["ret"][0])
        pool.dma_start(dpos[:, :, :], A["dist"][:, 0:2, :]).then_inc(dist_in, 16)
        pool.dma_start(dneg[:, :, :], A["dist"][:, 2:4, :]).then_inc(dist_in, 16)
        pool.dma_start(lg[:, 0, :], spread(A["ret_decay_exp_2"], 2 * RH)).then_inc(dist_in, 16)
        pool.wait_ge(x3_ready, FB * J)
        pool.dma_start(rc[:, :, :], A["rope2_c"]).then_inc(rr_in, 16)
        pool.dma_start(rs_[:, :, :], A["rope2_s"]).then_inc(rr_in, 16)
        pool.dma_start(rows(scr_x3), X3[:, :, :]).then_inc(x3_st, 16)
        pool.wait_ge(x3_st, 16)
        pool.wait_ge(tb_done, TB["ret"] + 2 * RH)
        pool.dma_start(lnG2[:, :], spread(A["ln_gain_2"][1], D)).then_inc(ln2_in, 16)
        pool.dma_start(lnB2[:, :], spread(A["ln_bias_2"][1], D)).then_inc(ln2_in, 16)
        for b in range(FB):
            if b >= 2:
                pool.wait_ge(acc_out[(BLK["out3"] + b) % 2], 2 * ((BLK["out3"] + b) // 2))
            pool.dma_start(xr4[:, b % 2, :, :], rows(scr_x3)[:, :, b * W:(b + 1) * W]).then_inc(xr4_in[b % 2], 16)

    @block.scalar
    def _(act):
        ch = Chain(act, act_c)

        def rstd(ms, ms_sem, n, done):
            act.wait_ge(ms_sem, n)
            ch.link(act.activation(ms, ms, ACT.Ln))
            act.activation(ms, ms, ACT.Exp, scale=-0.5).then_inc(done, 1)

        for fb in range(FB):
            cs = slice(fb * W, (fb + 1) * W)
            act.dma_start(gB[:, cs], spread(A["norm_mix"], W, fb * W)).then_inc(g_in[fb], 16)
            if fb == 0:
                act.dma_start(cst[:, 0:1, :], A["cst"][:, 0:1, :]).then_inc(cst_in, 16)
        act.dma_start(cst[:, 1:5, :], A["cst"][:, 1:5, :]).then_inc(rest_in, 16)

        def out1_block(b):
            _, n, dst = BLOCKS1[b]
            block_done(act, "in1", 4 * b + 3)
            if b == 0:
                act.wait_ge(rs1, 1)
            if dst is Bb:
                act.wait_ge(vscr, 16)
            for j in range(J):
                f = ACT.Gelu_apprx_tanh if dst in (Cu, Cv) else ACT.Copy
                act.activation(dst[:, j, :n], ACC[b % 2][j][:, :n], f, scale=rstd1[:, j:j + 1]).then_inc(acc_out[b % 2], 1)

        def head_evac(dst, n, done):
            act.activation(dst[:, :, n * 4 * HD:(n + 1) * 4 * HD].rearrange("p j (h d) -> p h j d", d=HD),
                           bank[7].rearrange("p (h j d) -> p h j d", h=4, j=J), ACT.Copy).then_inc(done, 1)

        def squares(n):
            g, src = MIX[n]
            for j in range(J):
                ch.link(act.activation(junk[:, :], src[:, j, :], ACT.Square, accum_out=gss[:, 2 * g + j:2 * g + j + 1]))
            act.sem_inc(g_sq, 1)

        def mix_rstd(n):
            g = MIX[n][0]
            rstd(grs[:, 2 * g:2 * g + 2], g_ms, n + 1, g_rs)

        def mix_at(p):
            if p == 23:
                for n in range(2):
                    act.wait_ge(w_T, n + 1)
                    act.activation(WT[:, 4 * n:4 * n + 4, :], bank[4 + n].rearrange("p (h t) -> p h t", h=4), ACT.Copy).then_inc(wT_out, 1)
            if p == 27:
                act.wait_ge(acc_out[0], 4)
                act.wait_ge(acc_out[1], 2)
                for n in range(2):
                    act.activation(zd[:, :, :, n, :], Akv[:, :, 0:4 * HD].rearrange("p j (u d) -> p j u d", d=HD), ACT.Copy).then_inc(zd_ready, 1)
            if p == 28:
                rstd(ntmp, nsa_ms, 1, nsa_rs)
                act.activation(gtmp, Akw[:, :, 256:KV1W], ACT.Exp, scale=-1.0).then_inc(gexp, 1)
            if p == 31:
                for j in range(J):
                    act.wait_ge(qk_T, j + 1)
                    act.activation(qT[:, :, j * P:(j + 1) * P], bank[6 + j].rearrange("p (r t) -> p r t", r=4), ACT.Copy).then_inc(qkT_out, 1)
            if p == 33:
                act.wait_ge(qk_T, 3)
                act.activation(kT[:, :, :], bank[4].rearrange("p (k t) -> p k t", k=2), ACT.Copy).then_inc(qkT_out, 1)
                act.wait_ge(cmp1, 1)
                act.activation(hT[0:HD, :].rearrange("p (i n) -> p i n", i=2), bank[5][0:HD, 0:64].rearrange("p (i n) -> p i n", i=2)[:, :, 0:2 * NCMP],
                               ACT.Gelu_apprx_tanh).then_inc(hT_ready, 1)
            if p == 35:
                rstd(cmx[0:NCMP, 0:2], kc_ms, 1, kc_rs)
            if p == 38:
                act.wait_ge(kc_T, 1)
                act.activation(kcT[:, 0:NCMP], bank[7][:, 0:NCMP], ACT.Copy).then_inc(kcT_out, 1)
            if p == 40:
                act.wait_ge(cs_sub, 2)
                act.activation(pcm[:, :, 0:NCMP], pcm[:, :, 0:NCMP], ACT.Exp).then_inc(cs_exp, 1)
            for n in range(4):
                if p == 42 + n // 2:
                    act.wait_ge(pc_T, n + 1)
                    act.activation(PcT[:, 4 * n:4 * n + 4, :], bank[6 + n % 2][0:NCMP, :].rearrange("p (u t) -> p u t", u=4), ACT.Copy).then_inc(pcT_out, 1)
            for n in range(2):
                if p == U0 + 8 * n + 14:
                    act.wait_ge(nsa_pv, 4 * n + 4)
                    head_evac(Aq, n, nsa_o)
            u = p - U0 - 2
            if 0 <= u < NU:
                act.wait_ge(s_max, u + 1)
                if u >= 4:
                    act.wait_ge(p_T, u - 3)
                for j, (a, z) in enumerate(SW):
                    c = 2 * (u % 4) + j
                    act.activation(PB[:, u // 2 % 2, u % 2, a:z], ubank(u)[:, a:z], ACT.Exp,
                                   bias=nmx[:, c:c + 1], accum_out=nsum[:, c:c + 1]).then_inc(s_exp, 1)
            u = p - U0 - 5
            if 0 <= u < NU:
                act.wait_ge(p_T, u + 1)
                if u >= 4:
                    act.wait_ge(nsa_pv, u // 2 - 1)
                act.activation(PT[:, u // 2 % 2, u % 2, :], bank[6][:, 0:384], ACT.Copy).then_inc(pT_out, 1)
            for n in range(4):
                if p == U0 + 19 + 2 * (n // 2):
                    act.wait_ge(d_T, n + 1)
                    dst = (dqT, dkT)[n // 2][:, :, (n % 2) * P:(n % 2 + 1) * P]
                    act.activation(dst, bank[4 + n % 2].rearrange("p (r t) -> p r t", r=4), ACT.Copy,
                                   scale=HD ** -0.5 if n < 2 else 1.0).then_inc(dT_out, 1)
            for n in range(2):
                if p == Z0 + 9 * n + 15:
                    act.wait_ge(d_pv, 4 * n + 4)
                    head_evac(Dq, n, d_o)
            for k in range(NH):
                if p == Z0 + 2 * k + 7:
                    act.wait_ge(d_cap, k + 1)
                    act.activation(AR[:, k % 2, :], AR[:, k % 2, :], ACT.Exp).then_inc(d_a, 1)
                if p == Z0 + 2 * k + 2:
                    act.wait_ge(z_full, k + 1)
                    if k >= 2:
                        act.wait_ge(d_arg, k - 1)
                    lb = LB[:, k % 2, :]
                    ch.link(act.activation(lb, zbank(k)[:, 0:384], ACT.Abs))
                    ch.link(act.activation(lb, lb, ACT.Exp, scale=-1.0))
                    act.activation(lb, lb, ACT.Ln, bias=1.0).then_inc(d_log, 1)
            if p == U0 + 23:
                act.wait_ge(nsa_o, 2)
                squares(0)
            if p == U0 + 25:
                mix_rstd(0)
            if p == 85:
                rstd(brs, cv_ms, 1, cv_rs)
            if p == 84:
                act.wait_ge(ob_ready, 1)
                squares(1)
            if p == 86:
                mix_rstd(1)
            if p == 87:
                act.wait_ge(d_o, 2)
                squares(2)

        for b in range(NB1):
            for h in range(8):
                split_hi(act, "in1", 4 * b + h // 2, h % 2, BLOCKS1[b][1])
                if b == 0:
                    for n in ((0, 1) if h == 0 else (h + 1,) if h < 7 else ()):
                        tr_act(act, n, part(T1H, n // 2, n % 2), (4, 5, 6, 7), n)
                if b == 0 and h == 7:
                    for fb in range(FB):
                        for j in range(J):
                            ch.link(act.activation(Aq[:, 0, :], X[:, j, fb * W:(fb + 1) * W], ACT.Square,
                                                   accum_out=ssx[:, 4 * j + fb:4 * j + fb + 1]))
                    act.sem_inc(ssx_done, 1)
                if b == 1 and h == 1:
                    rstd(rstd1, ms1, 1, rs1)
                if h == 3 and b:
                    out1_block(b - 1)
                mix_at(8 * b + h)

        def x1_squares(b):
            act.wait_ge(acc_out[(BLK["out1"] + b) % 2], 2 * ((BLK["out1"] + b) // 2) + 2)
            for j in range(J):
                ch.link(act.activation(junk2[:, :], x1b[:, b % 2, j, :], ACT.Square, accum_out=ss1[:, 4 * j + b:4 * j + b + 1]))
            act.sem_inc(x1_sq, 1)

        for b in range(FB):
            for h in range(8):
                split_hi(act, "out1", 4 * b + h // 2, h % 2)
                if b == 0:
                    if h == 1:
                        mix_rstd(2)
                    if h == 2:
                        out1_block(NB1 - 1)
                    if 1 <= h < 7:
                        for n in ((0, 1), (2, 3), (4,), (5,), (6,), (7,))[h - 1]:
                            tr_act(act, TB["mix"] + n, part(T2aH, MIX[n // 2][0], n % 2), (6, 7), n)
                    if h == 3:
                        act.wait_ge(oc_ready, NH)
                        squares(3)
                    if h == 4:
                        mix_rstd(3)
                if b and h == 4:
                    x1_squares(b - 1)
                if b and h == 7:
                    for j in range(J):
                        tr_act(act, TB["out1"] + 2 * (b - 1) + j, part(T1H, b - 1, j), k=j)

        def ffn(f, first):
            for h in range(16):
                split_hi(act, "ffn", h // 2, h % 2, i=f)
                if first and h == 1:
                    x1_squares(FB - 1)
                if first and h == 3:
                    for j in range(J):
                        tr_act(act, TB["out1"] + 6 + j, part(T1H, 3, j), k=j)
                if first and h == 4:
                    rstd(rstd2, ms2, 1, rs2)
                if not first and h == 7:
                    for j in range(J):
                        n = f * 2 + (TB["ffn"] - 2 + j)
                        tr_act(act, n, T2bH[:, bass.ds(f * 4 - 4, 4), j * P:(j + 1) * P], k=j)
                if first and h == 11:
                    act.wait_ge(x1_st[0], 32)
                    act.wait_ge(x1_st[1], 32)
                if h == 11:
                    block_done(act, "ffn", 3, f)
                    if not first:
                        act.wait_ge(acc_out[(BLK["ffn"] + 1) % 2], f * 2 + 2 * ((BLK["ffn"] + 1) // 2))
                    for j in range(J):
                        act.activation(sg[:, j, :], ACC[BLK["ffn"] % 2][j], ACT.Silu, scale=rstd2[:, j:j + 1]).then_inc(acc_out[BLK["ffn"] % 2], 1)

        ffn(0, True)
        with act.Fori(1, NF) as f:
            ffn(f, False)

        for b in range(FB):
            for h in range(22):
                split_hi(act, "down", 11 * b + h // 2, h % 2)
                if b == 0 and h == 7:
                    for j in range(J):
                        tr_act(act, TB["ffn"] + 20 + j, part(T2bH, 10, j), k=j)
                if b and h == 7:
                    for j in range(J):
                        tr_act(act, TB["down"] + 2 * (b - 1) + j, part(T1H, b - 1, j), k=j)

        def exps(g, a):
            u = 4 * g + a
            act.wait_ge(a_max, u + 1)
            if u >= 2:
                act.wait_ge(a_PT, u - 1)
            for j in range(J):
                c = 2 * (u % 2) + j
                act.activation(PA[:, u % 2, j, :], bank[6][:, j * T:(j + 1) * T], ACT.Exp, bias=nmx[:, c:c + 1],
                               accum_out=nsum[:, c:c + 1]).then_inc(a_exp, 1)

        def pt_out(u):
            act.wait_ge(a_PT, u + 1)
            if u >= 2:
                act.wait_ge(a_PV, u - 1)
            act.activation(PTa[:, u % 2, :, :], bank[7].rearrange("p (s t) -> p s t", s=2), ACT.Copy).then_inc(a_PTo, 1)

        def in2_at(p):
            if p == 3:
                for j in range(J):
                    tr_act(act, TB["down"] + 6 + j, part(T1H, 3, j), k=j)
            for b, (kind, g) in enumerate(BLOCKS2):
                if p == 8 * b + 11:
                    B = BLK["in2"] + b
                    block_done(act, "in2", 4 * b + 3)
                    dst = {"q": xq, "k": xq, "v": vA, "g": gA}[kind]
                    n_rot = [r[0] for r in ROT]
                    if kind in "qk" and n_rot.index(b):
                        act.wait_ge(rot, n_rot.index(b))
                    if kind == "g" and g:
                        act.wait_ge(a_og, 2 * g)
                    for j in range(J):
                        act.activation(dst[:, j, :], ACC[B % 2][j], ACT.Silu if kind == "g" else ACT.Copy).then_inc(acc_out[B % 2], 1)
            for n, (b, e, kind, g) in enumerate(ROT):
                if p == e:
                    act.wait_ge(acc_out[(BLK["in2"] + b) % 2], 2 * ((BLK["in2"] + b) // 2) + 2)
                    if n:
                        act.wait_ge(rot, n)
                    act.activation(tb[:, :, :], xq[:, :, :], ACT.Square).then_inc(q_sq, 1)
                if p == e + 1:
                    rstd(nrx, q_ms, n + 1, q_rs)
                for j in range(J):
                    if p == e + 7 + 2 * j:
                        act.wait_ge(rot_T, 2 * n + j + 1)
                        dst = kTa[:, :, j * P:(j + 1) * P] if kind == "k" else qTa[:, g % 2, :, j * P:(j + 1) * P]
                        act.activation(dst, bank[4].rearrange("p (a t) -> p a t", a=4), ACT.Copy,
                                       scale=1.0 if kind == "k" else AD ** -0.5).then_inc(rotT_out, 1)
            for g in range(AKV):
                for a in range(4):
                    if p == S_AT[g] + 3 * a + 2:
                        exps(g, a)
                    if p == S_AT[g] + 3 * a + 5:
                        pt_out(4 * g + a)
                for j in range(J):
                    if p == OT_AT[g][j] + 3:
                        tr_act(act, TB["in2"] + 2 * g + j, part(T2cH, g, j), (4, 4), j)

        for p in range(80):
            split_hi(act, "in2", p // 2, p % 2)
            in2_at(p)
        for b in range(FB):
            for h in range(8):
                split_hi(act, "out2", 4 * b + h // 2, h % 2)
                in2_at(80 + 8 * b + h)
        for h in range(3):
            split_hi(act, "ret", h // 2, h % 2)
        rstd(brs, ln_ms, 1, ln_rs)

        def ret(i, rc_, first):
            def rstd_(ms, ms_sem, n, done):
                act.wait_ge(ms_sem, n)
                rc_.link(act.activation(ms, ms, ACT.Ln))
                act.activation(ms, ms, ACT.Exp, scale=-0.5).then_inc(done, 1)

            def gate(e, k):
                n = i * 2 + (e + 2 * k)
                block_done(act, "ret", 12 * e + 11, i + k if k else i)
                B = BLK["ret"] + 3 * e + 2
                for j in range(J):
                    act.activation(gR[:, j, :], ACC[B % 2][j], ACT.Silu).then_inc(acc_out[B % 2], 1)

            def tr(e, k):
                for j in range(J):
                    n = i * 4 + (4 * k + 2 * e + j)
                    tr_act(act, n + TB["ret"], T2dH[:, bass.ds(i * 8 + (8 * k + 4 * e), 4), j * P:(j + 1) * P] if not isinstance(i, int)
                           else part(T2dH, 2 * (i + k) + e, j), (4, 6), j)

            for h in range(48):
                e, p = h // 24, h % 24
                if not first or h >= 3:
                    split_hi(act, "ret", h // 2, h % 2, i=i)
                if first and 2 <= h < 8:
                    for n in ((0, 1), (2, 3), (4,), (5,), (6,), (7,))[h - 2]:
                        tr_act(act, TB["out2"] + n, part(T1H, n // 2, n % 2), (4, 5, 6, 7), n)
                if first and h == 6:
                    act.wait_ge(dist_in, 48)
                    rc_.link(act.activation(lg[:, 1, :], lg[:, 0, :], ACT.Exp, scale=-math.log(2.0)))
                    rc_.link(act.activation(lg[:, 2, :], lg[:, 1, :], ACT.Copy, scale=-1.0, bias=1.0))
                    act.activation(lg[:, 5, :], lg[:, 2, :], ACT.Ln).then_inc(lg1, 1)
                if first and 9 <= h < 9 + RH:
                    m = h - 9
                    act.wait_ge(mt_ready, m + 1)
                    act.activation(MM[:, m, :, :], mt[:, m % 2, :].rearrange("p (s t) -> p s t", s=2), ACT.Exp).then_inc(mm_ready, 1)
                if p == 11:
                    block_done(act, "ret", 12 * e + 3, i)
                    B = BLK["ret"] + 3 * e
                    if not first or e:
                        act.wait_ge(tb_done, i * 4 + (TB["ret"] + 2 * e))
                    for j in range(J):
                        act.activation(xr[:, j, :], ACC[B % 2][j], ACT.Copy).then_inc(acc_out[B % 2], 1)
                if p == 17:
                    for j in range(J):
                        act.wait_ge(r_T, i * 4 + (2 * e + j + 1))
                        v = bank[4 + j].rearrange("p (k d t) -> p k d t", k=2, d=2)
                        act.activation(rT[:, 0, :, j * P:(j + 1) * P], v[:, 0, :, :], ACT.Copy).then_inc(r_Tout, 1)
                        act.activation(rT[:, 1, :, j * P:(j + 1) * P], v[:, 1, :, :], ACT.Copy, scale=RD ** -0.5).then_inc(r_Tout, 1)
                if p == 19:
                    block_done(act, "ret", 12 * e + 7, i)
                    B = BLK["ret"] + 3 * e + 1
                    if not first or e:
                        act.wait_ge(r_out, i * 2 + e)
                    for j in range(J):
                        act.activation(vR[:, j, :], ACC[B % 2][j], ACT.Copy).then_inc(acc_out[B % 2], 1)
                if h == 24 or (h == 0 and not first):
                    rstd_(brs, r_ms, i * 2 + e, r_rs)
                if h == 27:
                    gate(0, 0)
                if h == 31:
                    tr(0, 0)
                if h == 3 and not first:
                    gate(1, -1)
                if h == 7 and not first:
                    tr(1, -1)

        RETA = (3, 2)
        rc_ = Chain(act, reta_c)
        ret(0, rc_, True)
        assert rc_.n == RETA[0], rc_.n
        with act.Fori(1, RH // 2) as i:
            rc_.base, rc_.n = i * RETA[1] + (RETA[0] - RETA[1]), 0
            ret(i, rc_, False)
            assert rc_.n == RETA[1], rc_.n
        last = RH // 2
        for b in range(FB):
            for h in range(16):
                split_hi(act, "out3", 8 * b + h // 2, h % 2)
                if b == 0 and h == 0:
                    rstd(brs, r_ms, RH, r_rs)
                if b == 0 and h == 3:
                    block_done(act, "ret", 23, last - 1)
                    B = BLK["ret"] + 5
                    for j in range(J):
                        act.activation(gR[:, j, :], ACC[B % 2][j], ACT.Silu).then_inc(acc_out[B % 2], 1)
                if b == 0 and h == 7:
                    for j in range(J):
                        tr_act(act, TB["ret"] + 2 * RH - 2 + j, part(T2dH, RH - 1, j), (4, 6), j)
        rstd(brs, ln_ms, 2, ln_rs)

    @block.vector
    def _(dve):
        ch = Chain(dve, dve_c)
        tt, ts, stt = dve.tensor_tensor, dve.tensor_scalar, dve.scalar_tensor_tensor
        MUL, ADD, SUB, MAX, MIN = ALU.mult, ALU.add, ALU.subtract, ALU.max, ALU.min

        def gain(fb):
            dve.wait_ge(x_in[fb], 16)
            dve.wait_ge(g_in[fb], 16)
            cs = slice(fb * W, (fb + 1) * W)
            tt(XG[:, :, cs], X[:, :, cs], rep(gB[:, cs], 0, J), MUL).then_inc(xg_ready, 1)

        def tr1(n):
            tr_dve(dve, n, part(T1H, n // 2, n % 2), part(T1L, n // 2, n % 2), (4, 5, 6, 7), n)

        ks, kw = Akv[:, :, 256:384], Akw[:, :, 0:128]
        gv = gsig.rearrange("p (j h k) -> p j h k", j=J, h=NH)
        kcv = KVC[:, 0, :, :]
        sq = TQ[0:NCMP, 0, 0:P].rearrange("p (g d) -> p g d", g=NG)

        def mix_ms(n):
            g = MIX[n][0]
            dve.wait_ge(g_sq, n + 1)
            ts(grs[:, 2 * g:2 * g + 2], gss[:, 2 * g:2 * g + 2], 1.0 / GW, RMS_EPS, MUL, ADD).then_inc(g_ms, 1)

        def mix_norm(n):
            g, src = MIX[n]
            dve.wait_ge(g_rs, n + 1)
            if n == 0:
                dve.wait_ge(gg_in, 16)
            for j in range(J):
                stt(src[:, j, :], src[:, j, :], grs[:, 2 * g + j:2 * g + j + 1], gB[:, g * W:(g + 1) * W], MUL, MUL).then_inc(mixed_ready, 1)

        def mix_at(p):
            if p == 18:
                dve.wait_ge(sg_in, 16)
                dve.wait_ge(rest_in, 16)
                tt(SG[:, :, :], SG[:, :, :], rep(tril, 0, NH), MUL).then_inc(sg_ready, 1)
            if p == 27:
                dve.wait_ge(acc_out[0], 4)
                dve.wait_ge(acc_out[1], 2)
                dve.wait_ge(tb_full, 8)
                dve.wait_ge(ssx_done, 1)
                ch.link(tt(TQ[:, :, :], Aq[:, :, :], Aq[:, :, :], MUL))
                ch.link(tt(TK[:, 0, :, :], ks, ks, MUL))
                ch.link(tt(TK[:, 1, :, :], kw, kw, MUL))
                ch.link(dve.tensor_reduce(nss[:, 0:16], heads(TQ[:, :, :], HD), AX, ADD))
                ch.link(dve.tensor_reduce(nss[:, 16:24], TK[:, :, :, :].rearrange("p k j (h d) -> p (k j h) d", d=HD), AX, ADD))
                ts(ntmp, nss, 1.0 / HD, RMS_EPS, MUL, ADD).then_inc(nsa_ms, 1)
            if p == 28:
                dve.wait_ge(nsa_rs, 1)
                ch.link(tt(heads(Aq[:, :, :], HD), heads(Aq[:, :, :], HD), rep(ntmp[:, 0:16], 1, HD), MUL))
                for j in range(J):
                    tt(TQ[:, j, :].rearrange("p (r g d) -> p g r d", r=4, g=NG), Aq[:, j, :].rearrange("p (g r d) -> p g r d", r=4, g=NG),
                       rep(rep(qg8, 0, 4), 0, NG), MUL).then_inc(nsa_qk, 1)
            if p == 29:
                for i in range(2):
                    zb = bank[4 + i]
                    dve.wait_ge(z_T, i + 1)
                    tt(zz[0:HD, i, :, :].rearrange("p g (n l) -> p (g n) l", l=CS), zb[0:HD, :].rearrange("p (n l) -> p n l", l=CS),
                       rep(posT[0:HD, i * CL:i * CL + CS], 0, NG * T // CS), ADD).then_inc(zz_ready, 1)
                    for g in range(NG):
                        tt(zz[HD:P, i, g, 0:T - CS].rearrange("p (n l) -> p n l", l=CS),
                           zb[HD:P, g * T + CS:(g + 1) * T].rearrange("p (n l) -> p n l", l=CS),
                           rep(posT[HD:P, i * CL + CS:(i + 1) * CL], 0, NCMP), ADD).then_inc(zz_ready, 1)
            if p == 30:
                for n, src in enumerate((ks, kw)):
                    tt(TK[:, n, :, :].rearrange("p j (h d) -> p j h d", d=HD), src.rearrange("p j (h d) -> p j h d", d=HD),
                       rep(ntmp[:, 16 + 4 * n:20 + 4 * n].rearrange("p (j h) -> p j h", j=J), 2, HD), MUL).then_inc(dve_c, 1)
                ch.n += 2
                dve.wait_ge(dve_c, ch.n)
                kf = TK[:, :, :, :].rearrange("p k j (h d) -> p (k j h) d", d=HD)
                tt(kf, kf, rep(kg, 0, 8), MUL).then_inc(nsa_qk, 1)
                dve.wait_ge(gexp, 1)
                ch.link(ts(gsig, gtmp, 1.0, None, ADD))
                ch.link(dve.reciprocal(gsig, gsig))
            if p == 35:
                dve.wait_ge(cmp2, 1)
                ch.link(dve.tensor_copy(KVC[:, :, :, :], bank[6][0:NCMP, 0:4 * HD].rearrange("p (i g d) -> p i g d", i=2, g=NG)))
                dve.wait_ge(qk_T, 3)
                ch.link(tt(sq, kcv, kcv, MUL))
                ch.link(dve.tensor_reduce(cmx[0:NCMP, 0:2], sq, AX, ADD))
                ts(cmx[0:NCMP, 0:2], cmx[0:NCMP, 0:2], 1.0 / HD, RMS_EPS, MUL, ADD).then_inc(kc_ms, 1)
            if p == 36:
                dve.wait_ge(kc_rs, 1)
                ch.link(tt(sq, kcv, rep(cmx[0:NCMP, 0:2], 1, HD), MUL))
                tt(sq, sq, rep(kg[0:NCMP, :], 0, NG), MUL).then_inc(kcn_ready, 1)
            if p == 40:
                dve.wait_ge(cs_full, 1)
                cs = [bank[6 + g][:, 0:128].rearrange("p (u n) -> p u n", n=16)[:, :, 0:NCMP] for g in range(NG)]
                for g in range(NG):
                    ch.link(dve.tensor_reduce(cmx[:, 8 * g:8 * g + 8], cs[g], AX, MAX))
                ch.link(ts(cmx, cmx, 0.1 * NEG, None, MAX))
                for g in range(NG):
                    tt(pcm[:, 8 * g:8 * g + 8, 0:NCMP], cs[g], rep(cmx[:, 8 * g:8 * g + 8], 1, NCMP), SUB).then_inc(cs_sub, 1)
            if p == 41:
                dve.wait_ge(cs_exp, 1)
                ch.link(dve.tensor_reduce(csum, pcm[:, :, 0:NCMP], AX, ADD))
                ch.link(ts(csum, csum, 1e-30, None, MAX))
                ch.link(dve.reciprocal(csum, csum))
                ch.link(tt(crw.rearrange("p (h j) -> p h j", j=J), csum.rearrange("p (h j) -> p h j", j=J),
                           gv[:, :, :, 0].rearrange("p j h -> p h j"), MUL))
                tt(pcm[:, :, 0:NCMP], pcm[:, :, 0:NCMP], rep(crw, 1, NCMP), MUL).then_inc(pc_ready, 1)
            u = p - U0 - 2
            if 0 <= u < NU:
                dve.wait_ge(s_full, u + 1)
                c = 2 * (u % 4)
                for j, (a, z) in enumerate(SW):
                    m = dve.tensor_reduce(nmx[:, c + j:c + j + 1], ubank(u)[:, a:z], AX, MAX, negate=True)
                    m.then_inc(s_max, 1) if j else ch.link(m)
            u = p - U0 - 3
            if 0 <= u < NU:
                c = 2 * (u % 4)
                dve.wait_ge(s_exp, 2 * u + 2)
                ch.link(dve.reciprocal(nsum[:, c:c + 2], nsum[:, c:c + 2]))
                ch.link(tt(nrw[:, c:c + 2], nsum[:, c:c + 2], gv[:, :, u // 2, 1 + u % 2], MUL))
                for j, (a, z) in enumerate(SW):
                    pb = PB[:, u // 2 % 2, u % 2, a:z]
                    ts(pb, pb, nrw[:, c + j:c + j + 1], None, MUL).then_inc(p_norm, 1)
            if p == Z0:
                dve.wait_ge(msk_in, 32)
            for k in range(NH):
                if p == Z0 + 2 * k + 6:
                    dve.wait_ge(d_arg, k + 1)
                    if k >= 2:
                        dve.wait_ge(d_pv, k - 1)
                    tt(AR[:, k % 2, :], zbank(k)[:, 0:384], cap3[:, :], MIN).then_inc(d_cap, 1)
                if p == Z0 + 2 * k + 3:
                    dve.wait_ge(d_log, k + 1)
                    lb = LB[:, k % 2, :]
                    ch.link(stt(lb, zbank(k)[:, 0:384], 0.0, lb, MAX, ADD))
                    tt(lb, lb, msk3[:, :], MUL).then_inc(d_sp, 1)
            if p == U0 + 24:
                mix_ms(0)
            if p == U0 + 26:
                mix_norm(0)
            if p == 85:
                mix_ms(1)
            if p == 87:
                mix_norm(1)
            if p == 84:
                dve.wait_ge(acc_out[1], 10)
                for j in range(J):
                    ch.link(dve.bn_stats(bst[:, 6 * j:6 * j + 6], Cv[:, j, :]))
                    ch.link(dve.bn_aggr(bag[:, 2 * j:2 * j + 2], bst[:, 6 * j:6 * j + 6]))
                ts(brs, bag.rearrange("p (j k) -> p j k", j=J)[:, :, 1], LN_EPS, None, ADD).then_inc(cv_ms, 1)
            if p == 85:
                dve.wait_ge(cv_rs, 1)
                for j in range(J):
                    ts(Cv[:, j, :], Cv[:, j, :], bag[:, 2 * j:2 * j + 1], brs[:, j:j + 1], SUB, MUL).then_inc(cv_ready, 1)

        def sgu_out():
            dve.wait_ge(acc_out[0], 12)
            dve.wait_ge(par_out, 2)
            for h in range(NH):
                if h % 4 == 0:
                    dve.wait_ge(sgu_full, h // 4 + 1)
                u = Cu[:, :, h * HD:(h + 1) * HD]
                stt(u, bank[4 + h // 4][:, (h % 4) * P:(h % 4 + 1) * P].rearrange("p (j d) -> p j d", j=J), sgubT[:, h:h + 1], u,
                    ADD, MUL).then_inc(oc_ready, 1)

        gain(0)
        for b in range(NB1):
            for h in range(8):
                split_lo(dve, "in1", 4 * b + h // 2, h % 2, BLOCKS1[b][1])
                if b == 0:
                    if h < 6 and h % 2 == 0:
                        gain(h // 2 + 1)
                    for n in ((0, 1) if h == 0 else (h + 1,) if h < 7 else ()):
                        tr1(n)
                if b == 1 and h == 0:
                    dve.wait_ge(ssx_done, 1)
                    ch.link(dve.tensor_reduce(rstd1, ssx.rearrange("p (j f) -> p j f", j=J), AX, ADD))
                    ts(rstd1, rstd1, 1.0 / D, RMS_EPS, MUL, ADD).then_inc(ms1, 1)
                if b == 1 and h == 3:
                    dve.wait_ge(vrow_ps, 1)
                    dve.tensor_copy(vrow[:, :], bank[6][0:NH, :]).then_inc(vrow_sb, 1)
                    dve.wait_ge(par_T, 1)
                    dve.tensor_copy(posT, bank[7][:, 0:HD]).then_inc(par_out, 1)
                    dve.tensor_copy(sgubT, bank[7][:, HD:HD + NH]).then_inc(par_out, 1)
                    ch.link(ts(qg8, qg8, HD ** -0.5, None, MUL))
                mix_at(8 * b + h)

        def x1_block(b):
            B = BLK["out1"] + b
            block_done(dve, "out1", 4 * b + 3)
            dve.wait_ge(xr1_in[b % 2], 16 * (b // 2 + 1))
            if b >= 2:
                dve.wait_ge(x1_st[b % 2], 16 * (b // 2))
                dve.wait_ge(x1_sq, b - 1)
            for j in range(J):
                tt(x1b[:, b % 2, j, :], ACC[B % 2][j], xrb[:, b % 2, j, :], ADD).then_inc(acc_out[B % 2], 1)
            dve.wait_ge(acc_out[B % 2], 2 * (B // 2) + 2)
            dve.wait_ge(gF_in, 16)
            if b >= 2:
                dve.wait_ge(tb_full, TB["out1"] + 2 * (b - 1))
            tt(xgb[:, b % 2, :, :], x1b[:, b % 2, :, :], rep(gF[:, b * W:(b + 1) * W], 0, J), MUL).then_inc(xg2, 1)

        for b in range(FB):
            for h in range(8):
                split_lo(dve, "out1", 4 * b + h // 2, h % 2)
                if b == 0:
                    if h == 0:
                        mix_ms(2)
                    if h == 1:
                        mix_norm(2)
                    if 1 <= h < 7:
                        for n in ((0, 1), (2, 3), (4,), (5,), (6,), (7,))[h - 1]:
                            tr_dve(dve, TB["mix"] + n, part(T2aH, MIX[n // 2][0], n % 2), part(T2aL, MIX[n // 2][0], n % 2), (6, 7), n)
                    if h == 2:
                        sgu_out()
                    if h == 3:
                        mix_ms(3)
                    if h == 4:
                        mix_norm(3)
                if b and h == 3:
                    x1_block(b - 1)
                if b and h == 7:
                    for j in range(J):
                        tr_dve(dve, TB["out1"] + 2 * (b - 1) + j, part(T1H, b - 1, j), part(T1L, b - 1, j), k=j)

        def up(k, j, i):
            B = BLK["ffn"] + 1
            return stt(av[:, j, :], ACC[B % 2][j], rstd2[:, j:j + 1], sg[:, j, :], MUL, MUL)

        def gated(f):
            B = BLK["ffn"] + 1
            block_done(dve, "ffn", 7, f)
            dve.wait_ge(acc_out[BLK["ffn"] % 2], f * 2 + (2 * (BLK["ffn"] // 2) + 2) if not isinstance(f, int) else 2 * (BLK["ffn"] // 2) + 2 + 2 * f)
            dve.wait_ge(tb_full, f * 2 + TB["ffn"])
            for j in range(J):
                up(None, j, f).then_inc(acc_out[B % 2], 1)

        def ffn(f, first):
            for h in range(16):
                split_lo(dve, "ffn", h // 2, h % 2, i=f)
                if first and h == 0:
                    x1_block(FB - 1)
                if first and h == 2:
                    dve.wait_ge(x1_sq, FB)
                    ch.link(dve.tensor_reduce(rstd2, ss1.rearrange("p (j f) -> p j f", j=J), AX, ADD))
                    ts(rstd2, rstd2, 1.0 / D, RMS_EPS, MUL, ADD).then_inc(ms2, 1)
                if first and h == 3:
                    for j in range(J):
                        tr_dve(dve, TB["out1"] + 6 + j, part(T1H, 3, j), part(T1L, 3, j), k=j)
                if first and h == 9:
                    dve.wait_ge(x1_st[0], 32)
                    dve.wait_ge(x1_st[1], 32)
                if not first and h == 3:
                    gated(f - 1)
                if not first and h == 8:
                    for j in range(J):
                        cols_, ts_ = bass.ds(f * 4 - 4, 4), slice(j * P, (j + 1) * P)
                        tr_dve(dve, f * 2 + (TB["ffn"] - 2 + j), T2bH[:, cols_, ts_], T2bL[:, cols_, ts_], k=j)

        ffn(0, True)
        with dve.Fori(1, NF) as f:
            ffn(f, False)

        def x2_block(b):
            B = BLK["down"] + b
            block_done(dve, "down", 11 * b + 10)
            dve.wait_ge(xr2_in, 16 * (b + 1))
            if b:
                dve.wait_ge(x2_st, 16 * b)
                dve.wait_ge(tb_full, TB["down"] + 2 * b)
            for j in range(J):
                tt(x2b[:, j, :], ACC[B % 2][j], xr2[:, j, :], ADD).then_inc(acc_out[B % 2], 1)

        for b in range(FB):
            for h in range(22):
                split_lo(dve, "down", 11 * b + h // 2, h % 2)
                if b == 0 and h == 3:
                    gated(NF - 1)
                if b == 0 and h == 8:
                    for j in range(J):
                        tr_dve(dve, TB["ffn"] + 20 + j, part(T2bH, 10, j), part(T2bL, 10, j), k=j)
                if b and h == 3:
                    x2_block(b - 1)
                if b and h == 8:
                    for j in range(J):
                        tr_dve(dve, TB["down"] + 2 * (b - 1) + j, part(T1H, b - 1, j), part(T1L, b - 1, j), k=j)

        def max_of(u):
            dve.wait_ge(a_S, u + 1)
            c = 2 * (u % 2)
            dve.tensor_reduce(nmx[:, c:c + 2], bank[6].rearrange("p (j s) -> p j s", j=J), AX, MAX, negate=True).then_inc(a_max, 1)

        def head_out(u):
            g, a = u // 4, u % 4
            dve.wait_ge(a_PV, u + 1)
            c = 2 * (u % 2)
            ch.link(dve.reciprocal(nrw[:, c:c + 2], nsum[:, c:c + 2]))
            for j in range(J):
                ts(oA[:, g, j, a * P:(a + 1) * P], bank[5][:, j * P:(j + 1) * P], nrw[:, c + j:c + j + 1], None, MUL).then_inc(a_O, 1)

        def in2_at(p):
            if p == 0:
                x2_block(FB - 1)
            if p == 3:
                for j in range(J):
                    tr_dve(dve, TB["down"] + 6 + j, part(T1H, 3, j), part(T1L, 3, j), k=j)
            for n, (b, e, kind, g) in enumerate(ROT):
                C_ = flat(tabs[2 if kind == "k" else 0][:, :, :, :])
                if p == e + 1:
                    dve.wait_ge(q_sq, n + 1)
                    ch.link(dve.tensor_reduce(nsx, heads(tb[:, :, :], P), AX, ADD))
                    ts(nrx, nsx, 1.0 / AD, RMS_EPS, MUL, ADD).then_inc(q_ms, 1)
                if p == e + 2:
                    dve.wait_ge(q_rs, n + 1)
                    tt(heads(xq[:, :, :], P), heads(xq[:, :, :], P), rep(nrx, 1, P), MUL).then_inc(q_norm, 1)
                if p == e + 3:
                    dve.wait_ge(q_norm, n + 1)
                    if n:
                        dve.wait_ge(rot_T, 2 * n)
                    if n == 0:
                        dve.wait_ge(tab_ready, 4)
                    ch.link(tt(ta[:, :, :], xq[:, :, :], C_, MUL))
                if p == e + 4:
                    dve.wait_ge(q_swap, n + 1)
                    tt(ta[:, :, :], ta[:, :, :], tb[:, :, :], ADD).then_inc(rot, 1)
            for g in range(AKV):
                for a in range(4):
                    if p == S_AT[g] + 3 * a + 2:
                        max_of(4 * g + a)
                    if p == S_AT[g] + 3 * a + 8:
                        head_out(4 * g + a)
                if p == 60 + 8 * g:
                    B = BLK["in2"] + 6 + g
                    dve.wait_ge(acc_out[B % 2], 2 * (B // 2) + 2)
                    dve.wait_ge(a_O, 8 * g + 8)
                    for j in range(J):
                        tt(oA[:, g, j, :], oA[:, g, j, :], gA[:, j, :], MUL).then_inc(a_og, 1)
                for j in range(J):
                    if p == OT_AT[g][j] + 3:
                        tr_dve(dve, TB["in2"] + 2 * g + j, part(T2cH, g, j), part(T2cL, g, j), (4, 4), j)

        for p in range(80):
            split_lo(dve, "in2", p // 2, p % 2)
            in2_at(p)

        def ln_block(ph, dst, res, res_in, b, cpb):
            B = BLK[ph] + b
            block_done(dve, ph, cpb * b + cpb - 1)
            dve.wait_ge(res_in[b % 2], 16 * (b // 2 + 1))
            for j in range(J):
                stt(dst[:, j, b * W:(b + 1) * W], res[:, b % 2, j, :], ALPHA, ACC[B % 2][j], MUL, ADD).then_inc(acc_out[B % 2], 1)
            dve.wait_ge(acc_out[B % 2], 2 * (B // 2) + 2)
            for j in range(J):
                c = 6 * (FB * j + b)
                ch.link(dve.bn_stats(bst[:, c:c + 6], dst[:, j, b * W:(b + 1) * W]))

        def ln_end(dst, layer, gain_in, G, Bv, ready, each):
            for j in range(J):
                ch.link(dve.bn_aggr(bag[:, 2 * j:2 * j + 2], bst[:, 24 * j:24 * j + 24]))
            ts(brs, bag.rearrange("p (j k) -> p j k", j=J)[:, :, 1], LN_EPS, None, ADD).then_inc(ln_ms, 1)
            dve.wait_ge(ln_rs, layer)
            dve.wait_ge(gain_in, 32)
            for n in range(FB * J):
                cs_, j = slice(n // J * W, (n // J + 1) * W), n % J
                d = dst[:, j, cs_]
                ch.link(stt(d, d, bag[:, 2 * j:2 * j + 1], G[:, cs_], SUB, MUL))
                stt(d, d, brs[:, j:j + 1], Bv[:, cs_], MUL, ADD).then_inc(ready, 1)
                each(n)

        for b in range(FB):
            for h in range(8):
                split_lo(dve, "out2", 4 * b + h // 2, h % 2)
                in2_at(80 + 8 * b + h)
                if b and h == 6:
                    ln_block("out2", X3, xr3, xr3_in, b - 1, 4)
        for h in range(3):
            split_lo(dve, "ret", h // 2, h % 2)
        ln_block("out2", X3, xr3, xr3_in, FB - 1, 4)

        def x3_tr(n):
            if n:
                m = n - 1
                tr_dve(dve, TB["out2"] + m, part(T1H, m // 2, m % 2), part(T1L, m // 2, m % 2), (4, 5, 6, 7), m)
            if n in (2, 4, 5, 6):
                h = {2: 3, 4: 4, 5: 5, 6: 6}[n]
                split_lo(dve, "ret", h // 2, h % 2)

        ln_end(X3, 1, ln_in, lnG, lnB, x3_ready, x3_tr)
        x3_tr(8)

        def ret(i, rc_, first):
            def stats(n):
                dve.wait_ge(r_out, n + 1)
                for j in range(J):
                    dve.bn_stats(bst[:, 6 * j:6 * j + 6], bank[(7, 5)[j]]).then_inc(rc_.s, 1)
                rc_.n += 2
                dve.wait_ge(rc_.s, rc_.base + rc_.n)
                v = bst[:, 0:12].rearrange("p (j k) -> p k j", j=J)
                mean, dif = bag.rearrange("p (j k) -> p k j", j=J)[:, 0, :], bag.rearrange("p (j k) -> p k j", j=J)[:, 1, :]
                rc_.link(tt(mean, v[:, 1, :], v[:, 4, :], ADD))
                rc_.link(tt(dif, v[:, 1, :], v[:, 4, :], SUB))
                rc_.link(tt(brs, v[:, 2, :], v[:, 5, :], ADD))
                rc_.link(ts(mean, mean, 0.5, None, MUL))
                rc_.link(tt(dif, dif, dif, MUL))
                rc_.link(ts(dif, dif, 0.25, LN_EPS, MUL, ADD))
                stt(brs, brs, 1.0 / RV, dif, MUL, ADD).then_inc(r_ms, 1)

            def norm(n):
                dve.wait_ge(r_rs, n + 1)
                for j in range(J):
                    ts(oR[:, j, :], bank[(7, 5)[j]], bag[:, 2 * j:2 * j + 1], brs[:, j:j + 1], SUB, MUL).then_inc(r_norm, 1)

            def gate(n, e, k):
                B = BLK["ret"] + 3 * e + 2
                dve.wait_ge(r_norm, n * 2 + 2)
                v = 2 * (B // 2) + 2 + 6 * k
                dve.wait_ge(acc_out[B % 2], i * 6 + v if not isinstance(i, int) else 6 * i + v)
                for j in range(J):
                    tt(oR[:, j, :], oR[:, j, :], gR[:, j, :], MUL).then_inc(r_og, 1)

            def tr(e, k):
                for j in range(J):
                    n = i * 4 + (4 * k + 2 * e + j)
                    if isinstance(i, int):
                        h_, l_ = part(T2dH, 2 * (i + k) + e, j), part(T2dL, 2 * (i + k) + e, j)
                    else:
                        c_, t_ = bass.ds(i * 8 + (8 * k + 4 * e), 4), slice(j * P, (j + 1) * P)
                        h_, l_ = T2dH[:, c_, t_], T2dL[:, c_, t_]
                    tr_dve(dve, n + TB["ret"], h_, l_, (4, 6), j)

            for h in range(48):
                e, p = h // 24, h % 24
                if not first or h >= 7:
                    split_lo(dve, "ret", h // 2, h % 2, i=i)
                hd = i * 2 + e
                if first and h == 7:
                    dve.wait_ge(lg1, 1)
                    y, u, d_, e_, l_ = (lg[:, n, :] for n in range(1, 6))
                    rc_.link(ts(d_, u, -1.0, 1.0, MUL, ADD))
                    rc_.link(ts(e_, d_, 0.0, None, ALU.is_equal))
                    rc_.link(tt(d_, d_, e_, ADD))
                    rc_.link(dve.reciprocal(d_, d_))
                    rc_.link(tt(d_, d_, y, MUL))
                    rc_.link(tt(l_, l_, d_, MUL))
                    rc_.link(tt(e_, e_, y, MUL))
                    rc_.link(tt(l_, l_, e_, SUB))
                if first and 8 <= h < 8 + RH:
                    m = h - 8
                    if m >= 2:
                        dve.wait_ge(mm_ready, m - 1)
                    b_ = mt[:, m % 2, :]
                    rc_.link(ts(b_, dpos[:, :, :].rearrange("p s t -> p (s t)"), lg[:, 5, m:m + 1], None, MUL))
                    stt(b_, dneg[:, :, :].rearrange("p s t -> p (s t)"), lg[:, 5, RH + m:RH + m + 1], b_, MUL, ADD).then_inc(mt_ready, 1)
                if p == 12:
                    B = BLK["ret"] + 3 * e
                    v = 2 * (B // 2) + 2
                    dve.wait_ge(acc_out[B % 2], v if first else i * 6 + v)
                    dve.wait_ge(rr_in, 32)
                    for ins in swapped(dve, rb[:, :, :], xr[:, :, :], rs_[:, :, :], 64):
                        ins.then_inc(rc_.s, 1)
                    rc_.n += 2
                    dve.wait_ge(rc_.s, rc_.base + rc_.n)
                    rc_.link(tt(xr[:, :, :], xr[:, :, :], rc[:, :, :], MUL))
                    tt(xr[:, :, :], xr[:, :, :], rb[:, :, :], ADD).then_inc(r_rot, 1)
                if p == 20:
                    dve.wait_ge(r_S, hd + 1)
                    if first and e == 0:
                        dve.wait_ge(mm_ready, RH)
                    M_ = MM[:, bass.ds(hd, 1), :, :].rearrange("p h s t -> p (h s) t") if not isinstance(i, int) else MM[:, hd, :, :]
                    tt(SM[:, :, :], bank[6].rearrange("p (s t) -> p s t", s=2), M_, MUL).then_inc(r_SM, 1)
                if h == 23:
                    stats(hd)
                if h == 24:
                    norm(i * 2)
                if h == 28:
                    gate(i * 2, 0, 0)
                if first and h == 30:
                    dve.wait_ge(x3_st, 16)
                if h == 31:
                    tr(0, 0)
                if h == 47:
                    stats(hd)
                if not first:
                    if h == 0:
                        norm(i * 2 - 1)
                    if h == 4:
                        gate(i * 2 - 1, 1, -1)
                    if h == 7:
                        tr(1, -1)

        RET = (8 + 8 + 6 + 16, 6 + 16)
        rc_ = Chain(dve, ret_c)
        ret(0, rc_, True)
        assert rc_.n == RET[0], rc_.n
        with dve.Fori(1, RH // 2) as i:
            rc_.base, rc_.n = i * RET[1] + (RET[0] - RET[1]), 0
            ret(i, rc_, False)
            assert rc_.n == RET[1], rc_.n

        for b in range(FB):
            for h in range(16):
                split_lo(dve, "out3", 8 * b + h // 2, h % 2)
                if b == 0 and h == 0:
                    dve.wait_ge(r_rs, RH)
                    for j in range(J):
                        ts(oR[:, j, :], bank[(7, 5)[j]], bag[:, 2 * j:2 * j + 1], brs[:, j:j + 1], SUB, MUL).then_inc(r_norm, 1)
                if b == 0 and h == 4:
                    B = BLK["out3"] - 1
                    dve.wait_ge(r_norm, 2 * RH)
                    dve.wait_ge(acc_out[B % 2], 2 * (B // 2) + 2)
                    for j in range(J):
                        tt(oR[:, j, :], oR[:, j, :], gR[:, j, :], MUL).then_inc(r_og, 1)
                if b == 0 and h == 7:
                    for j in range(J):
                        tr_dve(dve, TB["ret"] + 2 * RH - 2 + j, part(T2dH, RH - 1, j), part(T2dL, RH - 1, j), (4, 6), j)
                if b and h == 3:
                    ln_block("out3", X4, xr4, xr4_in, b - 1, 8)
        ln_block("out3", X4, xr4, xr4_in, FB - 1, 8)
        ln_end(X4, 2, ln2_in, lnG2, lnB2, x4_ready, lambda n: None)

    @block.tensor
    def _(pe):
        mm = pe.matmul

        def tr1(n):
            pe.wait_ge(xg_ready, n // 2 + 1)
            tr_pe(pe, n, XG[:, n % 2, (n // 2) * W:(n // 2 + 1) * W], (4, 5, 6, 7), n)

        def half1(p):
            b, h = p // 8, p % 8
            if b == 0 and h % 2 == 0:
                pe.wait_ge(tb_done, h + 2)
            products(pe, "in1", 4 * b + h // 2, h % 2, T1H, T1L, 4 * (h // 2), b, BLOCKS1[b][1], h == 0, h == 7)

        def scores(u):
            h, kind = u // 2, u % 2
            gs, r, o = slice(HD * (h // 4), HD * (h // 4 + 1)), h % 4, ubank(u)
            if u >= 2:
                pe.wait_ge(s_exp, 2 * (u - 1))
            mm(o[:, 0:P], flip, bias[:, h, P:2 * P], start=True, stop=False)
            mm(o[:, 0:P], qT[gs, r, 0:P], kT[gs, kind, 0:P], start=False, stop=True)
            mm(o[:, P:3 * P], flip, bias[:, h, 0:T], start=True, stop=False)
            mm(o[:, P:3 * P], qT[gs, r, P:T], kT[gs, kind, :], start=False, stop=True).then_inc(s_full, 1)

        def prob_T(u):
            pe.wait_ge(p_norm, 2 * u + 2)
            if u:
                pe.wait_ge(pT_out, u)
            for n in range(3):
                m = pe.transpose(bank[6][:, n * P:(n + 1) * P], PB[:, u // 2 % 2, u % 2, n * P:(n + 1) * P], ident)
            m.then_inc(p_T, 1)

        def values(h):
            g = h // 4
            pe.wait_ge(pT_out, 2 * h + 2)
            if h == 4:
                pe.wait_ge(nsa_o, 1)
            for j in range(J):
                o = bank[7][:, head_cols(h, j)]
                mm(o, PcT[:, 2 * h + j, :], KVC[:, 1, g, :], start=True, stop=False)
                for kind in range(2):
                    for s in range(j + 1):
                        v = Akv[:, s, 384 + g * HD:384 + (g + 1) * HD] if kind == 0 else Akw[:, s, P + g * HD:P + (g + 1) * HD]
                        n = (j + s) * P
                        m = mm(o, PT[:, h % 2, kind, n:n + P], v, start=False, stop=kind == 1 and s == j)
            m.then_inc(nsa_pv, 1)

        def stick_z(k):
            hs, o = slice(HD * (k % 2), HD * (k % 2 + 1)), zbank(k)
            if k == 0:
                pe.wait_ge(dT_out, 4)
            if k == 2:
                pe.wait_ge(pT_out, NU)
            if k >= 3:
                pe.wait_ge(d_cap, k - 2)
            mm(o[:, 0:T], dkT[hs, k // 2, 0:P], dqT[hs, k // 2, :], start=True, stop=False, skip_group_check=True)
            mm(o[:, T:T + P], dkT[hs, k // 2, P:T], dqT[hs, k // 2, P:T], start=False, stop=False,
               skip_group_check=True).then_inc(z_full, 1)

        def stick_sums(k):
            o, s_ = zbank(k), LB[:, k % 2, :]
            pe.wait_ge(d_sp, k + 1)
            mm(o[:, 0:T], ntri, s_[:, 0:T], start=False, stop=False, skip_group_check=True)
            mm(o[:, P:T], nones, s_[:, T:T + P], start=False, stop=False, skip_group_check=True)
            mm(o[:, T:T + P], ntri, s_[:, T:T + P], start=False, stop=True, skip_group_check=True).then_inc(d_arg, 1)

        def stick_values(h):
            pe.wait_ge(d_a, h + 1)
            if h == 0:
                pe.wait_ge(nsa_o, 2)
                pe.wait_ge(acc_out[1], 6)
            if h == 4:
                pe.wait_ge(d_o, 1)
            a, vs = AR[:, h % 2, :], slice(h * HD, (h + 1) * HD)
            mm(bank[7][:, head_cols(h, 0)], a[:, 0:P], Dv[:, 0, vs], start=True, stop=True)
            mm(bank[7][:, head_cols(h, 1)], a[:, P:T], Dv[:, 0, vs], start=True, stop=False)
            mm(bank[7][:, head_cols(h, 1)], a[:, T:T + P], Dv[:, 1, vs], start=False, stop=True).then_inc(d_pv, 1)

        def mix_at(p):
            if p == 20:
                pe.wait_ge(sg_ready, 1)
                for h in range(NH):
                    m = pe.transpose(bank[4 + h // 4][:, (h % 4) * P:(h % 4 + 1) * P], SG[:, h, :], ident)
                    if h % 4 == 3:
                        m.then_inc(w_T, 1)
            if p == 27:
                pe.wait_ge(zd_ready, 2)
                pe.wait_ge(wT_out, 2)
                for i in range(2):
                    for g in range(NG):
                        for j in range(J):
                            o = (2 * g + j) * P
                            m = pe.transpose(bank[4 + i][:, o:o + P], zd[:, j, 2 * i + g, :, :].rearrange("p n d -> p (n d)"), ident)
                    m.then_inc(z_T, 1)
            if p == 29:
                pe.wait_ge(par_out, 2)
                pe.wait_ge(nsa_qk, 2)
                for j in range(J):
                    for r in range(4):
                        m = pe.transpose(bank[6 + j][:, r * P:(r + 1) * P], TQ[:, j, r * P:(r + 1) * P], ident)
                    m.then_inc(qk_T, 1)
            if p == 31:
                pe.wait_ge(nsa_qk, 3)
                pe.wait_ge(zz_ready, 6)
                pe.wait_ge(w1_in, 80)
                for kind in range(2):
                    for j in range(J):
                        o = (2 * kind + j) * P
                        m = pe.transpose(bank[4][:, o:o + P], TK[:, kind, j, :], ident)
                m.then_inc(qk_T, 1)
                for i in range(2):
                    for l in range(CS):
                        m = mm(bank[5][0:HD, 32 * i:32 * i + 2 * NCMP], w1s[:, i, l, :], zz[:, i, :, l:l + CS * (NCMP - 1) + 1:CS],
                               start=l == 0, stop=l == CS - 1)
                m.then_inc(cmp1, 1)
            if p == 33:
                pe.wait_ge(hT_ready, 1)
                pe.wait_ge(qkT_out, 3)
                for i in range(2):
                    for g in range(NG):
                        o = (2 * i + g) * HD
                        m = mm(bank[6][0:NCMP, o:o + HD], hT[0:HD, (2 * i + g) * NCMP:(2 * i + g + 1) * NCMP], w2s[:, i, :], start=True, stop=True)
                m.then_inc(cmp2, 1)
            if p == 36:
                pe.wait_ge(kcn_ready, 1)
                pe.transpose(bank[7][:, 0:NCMP], TQ[0:NCMP, 0, 0:P], ident[0:NCMP, 0:NCMP]).then_inc(kc_T, 1)
            if p == 38:
                pe.wait_ge(bias_in, 16)
                pe.wait_ge(rest_in, 16)
                pe.wait_ge(kcT_out, 1)
                for h in range(NH):
                    gs, r = slice(HD * (h // 4), HD * (h // 4 + 1)), h % 4
                    for j in range(J):
                        o = bank[6 + h // 4][:, (2 * h + j) % 8 * 16:(2 * h + j) % 8 * 16 + NCMP]
                        a = 159 - P * j
                        mm(o, flip, bias[:, h, a:a + CS * (NCMP - 1) + 1:CS], start=True, stop=False)
                        m = mm(o, qT[gs, r, j * P:(j + 1) * P], kcT[gs, 0:NCMP], start=False, stop=True)
                m.then_inc(cs_full, 1)
            for n in range(4):
                if p == 41 + n // 2:
                    pe.wait_ge(pc_ready, 1)
                    if n >= 2:
                        pe.wait_ge(pcT_out, n - 1)
                    for u in range(4 * n, 4 * n + 4):
                        m = pe.transpose(bank[6 + n % 2][0:NCMP, (u % 4) * P:(u % 4 + 1) * P], pcm[:, u, 0:NCMP], ident)
                    m.then_inc(pc_T, 1)
            if p == U0:
                pe.wait_ge(qkT_out, 3)
                pe.wait_ge(hT_ready, 1)
            if p == U0 + 3:
                pe.wait_ge(pcT_out, 4)
            if 0 <= p - U0 < NU:
                scores(p - U0)
            if 0 <= p - U0 - 3 < NU:
                prob_T(p - U0 - 3)
            for h in range(NH):
                if p == U0 + 2 * h + 6:
                    values(h)
            for n in range(4):
                if p == U0 + 18 + 2 * (n // 2):
                    if n == 0:
                        pe.wait_ge(s_exp, 2 * NU)
                        pe.wait_ge(acc_out[1], 4)
                        pe.wait_ge(acc_out[0], 6)
                    if n >= 2:
                        pe.wait_ge(dT_out, n - 1)
                    for r in range(4):
                        m = pe.transpose(bank[4 + n % 2][:, r * P:(r + 1) * P], (Dq, Dk)[n // 2][:, n % 2, r * P:(r + 1) * P], ident)
                    m.then_inc(d_T, 1)
            for k in range(NH):
                if p == Z0 + 2 * k + 8:
                    stick_values(k)
                if p == Z0 + 2 * k + 4:
                    stick_sums(k)
                if p == Z0 + 2 * k:
                    stick_z(k)
            if p == 87:
                pe.wait_ge(d_cap, NH)
                pe.wait_ge(cv_ready, 2)
                for h in range(NH):
                    m = mm(bank[4 + h // 4][:, (h % 4) * P:(h % 4 + 1) * P], WT[:, h, :], Cv[:, :, h * HD:(h + 1) * HD], start=True, stop=True)
                    if h % 4 == 3:
                        m.then_inc(sgu_full, 1)

        pe.wait_ge(cst_in, 16)
        for p in range(8 * NB1):
            if p < 8:
                for n in range(0 if p == 0 else p + 2, min(p + 3, 8)):
                    tr1(n)
            half1(p)
            if p == 9:
                pe.wait_ge(tb_done, 8)
                pe.wait_ge(oh_in, 32)
                mm(bank[6][0:NH, :], tabaug[:, :], onehot[:, :], start=True, stop=True).then_inc(vrow_ps, 1)
                pe.wait_ge(par_in, 80)
                pe.transpose(bank[7][:, 0:HD], prow[:, :], ident[0:HD, 0:HD])
                pe.transpose(bank[7][:, HD:HD + NH], sbrow[:, :], ident[0:NH, 0:NH]).then_inc(par_T, 1)
            mix_at(p)

        def x1_tr(b):
            pe.wait_ge(xg2, b + 1)
            for j in range(J):
                tr_pe(pe, TB["out1"] + 2 * b + j, xgb[:, b % 2, j, :], k=j)

        for b in range(FB):
            for h in range(8):
                if b == 0:
                    for n in ((0, 1), (2, 3), (4,), (5,), (6,), (7,), (), ())[h]:
                        if n == 0:
                            pe.wait_ge(d_o, 2)
                        pe.wait_ge(mixed_ready, n + 1)
                        tr_pe(pe, TB["mix"] + n, MIX[n // 2][1][:, n % 2, :], (6, 7), n)
                    if h % 2 == 0:
                        pe.wait_ge(tb_done, TB["mix"] + h + 2)
                products(pe, "out1", 4 * b + h // 2, h % 2, T2aH, T2aL, 4 * MIX[h // 2][0], BLK["out1"] + b, W, h == 0, h == 7)
                if b and h == 5:
                    x1_tr(b - 1)

        def ffn(f, first):
            for h in range(16):
                if first and h == 6:
                    pe.wait_ge(tb_done, TB["out1"] + 8)
                products(pe, "ffn", h // 2, h % 2, T1H, T1L, 4 * (h % 8 // 2), BLK["ffn"] + h // 8, W, h % 8 == 0, h % 8 == 7, f)
                if first and h == 1:
                    x1_tr(FB - 1)
                if not first and h == 5:
                    gated_tr(f)

        def gated_tr(f):
            B = BLK["ffn"] + 1
            v = 2 * (B // 2)
            pe.wait_ge(acc_out[B % 2], f * 2 + v if not isinstance(f, int) else v + 2 * f)
            for j in range(J):
                tr_pe(pe, f * 2 + (TB["ffn"] - 2 + j), av[:, j, :], k=j)

        ffn(0, True)
        with pe.Fori(1, NF) as f:
            ffn(f, False)

        def x2_tr(b):
            B = BLK["down"] + b
            pe.wait_ge(acc_out[B % 2], 2 * (B // 2) + 2)
            for j in range(J):
                tr_pe(pe, TB["down"] + 2 * b + j, x2b[:, j, :], k=j)

        for b in range(FB):
            for h in range(22):
                if b == 0 and h == 20:
                    pe.wait_ge(tb_done, TB["down"])
                products(pe, "down", 11 * b + h // 2, h % 2, T2bH, T2bL, 4 * (h // 2), BLK["down"] + b, W, h == 0, h == 21)
                if b == 0 and h == 5:
                    gated_tr(NF)
                if b and h == 5:
                    x2_tr(b - 1)

        def in2_at(p):
            for n, (b, e, kind, g) in enumerate(ROT):
                for j in range(J):
                    if p == e + 5 + 2 * j:
                        pe.wait_ge(rot, n + 1)
                        pe.wait_ge(rotT_out, 2 * n + j)
                        for a in range(4):
                            m = pe.transpose(bank[4][:, a * P:(a + 1) * P], ta[:, j, a * P:(a + 1) * P], ident)
                        m.then_inc(rot_T, 1)
            for g in range(AKV):
                for a in range(4):
                    u = 4 * g + a
                    if p == S_AT[g] + 3 * a:
                        if u == 0:
                            pe.wait_ge(rotT_out, 4)
                        elif a == 0:
                            pe.wait_ge(rotT_out, 4 + 2 * g)
                        if u:
                            pe.wait_ge(a_exp, 2 * u)
                        for j in range(J):
                            m = mm(bank[6][:, j * T:(j + 1) * T], qTa[:, g % 2, a, j * P:(j + 1) * P], kTa[:, g, :], start=True, stop=True)
                        m.then_inc(a_S, 1)
                    if p == S_AT[g] + 3 * a + 3:
                        pe.wait_ge(a_exp, 2 * u + 2)
                        pe.wait_ge(a_PTo, u)
                        for s in range(2):
                            for j in range(J):
                                m = pe.transpose(bank[7][:, (2 * s + j) * P:(2 * s + j + 1) * P], PA[:, u % 2, j, s * P:(s + 1) * P], ident)
                        m.then_inc(a_PT, 1)
                    if p == S_AT[g] + 3 * a + 6:
                        pe.wait_ge(a_PTo, u + 1)
                        if u == 0:
                            B = BLK["in2"] + 2
                            pe.wait_ge(acc_out[B % 2], 2 * (B // 2) + 2)
                        if u:
                            pe.wait_ge(a_O, 2 * u)
                        for j in range(J):
                            for s in range(2):
                                m = mm(bank[5][:, j * P:(j + 1) * P], PTa[:, u % 2, s, j * P:(j + 1) * P], vA[:, s, g * P:(g + 1) * P],
                                       start=s == 0, stop=s == 1)
                        m.then_inc(a_PV, 1)
                for j in range(J):
                    if p == OT_AT[g][j]:
                        pe.wait_ge(a_og, 2 * g + 2)
                        pe.wait_ge(tb_done, TB["in2"] + 2 * g + j)
                        pe.wait_ge(rotT_out, 10)
                        tr_pe(pe, TB["in2"] + 2 * g + j, oA[:, g, j, :], (4, 4), j)

        for p in range(80):
            b, h = p // 8, p % 8
            if p == 6:
                pe.wait_ge(tb_done, TB["down"] + 8)
            products(pe, "in2", p // 2, p % 2, T1H, T1L, 4 * (h // 2), BLK["in2"] + b, W, h == 0, h == 7)
            if p == 1:
                x2_tr(FB - 1)
            in2_at(p)
        for b in range(FB):
            for h in range(8):
                if b == 0 and h in (0, 4, 6):
                    pe.wait_ge(tb_done, TB["in2"] + max(h, 2) + 2)
                products(pe, "out2", 4 * b + h // 2, h % 2, T2cH, T2cL, 4 * (h // 2), BLK["out2"] + b, W, h == 0, h == 7)
                in2_at(80 + 8 * b + h)

        def ret(i, first):
            def tr(e, k):
                n = i * 2 + (e + 2 * k)
                pe.wait_ge(r_og, n * 2 + 2)
                for j in range(J):
                    m = i * 4 + (4 * k + 2 * e + j)
                    tr_pe(pe, m + TB["ret"], oR[:, j, :], (4, 6), j)

            for h in range(48):
                e, p = h // 24, h % 24
                hd = i * 2 + e
                if first:
                    for n in range(0 if h == 0 else h + 2, min(h + 3, 8)):
                        pe.wait_ge(x3_ready, n + 1)
                        tr_pe(pe, TB["out2"] + n, X3[:, n % 2, (n // 2) * W:(n // 2 + 1) * W], (4, 5, 6, 7), n)
                    if h < 8 and h % 2 == 0:
                        pe.wait_ge(tb_done, TB["out2"] + h + 2)
                products(pe, "ret", h // 2, h % 2, T1H, T1L, 4 * (h % 8 // 2), BLK["ret"] + h // 8, W, h % 8 == 0, h % 8 == 7, i)
                if p == 15:
                    pe.wait_ge(r_rot, hd + 1)
                    for j in range(J):
                        for a in range(4):
                            m = pe.transpose(bank[4 + j][:, a * P:(a + 1) * P], xr[:, j, a * P:(a + 1) * P], ident)
                        m.then_inc(r_T, 1)
                if p == 18:
                    pe.wait_ge(r_Tout, hd * 4 + 4)
                    for s in range(2):
                        for dc in range(2):
                            m = mm(bank[6][:, s * T:(s + 1) * T], rT[:, 1, dc, s * P:(s + 1) * P], rT[:, 0, dc, :], start=dc == 0, stop=dc == 1)
                    m.then_inc(r_S, 1)
                if p == 21:
                    pe.wait_ge(r_SM, hd + 1)
                    B = BLK["ret"] + 3 * e + 1
                    v = 2 * (B // 2) + 2
                    pe.wait_ge(acc_out[B % 2], v if first else i * 6 + v)
                    for j in range(J):
                        for s in range(2):
                            m = mm(bank[(7, 5)[j]], SM[:, s, j * P:(j + 1) * P], vR[:, s, :], start=s == 0, stop=s == 1)
                    m.then_inc(r_out, 1)
                if h == 29:
                    tr(0, 0)
                if h == 5 and not first:
                    tr(1, -1)

        ret(0, True)
        with pe.Fori(1, RH // 2) as i:
            ret(i, False)
        for b in range(FB):
            for h in range(16):
                if b == 0 and h == 0:
                    pe.wait_ge(tb_done, TB["ret"] + 2 * RH - 2)
                if b == 0 and h == 14:
                    pe.wait_ge(tb_done, TB["ret"] + 2 * RH)
                products(pe, "out3", 8 * b + h // 2, h % 2, T2dH, T2dL, 4 * (h // 2), BLK["out3"] + b, W, h == 0, h == 15)
                if b == 0 and h == 5:
                    pe.wait_ge(r_og, 2 * RH)
                    for j in range(J):
                        tr_pe(pe, TB["ret"] + 2 * RH - 2 + j, oR[:, j, :], (4, 6), j)

    ctx.close()


def constants():
    f = np.float32
    p = np.arange(P)
    c = {}
    cst = np.zeros((P, 5, P), f)
    cst[:, 0] = np.eye(P)
    cst[:, 1] = np.eye(P)[::-1]
    cst[:, 2] = -(p[:, None] >= p[None, :]).astype(f)
    cst[:, 3] = -1
    cst[:, 4] = p[None, :] <= p[:, None]
    c["cst"] = cst
    before = (p[:, None] < p[None, :]).astype(f)
    c["msk3"] = np.concatenate([before, np.ones((P, P), f), before], 1)
    c["cap3"] = np.concatenate([(before - 1) * f(-NEG), np.zeros((P, P), f), (before - 1) * f(-NEG)], 1).astype(f)
    d = np.arange(T)
    n = np.maximum(d, 1).astype(f)
    large = 16 + (np.log(n / f(16)).astype(f) / f(math.log(64)) * f(16)).astype(np.int32)
    bucket = np.where(d < 16, d, np.minimum(large, 31))
    oh = np.zeros((33, W), f)
    oh[bucket[::-1], np.arange(T)] = 1
    oh[32, T:] = NEG
    c["onehot"] = oh
    for name, hd, n in (("rope", AD, 4), ("rope2", RD, 2)):
        row, col = np.repeat(np.arange(4, dtype=f), 64), np.tile(np.arange(64, dtype=f), 4)
        half = hd // 2
        inv = (f(10000.0) ** (-np.arange(0, half, 2, dtype=f) / f(half))).astype(f)
        a, b = row[:, None] * inv, col[:, None] * inv
        ang = np.concatenate([a, a, b, b], -1)
        sign = np.repeat(np.array([-1, 1, -1, 1], f), hd // 4)
        for k, t in (("c", np.cos(ang)), ("s", np.sin(ang) * sign)):
            t = t.astype(f).reshape(J, P, 1, hd).transpose(1, 0, 2, 3)
            t = np.broadcast_to(t, (P, J, n, hd))
            c[f"{name}_{k}"] = np.ascontiguousarray(t if n == 4 else t.reshape(P, J, n * hd))
    dist = d[None, None, :] - (np.arange(2)[None, :, None] * P + p[:, None, None])
    c["dist"] = np.concatenate([np.maximum(dist, 0), np.maximum(-dist, 0)], 1).astype(f)
    return c


_INS = ["x", "w_in", "w_out", "norm_mix", "norm_ffn", "q_gain", "k_gain", "cmp_pos", "cmp_w1", "cmp_w2", "rel_table",
        "conv_w", "sgu_w", "sgu_b", "group_gain", "w_ffn_gate", "w_ffn_up", "w_ffn_down", "attn_w_in_2", "attn_q_gain_2",
        "attn_k_gain_2", "attn_w_out_2", "ret_w_in_2", "ret_decay_exp_2", "ret_w_out_2", "ln_gain_2", "ln_bias_2"]


def kernel(**inputs):
    import concourse.bacc as _bacc
    from concourse.bass_utils import run_bass_kernel_spmd as _run

    nc = _bacc.Bacc("TRN2", target_bir_lowering=False, num_devices=1)
    arrays, args = {}, {}
    given = {name: np.ascontiguousarray(inputs[name]) for name in _INS}
    for name, a in {**given, **constants()}.items():
        arrays[f"in_{name}"] = a
        args[name] = nc.dram_tensor(f"in_{name}", a.shape, mybir.dt.from_np(a.dtype), kind="ExternalInput").ap()
    out = nc.dram_tensor("out_0", (1, T, D), F32, kind="ExternalOutput").ap()
    two_blocks(nc, args, out)
    r = _run(nc, [arrays], core_ids=[0])
    return r.results[0]["out_0"]
```
